# Optimizing a Trainium2 kernel written in Bass

```python
import math
import jax, jax.numpy as jnp
from jax import lax
import numpy as np

D_MODEL = 1024
BATCH = 1
SEQ = 512
DEPTH = 1

CHUNK = 64
Q_BLOCK = 128
TOKEN_BLOCK = 128
EPS = 1e-6

SB_HEADS = 8
SB_HEAD_DIM = 64
SB_WIDTH = SB_HEADS * SB_HEAD_DIM

MLA_HEADS = 8
MLA_NOPE_DIM = 64
MLA_ROPE_DIM = 32
MLA_QK_DIM = MLA_NOPE_DIM + MLA_ROPE_DIM
MLA_V_DIM = 64
MLA_Q_RANK = 384
MLA_KV_RANK = 256
MLA_WIDTH = MLA_HEADS * MLA_V_DIM
ROPE_THETA = 10000.0

MIX_WIDTH = SB_WIDTH + MLA_WIDTH
IN_SPLITS = (SB_WIDTH, 2 * SB_WIDTH, 3 * SB_WIDTH,
             3 * SB_WIDTH + MLA_Q_RANK,
             3 * SB_WIDTH + MLA_Q_RANK + MLA_KV_RANK)
IN_PROJ_WIDTH = 3 * SB_WIDTH + MLA_Q_RANK + MLA_KV_RANK + MLA_ROPE_DIM

PEER_HEADS = 8
PEER_N_KEYS = 128
PEER_N_EXPERTS = PEER_N_KEYS * PEER_N_KEYS
PEER_KEY_DIM = 256
PEER_HALF_DIM = PEER_KEY_DIM // 2
PEER_TOPK = 16


def rms_norm(x, g):
    xf = x.astype(jnp.float32)
    y = xf * lax.rsqrt(jnp.mean(xf * xf, axis=-1, keepdims=True) + EPS)
    return (y * g.astype(jnp.float32)).astype(x.dtype)

def rope(x, pos):
    r = x.shape[-1]
    half = r // 2
    inv_freq = 1.0 / (ROPE_THETA ** (jnp.arange(half, dtype=jnp.float32) * (2.0 / r)))
    ang = pos.astype(jnp.float32)[..., None] * inv_freq
    cos = jnp.cos(ang)[:, :, None, :]
    sin = jnp.sin(ang)[:, :, None, :]
    xf = x.astype(jnp.float32)
    x1, x2 = xf[..., :half], xf[..., half:]
    out = jnp.concatenate([x1 * cos - x2 * sin, x1 * sin + x2 * cos], axis=-1)
    return out.astype(x.dtype)

def to_query_blocks(q):
    b, s, h, d = q.shape
    return q.reshape(b, s // Q_BLOCK, Q_BLOCK, h, d).transpose(1, 0, 3, 2, 4)

def from_query_blocks(o):
    nb, b, qb, h, d = o.shape
    return o.transpose(1, 0, 2, 3, 4).reshape(b, nb * qb, h * d)

def stick_breaking_attention(q, k, v):
    b, s, h, d = q.shape
    nb = s // Q_BLOCK
    scale = d ** -0.5
    kpos = jnp.arange(s)

    def block(args):
        qi, bi = args
        z = jnp.einsum('bhqd,bshd->bhqs', qi, k,
                       preferred_element_type=jnp.float32) * scale
        qpos = bi * Q_BLOCK + jnp.arange(Q_BLOCK)
        strict = kpos[None, :] < qpos[:, None]
        log_fail = jnp.where(strict, jax.nn.log_sigmoid(-z), 0.0)
        later = lax.cumsum(log_fail, axis=3, reverse=True) - log_fail
        a = jnp.where(strict, jnp.exp(jax.nn.log_sigmoid(z) + later), 0.0)
        return jnp.einsum('bhqs,bshd->bqhd', a.astype(v.dtype), v)

    out = lax.map(block, (to_query_blocks(q), jnp.arange(nb)))
    return from_query_blocks(out)

def chunk_causal_softmax_attention(q, k, v):
    b, s, h, dq = q.shape
    nb = s // Q_BLOCK
    scale = dq ** -0.5
    kchunk = jnp.arange(s) // CHUNK

    def block(args):
        qi, bi = args
        sc = jnp.einsum('bhqd,bshd->bhqs', qi, k,
                        preferred_element_type=jnp.float32) * scale
        qchunk = (bi * Q_BLOCK + jnp.arange(Q_BLOCK)) // CHUNK
        allowed = kchunk[None, :] <= qchunk[:, None]
        p = jax.nn.softmax(jnp.where(allowed, sc, -jnp.inf), axis=-1)
        return jnp.einsum('bhqs,bshd->bqhd', p.astype(v.dtype), v)

    out = lax.map(block, (to_query_blocks(q), jnp.arange(nb)))
    return from_query_blocks(out)

def peer_ffn(h, w_q, sub_keys, u, v):
    b, s, d = h.shape
    nb = (b * s) // TOKEN_BLOCK
    k = PEER_TOPK

    def block(xt):
        q = (xt @ w_q).reshape(TOKEN_BLOCK, PEER_HEADS, 2, PEER_HALF_DIM)
        sc = jnp.einsum('thcd,chnd->thcn', q, sub_keys,
                        preferred_element_type=jnp.float32)
        top_s, top_i = lax.top_k(sc, k)
        cand_s = top_s[:, :, 0, :, None] + top_s[:, :, 1, None, :]
        cand_i = top_i[:, :, 0, :, None] * PEER_N_KEYS + top_i[:, :, 1, None, :]
        best_s, best_pos = lax.top_k(cand_s.reshape(TOKEN_BLOCK, PEER_HEADS, k * k), k)
        idx = jnp.take_along_axis(cand_i.reshape(TOKEN_BLOCK, PEER_HEADS, k * k),
                                  best_pos, axis=-1)
        g = jax.nn.softmax(best_s, axis=-1)
        pre = jnp.einsum('td,thkd->thk', xt, u[idx], preferred_element_type=jnp.float32)
        coef = (g * jax.nn.gelu(pre, approximate=False)).astype(v.dtype)
        return jnp.einsum('thk,thkd->td', coef, v[idx])

    out = lax.map(block, h.reshape(nb, TOKEN_BLOCK, d))
    return out.reshape(b, s, d)

def first_inputs(seed: int = 0) -> dict:
    key = jax.random.key(seed)
    ks = jax.random.split(key, 20)
    f32 = jnp.float32

    def w(k_, shape, fan_in):
        return jax.random.normal(k_, shape, f32) * (fan_in ** -0.5)

    def gain(k_, shape):
        return 1.0 + 0.02 * jax.random.normal(k_, shape, f32)

    x = jax.random.normal(ks[0], (BATCH, SEQ, D_MODEL), f32)
    offset = jax.random.randint(ks[1], (BATCH, 1), 0, 1024, dtype=jnp.int32)
    positions = (offset + jnp.arange(SEQ, dtype=jnp.int32)[None, :]).astype(jnp.int32)
    return {
        "x": x,
        "positions": positions,
        "attn_norm": gain(ks[2], (DEPTH, D_MODEL)),
        "w_in": w(ks[3], (DEPTH, D_MODEL, IN_PROJ_WIDTH), D_MODEL),
        "cq_norm": gain(ks[4], (DEPTH, MLA_Q_RANK)),
        "w_uq": w(ks[5], (DEPTH, MLA_Q_RANK, MLA_HEADS * MLA_QK_DIM), MLA_Q_RANK),
        "ckv_norm": gain(ks[6], (DEPTH, MLA_KV_RANK)),
        "w_ukv": w(ks[7], (DEPTH, MLA_KV_RANK, MLA_HEADS * (MLA_NOPE_DIM + MLA_V_DIM)), MLA_KV_RANK),
        "q_norm": gain(ks[8], (DEPTH, MLA_QK_DIM)),
        "k_norm": gain(ks[9], (DEPTH, MLA_QK_DIM)),
        "sb_out_norm": gain(ks[10], (DEPTH, SB_WIDTH)),
        "mla_out_norm": gain(ks[11], (DEPTH, MLA_WIDTH)),
        "w_o": w(ks[12], (DEPTH, MIX_WIDTH, D_MODEL), MIX_WIDTH),
        "ffn_norm": gain(ks[13], (DEPTH, D_MODEL)),
        "peer_w_q": w(ks[14], (DEPTH, D_MODEL, PEER_HEADS * PEER_KEY_DIM), D_MODEL),
        "peer_sub_keys": w(ks[15], (DEPTH, 2, PEER_HEADS, PEER_N_KEYS, PEER_HALF_DIM), PEER_HALF_DIM),
        "peer_u": w(ks[16], (DEPTH, PEER_N_EXPERTS, D_MODEL), D_MODEL),
        "peer_v": w(ks[17], (DEPTH, PEER_N_EXPERTS, D_MODEL), D_MODEL),
    }

def first_block(x, positions, attn_norm, w_in, cq_norm, w_uq, ckv_norm, w_ukv, q_norm, k_norm,
              sb_out_norm, mla_out_norm, w_o, ffn_norm, peer_w_q, peer_sub_keys, peer_u, peer_v):
    b, s, _ = x.shape
    for l in range(DEPTH):
        h = rms_norm(x, attn_norm[l])
        proj = h @ w_in[l]
        sb_q, sb_k, sb_v, cq, ckv, k_pe = jnp.split(proj, IN_SPLITS, axis=-1)

        sb = stick_breaking_attention(sb_q.reshape(b, s, SB_HEADS, SB_HEAD_DIM),
                                      sb_k.reshape(b, s, SB_HEADS, SB_HEAD_DIM),
                                      sb_v.reshape(b, s, SB_HEADS, SB_HEAD_DIM))

        q = (rms_norm(cq, cq_norm[l]) @ w_uq[l]).reshape(b, s, MLA_HEADS, MLA_QK_DIM)
        kv = (rms_norm(ckv, ckv_norm[l]) @ w_ukv[l]).reshape(b, s, MLA_HEADS, MLA_NOPE_DIM + MLA_V_DIM)
        k_nope, v = kv[..., :MLA_NOPE_DIM], kv[..., MLA_NOPE_DIM:]
        k_rot = jnp.broadcast_to(k_pe[:, :, None, :], (b, s, MLA_HEADS, MLA_ROPE_DIM))
        k = jnp.concatenate([k_nope, k_rot], axis=-1)
        q = rms_norm(q, q_norm[l])
        k = rms_norm(k, k_norm[l])
        q = jnp.concatenate([q[..., :MLA_NOPE_DIM], rope(q[..., MLA_NOPE_DIM:], positions)], axis=-1)
        k = jnp.concatenate([k[..., :MLA_NOPE_DIM], rope(k[..., MLA_NOPE_DIM:], positions)], axis=-1)
        mla = chunk_causal_softmax_attention(q, k, v)

        mixed = jnp.concatenate([rms_norm(sb, sb_out_norm[l]),
                                 rms_norm(mla, mla_out_norm[l])], axis=-1)
        x = x + mixed @ w_o[l]

        x = x + peer_ffn(rms_norm(x, ffn_norm[l]), peer_w_q[l], peer_sub_keys[l],
                         peer_u[l], peer_v[l])
    return x


HEAD_DIM = 64
N_HEADS = D_MODEL // HEAD_DIM
ML_HEADS = N_HEADS // 4
FOX_HEADS = (N_HEADS - ML_HEADS) // 2
MOBA_HEADS = N_HEADS - ML_HEADS - FOX_HEADS
FOX_W = FOX_HEADS * HEAD_DIM
ML_W = ML_HEADS * HEAD_DIM
MOBA_W = MOBA_HEADS * HEAD_DIM
ML_CHUNK = 64
ML_CONV = 4
MOBA_BLOCK = 256
MOBA_TOPK = 3
ALIBI_MAX = 8.0
D_FF = ((8 * D_MODEL // 3 + 255) // 256) * 256
SPLIT_SIZES = (FOX_W, FOX_W, FOX_W, FOX_HEADS,
               ML_W, ML_W, ML_W, ML_HEADS, ML_HEADS, ML_W,
               MOBA_W, MOBA_W, MOBA_W)
IN_COLS = sum(SPLIT_SIZES)


def _rms(x, g=None):
    xf = x.astype(jnp.float32)
    y = xf * lax.rsqrt(jnp.mean(xf * xf, axis=-1, keepdims=True) + EPS)
    return y if g is None else y * g.astype(jnp.float32)

def _to_heads(x, h):
    b, t, _ = x.shape
    return x.reshape(b, t, h, HEAD_DIM).transpose(0, 2, 1, 3)

def _from_heads(x):
    b, h, t, d = x.shape
    return x.transpose(0, 2, 1, 3).reshape(b, t, h * d)

def _alibi_slopes(h):
    return jnp.exp2(-ALIBI_MAX * jnp.arange(1, h + 1, dtype=jnp.float32) / h)

def _causal_conv(x, w, bias):
    ch = x.shape[-1]
    y = lax.conv_general_dilated(x, w.astype(x.dtype)[:, None, :], window_strides=(1,),
                                 padding=((ML_CONV - 1, 0),),
                                 dimension_numbers=('NWC', 'WIO', 'NWC'),
                                 feature_group_count=ch)
    return y + bias.astype(x.dtype)

def _fox_attention(q, k, v, f_pre):
    b, h, t, d = q.shape
    nq = t // Q_BLOCK
    logf = jax.nn.log_sigmoid(f_pre).transpose(0, 2, 1)
    cum = jnp.cumsum(logf, axis=-1)
    kpos = jnp.arange(t)
    qb = q.reshape(b, h, nq, Q_BLOCK, d).transpose(2, 0, 1, 3, 4)
    cq = cum.reshape(b, h, nq, Q_BLOCK).transpose(2, 0, 1, 3)
    starts = jnp.arange(nq) * Q_BLOCK
    scale = HEAD_DIM ** -0.5

    def block(args):
        qc, cqc, st = args
        qpos = st + jnp.arange(Q_BLOCK)
        s = jnp.einsum('bhqd,bhkd->bhqk', qc, k) * scale
        s = s + (cqc[..., None] - cum[:, :, None, :])
        s = jnp.where(kpos[None, :] <= qpos[:, None], s, -jnp.inf)
        p = jax.nn.softmax(s, axis=-1)
        return jnp.einsum('bhqk,bhkd->bhqd', p, v)

    out = lax.map(block, (qb, cq, starts))
    return out.transpose(1, 2, 0, 3, 4).reshape(b, h, t, d)

def _mlstm(q, k, v, i_pre, f_pre):
    b, h, t, d = q.shape
    nc = t // ML_CHUNK
    k = k * (d ** -0.5)
    itil = i_pre.transpose(0, 2, 1).reshape(b, h, nc, ML_CHUNK)
    logf = jax.nn.log_sigmoid(f_pre).transpose(0, 2, 1).reshape(b, h, nc, ML_CHUNK)
    bcum = jnp.cumsum(logf, axis=-1)
    bend = bcum[..., -1]
    wlog = bend[..., None] - bcum + itil
    qc = q.reshape(b, h, nc, ML_CHUNK, d)
    kc = k.reshape(b, h, nc, ML_CHUNK, d)
    vc = v.reshape(b, h, nc, ML_CHUNK, d)

    def step(carry, xs):
        cmat, nvec, m = carry
        kx, vx, wx, bx = xs
        m_new = jnp.maximum(bx + m, wx.max(-1))
        decay = jnp.exp(bx + m - m_new)
        ws = jnp.exp(wx - m_new[..., None])
        c_new = decay[..., None, None] * cmat + jnp.einsum('bhs,bhsd,bhse->bhde', ws, vx, kx)
        n_new = decay[..., None] * nvec + jnp.einsum('bhs,bhse->bhe', ws, kx)
        return (c_new, n_new, m_new), (cmat, nvec, m)

    init = (jnp.zeros((b, h, d, d), jnp.float32), jnp.zeros((b, h, d), jnp.float32),
            jnp.zeros((b, h), jnp.float32))
    xs = (kc.transpose(2, 0, 1, 3, 4), vc.transpose(2, 0, 1, 3, 4),
          wlog.transpose(2, 0, 1, 3), bend.transpose(2, 0, 1))
    _, (cs, ns, ms) = lax.scan(step, init, xs)
    cs = cs.transpose(1, 2, 0, 3, 4)
    ns = ns.transpose(1, 2, 0, 3)
    ms = ms.transpose(1, 2, 0)

    causal = jnp.tril(jnp.ones((ML_CHUNK, ML_CHUNK), dtype=bool))
    logd = bcum[..., :, None] - bcum[..., None, :] + itil[..., None, :]
    logd = jnp.where(causal, logd, -jnp.inf)
    m_inter = bcum + ms[..., None]
    m_j = jnp.maximum(m_inter, logd.max(-1))
    smat = jnp.einsum('bhcjd,bhcsd->bhcjs', qc, kc) * jnp.exp(logd - m_j[..., None])
    inter = jnp.exp(m_inter - m_j)
    num = (inter[..., None] * jnp.einsum('bhcde,bhcje->bhcjd', cs, qc)
           + jnp.einsum('bhcjs,bhcsd->bhcjd', smat, vc))
    den = inter * jnp.einsum('bhce,bhcje->bhcj', ns, qc) + smat.sum(-1)
    hout = num / jnp.maximum(jnp.abs(den), jnp.exp(-m_j))[..., None]
    return hout.reshape(b, h, t, d)

def _moba_attention(q, k, v, slopes):
    b, h, t, d = q.shape
    nb = -(-t // MOBA_BLOCK)
    pad = nb * MOBA_BLOCK - t
    kb = jnp.pad(k, ((0, 0), (0, 0), (0, pad), (0, 0))).reshape(b, h, nb, MOBA_BLOCK, d)
    vb = jnp.pad(v, ((0, 0), (0, 0), (0, pad), (0, 0))).reshape(b, h, nb, MOBA_BLOCK, d)
    kmean = kb.mean(axis=3)
    qblk = jnp.arange(t) // MOBA_BLOCK
    gate = jnp.einsum('bhtd,bhnd->bhtn', q, kmean)
    gate = jnp.where(jnp.arange(nb)[None, :] < qblk[:, None], gate, -jnp.inf)
    topk = min(MOBA_TOPK, nb)
    _, sel = lax.top_k(gate, topk)
    valid = sel < qblk[:, None]
    nq = t // Q_BLOCK
    xs = (q.reshape(b, h, nq, Q_BLOCK, d).transpose(2, 0, 1, 3, 4),
          sel.reshape(b, h, nq, Q_BLOCK, topk).transpose(2, 0, 1, 3, 4),
          valid.reshape(b, h, nq, Q_BLOCK, topk).transpose(2, 0, 1, 3, 4),
          jnp.arange(nq))
    bi = jnp.arange(b)[:, None, None, None]
    hi = jnp.arange(h)[None, :, None, None]
    scale = HEAD_DIM ** -0.5
    offs = jnp.arange(MOBA_BLOCK)

    def block(args):
        qc, selc, validc, ci = args
        qpos = ci * Q_BLOCK + jnp.arange(Q_BLOCK)
        ks = kb[bi, hi, selc]
        vs = vb[bi, hi, selc]
        kpos_sel = selc[..., None] * MOBA_BLOCK + offs
        dist_sel = (qpos[:, None, None] - kpos_sel).astype(jnp.float32)
        s_sel = (jnp.einsum('bhqd,bhqkld->bhqkl', qc, ks) * scale
                 - slopes[:, None, None, None] * dist_sel)
        s_sel = jnp.where(validc[..., None], s_sel, -jnp.inf)
        own = (ci * Q_BLOCK) // MOBA_BLOCK
        ko = lax.dynamic_index_in_dim(kb, own, axis=2, keepdims=False)
        vo = lax.dynamic_index_in_dim(vb, own, axis=2, keepdims=False)
        dist_own = qpos[:, None] - (own * MOBA_BLOCK + offs)[None, :]
        s_own = (jnp.einsum('bhqd,bhld->bhql', qc, ko) * scale
                 - slopes[:, None, None] * dist_own.astype(jnp.float32))
        s_own = jnp.where(dist_own >= 0, s_own, -jnp.inf)
        s_all = jnp.concatenate([s_sel.reshape(b, h, Q_BLOCK, topk * MOBA_BLOCK), s_own], axis=-1)
        p = jax.nn.softmax(s_all, axis=-1)
        p_sel = p[..., :topk * MOBA_BLOCK].reshape(b, h, Q_BLOCK, topk, MOBA_BLOCK)
        p_own = p[..., topk * MOBA_BLOCK:]
        return (jnp.einsum('bhqkl,bhqkld->bhqd', p_sel, vs)
                + jnp.einsum('bhql,bhld->bhqd', p_own, vo))

    out = lax.map(block, xs)
    return out.transpose(1, 2, 0, 3, 4).reshape(b, h, t, d)

def _mixer(hn, w_in, fox_f_bias, fox_q_g, fox_k_g, ml_conv_w, ml_conv_b, ml_i_bias,
           ml_f_bias, ml_h_g, moba_q_g, moba_k_g):
    proj = (hn @ w_in).astype(jnp.float32)
    idx = [int(i) for i in np.cumsum(SPLIT_SIZES)[:-1]]
    fq, fk, fv, ff, mq, mk, mv, mi, mf, mo, bq, bk, bv = jnp.split(proj, idx, axis=-1)
    y_fox = _fox_attention(_rms(_to_heads(fq, FOX_HEADS), fox_q_g),
                           _rms(_to_heads(fk, FOX_HEADS), fox_k_g),
                           _to_heads(fv, FOX_HEADS),
                           ff + fox_f_bias.astype(jnp.float32))
    qk = jax.nn.silu(_causal_conv(jnp.concatenate([mq, mk], axis=-1), ml_conv_w, ml_conv_b))
    mq, mk = jnp.split(qk, 2, axis=-1)
    h_ml = _mlstm(_to_heads(mq, ML_HEADS), _to_heads(mk, ML_HEADS), _to_heads(mv, ML_HEADS),
                  mi + ml_i_bias.astype(jnp.float32), mf + ml_f_bias.astype(jnp.float32))
    y_ml = _from_heads(_rms(h_ml)) * ml_h_g.astype(jnp.float32) * jax.nn.sigmoid(mo)
    y_moba = _moba_attention(_rms(_to_heads(bq, MOBA_HEADS), moba_q_g),
                             _rms(_to_heads(bk, MOBA_HEADS), moba_k_g),
                             _to_heads(bv, MOBA_HEADS), _alibi_slopes(MOBA_HEADS))
    return jnp.concatenate([_from_heads(y_fox), y_ml, _from_heads(y_moba)], axis=-1)

def second_inputs(seed: int = 0) -> dict:
    key = jax.random.key(seed)
    ks = jax.random.split(key, 22)
    n = jax.random.normal
    f32 = jnp.float32
    return {
        'x': n(ks[0], (BATCH, SEQ, D_MODEL), f32),
        'c': n(ks[1], (BATCH, D_MODEL), f32),
        'w_ada': n(ks[2], (DEPTH, D_MODEL, 6 * D_MODEL), f32) * (0.5 * D_MODEL ** -0.5),
        'b_ada': n(ks[3], (DEPTH, 6 * D_MODEL), f32) * 0.01,
        'norm1_g': 1.0 + 0.02 * n(ks[4], (DEPTH, D_MODEL), f32),
        'norm2_g': 1.0 + 0.02 * n(ks[5], (DEPTH, D_MODEL), f32),
        'w_in': n(ks[6], (DEPTH, D_MODEL, IN_COLS), f32) * D_MODEL ** -0.5,
        'fox_f_bias': 2.0 + 0.1 * n(ks[7], (DEPTH, FOX_HEADS), f32),
        'fox_q_g': 1.0 + 0.02 * n(ks[8], (DEPTH, HEAD_DIM), f32),
        'fox_k_g': 1.0 + 0.02 * n(ks[9], (DEPTH, HEAD_DIM), f32),
        'ml_conv_w': n(ks[10], (DEPTH, ML_CONV, 2 * ML_W), f32) * ML_CONV ** -0.5,
        'ml_conv_b': 0.01 * n(ks[11], (DEPTH, 2 * ML_W), f32),
        'ml_i_bias': 0.1 * n(ks[12], (DEPTH, ML_HEADS), f32),
        'ml_f_bias': 3.0 + 0.1 * n(ks[13], (DEPTH, ML_HEADS), f32),
        'ml_h_g': 1.0 + 0.02 * n(ks[14], (DEPTH, ML_W), f32),
        'moba_q_g': 1.0 + 0.02 * n(ks[15], (DEPTH, HEAD_DIM), f32),
        'moba_k_g': 1.0 + 0.02 * n(ks[16], (DEPTH, HEAD_DIM), f32),
        'w_out': n(ks[17], (DEPTH, D_MODEL, D_MODEL), f32) * D_MODEL ** -0.5,
        'w_gate_up': n(ks[18], (DEPTH, D_MODEL, 2 * D_FF), f32) * D_MODEL ** -0.5,
        'w_down': n(ks[19], (DEPTH, D_FF, D_MODEL), f32) * D_FF ** -0.5,
    }

def second_block(x, c, w_ada, b_ada, norm1_g, norm2_g, w_in, fox_f_bias, fox_q_g, fox_k_g,
              ml_conv_w, ml_conv_b, ml_i_bias, ml_f_bias, ml_h_g, moba_q_g, moba_k_g,
              w_out, w_gate_up, w_down):
    for l in range(DEPTH):
        mod = jax.nn.silu(c) @ w_ada[l] + b_ada[l]
        sh1, sc1, g1, sh2, sc2, g2 = jnp.split(mod[:, None, :], 6, axis=-1)
        hn = (_rms(x, norm1_g[l]) * (1 + sc1) + sh1).astype(x.dtype)
        y = _mixer(hn, w_in[l], fox_f_bias[l], fox_q_g[l], fox_k_g[l], ml_conv_w[l],
                   ml_conv_b[l], ml_i_bias[l], ml_f_bias[l], ml_h_g[l], moba_q_g[l], moba_k_g[l])
        x = x + g1 * (y.astype(x.dtype) @ w_out[l])
        hn = (_rms(x, norm2_g[l]) * (1 + sc2) + sh2).astype(x.dtype)
        gate, up = jnp.split(hn @ w_gate_up[l], 2, axis=-1)
        x = x + g2 * ((jax.nn.silu(gate) * up) @ w_down[l])
    return x


def setup_inputs(seed=0):
    out = dict(first_inputs(seed))
    for name, value in second_inputs(seed + 1).items():
        if name != "x":
            out[name + "_2"] = value
    return out


def reference(
    x, positions, attn_norm, w_in, cq_norm, w_uq, ckv_norm, w_ukv, q_norm, k_norm, sb_out_norm,
    mla_out_norm, w_o, ffn_norm, peer_w_q, peer_sub_keys, peer_u, peer_v, c_2, w_ada_2, b_ada_2,
    norm1_g_2, norm2_g_2, w_in_2, fox_f_bias_2, fox_q_g_2, fox_k_g_2, ml_conv_w_2, ml_conv_b_2,
    ml_i_bias_2, ml_f_bias_2, ml_h_g_2, moba_q_g_2, moba_k_g_2, w_out_2, w_gate_up_2, w_down_2,
):
    x = first_block(
        x, positions, attn_norm, w_in, cq_norm, w_uq, ckv_norm, w_ukv, q_norm, k_norm,
        sb_out_norm, mla_out_norm, w_o, ffn_norm, peer_w_q, peer_sub_keys, peer_u, peer_v,
    )
    return second_block(
        x, c_2, w_ada_2, b_ada_2, norm1_g_2, norm2_g_2, w_in_2, fox_f_bias_2, fox_q_g_2,
        fox_k_g_2, ml_conv_w_2, ml_conv_b_2, ml_i_bias_2, ml_f_bias_2, ml_h_g_2, moba_q_g_2,
        moba_k_g_2, w_out_2, w_gate_up_2, w_down_2,
    )


_drawn_inputs = setup_inputs


def setup_inputs(seed=0):
    import zlib

    import numpy as np

    out = dict(_drawn_inputs(seed))
    spreads = {}
    factors = {'attn_norm': 2.718,
     'cq_norm': 5.819,
     'ckv_norm': 3.772,
     'q_norm': 5.11,
     'k_norm': 5.144,
     'sb_out_norm': 5.322,
     'mla_out_norm': 5.332,
     'ffn_norm': 8.0,
     'peer_w_q': 5.248,
     'peer_sub_keys': 5.24,
     'peer_u': 5.77,
     'peer_v': 5.215,
     'b_ada_2': 7.261,
     'norm1_g_2': 8.0,
     'norm2_g_2': 22.819,
     'fox_f_bias_2': 25.389,
     'fox_q_g_2': 23.049,
     'fox_k_g_2': 25.532,
     'ml_conv_b_2': 64.0,
     'ml_i_bias_2': 64.0,
     'ml_f_bias_2': 43.493,
     'ml_h_g_2': 64.0,
     'moba_q_g_2': 24.601,
     'moba_k_g_2': 22.799,
     'ml_conv_w_2': 6.075}
    for name, (base, spread) in spreads.items():
        noise = np.random.default_rng([zlib.crc32(name.encode()), seed]).standard_normal(out[name].shape)
        drawn = base * np.exp(spread * noise) if base else spread * noise
        out[name] = __import__('jax').numpy.asarray(drawn.astype(out[name].dtype))
    for name, factor in factors.items():
        out[name] = (out[name] * factor).astype(out[name].dtype)
    return out
```

```python
from contextlib import ExitStack
import math

import numpy as np
import concourse.bass as bass
import concourse.mybir as mybir

F32 = mybir.dt.float32
BF16 = mybir.dt.bfloat16
I32 = mybir.dt.int32
U32 = mybir.dt.uint32
ALU = mybir.AluOpType
ACT = mybir.ActivationFunctionType
AX = mybir.AxisListType.X
ds = bass.ds

P = 128
T = 512
TB = T // P
D = 1024
KD = D // P
EPS = 1e-6
MASKED = -1e30

SB_H, HD = 8, 64
SB_W = SB_H * HD
MLA_H, NOPE, ROPE, MLA_QK, MLA_V = 8, 64, 32, 96, 64
Q_RANK, KV_RANK = 384, 256
IN1 = 3 * SB_W + Q_RANK + KV_RANK + ROPE
CQ0, CKV0, KPE0 = 3 * SB_W, 3 * SB_W + Q_RANK, 3 * SB_W + Q_RANK + KV_RANK
IN1_TILE, IN1_TILES = IN1 // 6, 6
CHUNK = 64

PH, PK, PN, PD = 8, 16, 128, 128

ML_H, FOX_H, MOBA_H = 4, 6, 6
SM_H = FOX_H + MOBA_H
FOX_W, ML_W, MOBA_W = FOX_H * HD, ML_H * HD, MOBA_H * HD
SM_W = FOX_W + MOBA_W
FF0 = 3 * FOX_W
MQK0 = FF0 + FOX_H
MV0 = MQK0 + 2 * ML_W
MI0 = MV0 + ML_W
MF0 = MI0 + ML_H
MO0 = MF0 + ML_H
BQ0 = MO0 + ML_W
CONV = 4
D_FF = ((8 * D // 3 + 255) // 256) * 256
KF = D_FF // P


def program(nc, a, out):
    with ExitStack() as ctx:
        def sb(name, shape, dt=F32):
            return ctx.enter_context(nc.sbuf_tensor(name, shape, dt))

        def sem(name):
            return ctx.enter_context(nc.semaphore(name))

        psum = [ctx.enter_context(nc.psum_tensor(f"bank{i}", [P, 512], F32)) for i in range(8)]

        x = sb("x", [P, TB, D])
        rows = sb("rows", [P, TB, D])
        hT = sb("hT", [P, KD, T])
        ident = sb("ident", [P, P])
        ident_bf = sb("ident_bf", [P, P], BF16)
        strict_mask = sb("strict_mask", [P, P], BF16)
        causal_mask = sb("causal_mask", [P, P], BF16)
        chunk_mask = sb("chunk_mask", [P, P], BF16)
        ones = sb("ones", [P, T])
        vec_rows = sb("vec_rows", [P, P])
        vec = sb("vec", [P, P])
        small_rows = sb("small_rows", [8, P])
        small = sb("small", [P, 8])
        cos = sb("cos", [P, TB, ROPE // 2])
        sin = sb("sin", [P, TB, ROPE // 2])
        GQ, GK = 2, 2 + SM_H
        gains = sb("gains", [P, GK + SM_H])
        silu_c = sb("silu_c", [P, KD])
        mod = sb("mod", [P, 6 * KD])
        SH1, SC1, G1, SH2, SC2, G2 = (i * KD for i in range(6))
        stat = sb("stat", [P, 2, TB])
        rstd = sb("rstd", [P, 2, TB])
        ARENA = 38000
        arena = sb("arena", [P, ARENA])

        def view(start, *dims):
            n = math.prod(dims)
            assert start + n <= ARENA, (start, dims)
            ap = arena[:, start:start + n]
            if len(dims) == 2:
                ap = ap.rearrange("p (a b) -> p a b", b=dims[1])
            if len(dims) == 3:
                ap = ap.rearrange("p (a b c) -> p a b c", b=dims[1], c=dims[2])
            return ap

        at, place = 0, {}
        pieces = [("attn_norm", D), ("cq_norm", Q_RANK), ("ckv_norm", KV_RANK), ("sb_out_norm", SB_W),
                  ("mla_out_norm", MLA_H * MLA_V), ("norm1_g_2", D), ("norm2_g_2", D), ("c_2", D),
                  ("b_ada_2", 6 * D), ("ml_conv_b_2", 2 * ML_W), ("ml_conv_w_2", CONV * 2 * ML_W)]
        for name, n in pieces:
            place[name] = (at, n // P)
            at += n // P
        N_VEC = at

        def col(name, k):
            return vec[:, place[name][0] + k:place[name][0] + k + 1]

        def counts_from_zero(sems):
            with nc.Block() as block:
                @block.gpsimd
                def _(pool):
                    for s in sems:
                        pool.sem_clear(s)

        norm_sems = [sem("norm_" + n) for n in ("squared", "mean_ready", "rstd_ready", "normed", "turned", "evacuated")]

        def norm_T(tag, src, segments, dst, dstT, gain_cols=None, shift_cols=None, gain_row=None,
                   ready=None, loads=None, scratch=None, pool_part=None):
            squared, mean_ready, rstd_ready, normed, turned, evacuated = norm_sems
            counts_from_zero(norm_sems)
            kt = sum(w for _, w in segments) // P
            ns = len(segments)
            with nc.Block() as block:
                if loads:
                    @block.sync
                    def _(sync):
                        loads(sync)

                if pool_part:
                    @block.gpsimd
                    def _(pool):
                        pool_part(pool)

                @block.scalar
                def _(act):
                    act.preload_act_table_set("natural_log_exp_and_others")
                    for tb in range(TB):
                        if ready:
                            ready(act, tb)
                        for s, (c0, w) in enumerate(segments):
                            nc.scalar.activation((dst if scratch is None else scratch)[:, tb, c0:c0 + w],
                                                 src[:, tb, c0:c0 + w], ACT.Square,
                                                 accum_out=stat[:, s, tb:tb + 1]).then_inc(squared, 1)
                    act.wait_ge(mean_ready, ns)
                    nc.scalar.activation(stat[:, 0:ns, :], stat[:, 0:ns, :], ACT.Ln)
                    act.drain()
                    nc.scalar.activation(rstd[:, 0:ns, :], stat[:, 0:ns, :], ACT.Exp,
                                         scale=-0.5).then_inc(rstd_ready, 1)
                    for k in range(kt):
                        act.wait_ge(turned, k + 1)
                        o, i = dstT[:, k, :], psum[k % 4][:, :]
                        if shift_cols is not None:
                            ins = nc.scalar.activation(o, i, ACT.Identity, scale=gain_cols(k), bias=shift_cols(k))
                        elif gain_cols is not None:
                            ins = nc.scalar.activation(o, i, ACT.Copy, scale=gain_cols(k))
                        else:
                            ins = nc.scalar.copy(o, i)
                        ins.then_inc(evacuated, 1)

                @block.vector
                def _(dve):
                    dve.wait_ge(squared, ns * TB)
                    for s, (c0, w) in enumerate(segments):
                        nc.vector.tensor_scalar(stat[:, s, :], stat[:, s, :], 1.0 / w, EPS, ALU.mult,
                                                ALU.add).then_inc(mean_ready, 1)
                    dve.wait_ge(rstd_ready, 1)
                    for tb in range(TB):
                        for s, (c0, w) in enumerate(segments):
                            o, i, r = dst[:, tb, c0:c0 + w], src[:, tb, c0:c0 + w], rstd[:, s, tb:tb + 1]
                            if gain_row is not None:
                                ins = nc.vector.scalar_tensor_tensor(out=o, in0=i, scalar=r, in1=gain_row[:, c0:c0 + w],
                                                                     op0=ALU.mult, op1=ALU.mult)
                            else:
                                ins = nc.vector.tensor_scalar(o, i, r, None, ALU.mult)
                            ins.then_inc(normed, 1)

                @block.tensor
                def _(pe):
                    cols = [c0 + j for c0, w in segments for j in range(0, w, P)]
                    pe.wait_ge(normed, ns * TB)
                    for k, c in enumerate(cols):
                        if k >= 4:
                            pe.wait_ge(evacuated, k - 3)
                        for tb in range(TB):
                            ins = nc.tensor.transpose(psum[k % 4][:, tb * P:(tb + 1) * P], dst[:, tb, c:c + P],
                                                      ident[:, :])
                        ins.then_inc(turned, 1)

        def project_rows(tag, lhsT, kt, tiles, ready=None):
            summed, by_act, by_dve = sem(tag + "summed"), sem(tag + "by_act"), sem(tag + "by_dve")

            def pe_part(pe):
                for i, (w, n, _) in enumerate(tiles):
                    if ready:
                        ready(pe, i)
                    for tb in range(TB):
                        if i >= 2:
                            pe.wait_ge(by_act if tb < 2 else by_dve, 2 * (i - 2) + tb % 2 + 1)
                        for k in range(kt(i)):
                            ins = nc.tensor.matmul(psum[4 * (i % 2) + tb][:, 0:n], lhsT(i)[:, k, tb * P:(tb + 1) * P],
                                                   w[:, k, :], start=(k == 0), stop=(k == kt(i) - 1))
                        ins.then_inc(summed, 1)

            def act_part(act):
                for i, (_, n, dst) in enumerate(tiles):
                    for tb in (0, 1):
                        act.wait_ge(summed, TB * i + tb + 1)
                        nc.scalar.copy(dst(tb), psum[4 * (i % 2) + tb][:, 0:n]).then_inc(by_act, 1)

            def dve_part(dve):
                for i, (_, n, dst) in enumerate(tiles):
                    for tb in (2, 3):
                        dve.wait_ge(summed, TB * i + tb + 1)
                        nc.vector.tensor_copy(dst(tb), psum[4 * (i % 2) + tb][:, 0:n]).then_inc(by_dve, 1)
            return pe_part, act_part, dve_part

        attention_sems = [sem("att_" + n) for n in ("staged", "q_turned", "k_turned", "q_ready", "k_ready", "scores", "half",
                                           "ready_for_exp", "probs_ready", "probs_turned", "turned_out", "summed", "stored")]

        def attention(tag, kind, heads, K, scratch, stage, q_gain, k_gain, v, dst, mask, kbias=None,
                      decay=None, qk_T=None, beside=None, loads=None):
            s0 = scratch
            q_st, k_st = view(s0, TB, 96), view(s0 + 384, TB, 96)
            qT, kT = view(s0 + 768, 512), view(s0 + 1280, 512)
            probs = view(s0 + 1792, 2, 512)
            probsT = view(s0 + 2816, 2, 512)
            work = view(s0 + 3840, 4, 512)
            peak, total = view(s0 + 5888, TB), view(s0 + 5896, TB)
            recip = view(s0 + 5904, TB)
            q_ps, k_ps = psum[0], psum[1]
            s_ps, t_ps, o_ps = [psum[2], psum[3]], [psum[4], psum[5]], [psum[6], psum[7]]
            decay_ps = [psum[0], psum[1]]
            KB = K + 1 if kbias else K
            (staged, q_turned, k_turned, q_ready, k_ready, scores, half, ready_for_exp, probs_ready, turned, turned_out,
             summed, stored) = attention_sems
            counts_from_zero(attention_sems)

            def width(tb):
                return (tb + 1) * P

            with nc.Block() as block:
                if beside or loads:
                    @block.sync
                    def _(sync):
                        loads(sync) if loads else beside[0](sync)

                if stage:
                    @block.gpsimd
                    def _(pool):
                        if kbias:
                            nc.gpsimd.memset(qT[K:K + 1, :], 1.0)
                            pool.drain().then_inc(staged, 1)
                        else:
                            pool.sem_inc(staged, 1)
                        stage(0, q_st, k_st, staged)
                        with pool.Fori(1, heads) as h:
                            pool.wait_ge(q_turned, h)
                            pool.wait_ge(k_turned, h)
                            stage(h, q_st, k_st, staged)

                @block.tensor
                def _(pe):
                    if stage:
                        pe.wait_ge(staged, 1)

                    def turn(h):
                        pe.wait_ge(staged, 2 * h + 3)
                        pe.wait_ge(q_ready, h)
                        pe.wait_ge(k_ready, h)
                        if beside:
                            pe.wait_ge(beside[3], h)
                        pe.nop(nofuse=True)
                        for tb in range(TB):
                            ins = nc.tensor.transpose(q_ps[0:K, tb * P:(tb + 1) * P], q_st[:, tb, 0:K], ident[:, :])
                        ins.then_inc(q_turned, 1)
                        for tb in range(TB):
                            ins = nc.tensor.transpose(k_ps[0:K, tb * P:(tb + 1) * P], k_st[:, tb, 0:K], ident[:, :])
                        ins.then_inc(k_turned, 1)

                    def score(h, tb):
                        n = width(tb)
                        pe.wait_ge(probs_ready, TB * h + tb + 1)
                        nc.tensor.matmul(s_ps[tb % 2][:, 0:n], qT[0:KB, tb * P:(tb + 1) * P], kT[0:KB, 0:n],
                                         start=True, stop=(kind == "mlstm"))
                        if kind == "mlstm":
                            nc.tensor.matmul(decay_ps[tb % 2][:, 0:n], ones[0:1, 0:P], decay[0](h, n),
                                             start=True, stop=False)
                        o = decay_ps if kind == "mlstm" else s_ps
                        nc.tensor.matmul(o[tb % 2][:, tb * P:n], ident_bf[:, :], mask[:, :], start=False,
                                         stop=True).then_inc(scores, 1)

                    def turn_probs(h, tb):
                        pe.wait_ge(probs_ready, TB * h + tb + 3)
                        pe.wait_ge(turned_out, TB * h + tb + 1)
                        for j in range(tb + 1):
                            ins = nc.tensor.transpose(t_ps[tb % 2][:, j * P:(j + 1) * P],
                                                      probs[:, tb % 2, j * P:(j + 1) * P], ident[:, :])
                        ins.then_inc(turned, 1)

                    def values(h, tb):
                        pe.wait_ge(turned_out, TB * h + tb + 3)
                        pe.wait_ge(stored, TB * h + tb + 1)
                        for j in range(tb + 1):
                            ins = nc.tensor.matmul(o_ps[tb % 2][:, 0:HD],
                                                   probsT[:, tb % 2, j * P:(j + 1) * P], v(j, h),
                                                   start=(j == 0), stop=(j == tb))
                        ins.then_inc(summed, 1)

                    def head(h, last):
                        pe.wait_ge(q_ready, h + 1)
                        pe.wait_ge(k_ready, h + 1)
                        score(h, 0)
                        score(h, 1)
                        if beside:
                            beside[1](pe, h, q_ps)
                        turn_probs(h, 0)
                        score(h, 2)
                        values(h, 0)
                        turn_probs(h, 1)
                        score(h, 3)
                        if stage and not last:
                            turn(h + 1)
                        values(h, 1)
                        turn_probs(h, 2)
                        values(h, 2)
                        turn_probs(h, 3)
                        values(h, 3)

                    if stage:
                        turn(0)
                    with pe.Fori(0, heads - 1) as h:
                        head(h, False)
                    head(heads - 1, True)

                @block.scalar
                def _(act):
                    if kind != "mlstm":
                        act.sem_inc(probs_ready, 2)

                    def prepare(h):
                        if stage:
                            act.wait_ge(q_turned, h + 1)
                            act.wait_ge(scores, TB * h)
                            if q_gain is None:
                                nc.scalar.activation(qT[0:K, :], q_ps[0:K, :], ACT.Copy,
                                                     scale=float(HD) ** -0.5).then_inc(q_ready, 1)
                            else:
                                nc.scalar.activation(qT[0:K, :], q_ps[0:K, :], ACT.Copy,
                                                     scale=q_gain(h)).then_inc(q_ready, 1)
                        else:
                            act.wait_ge(scores, TB * h)
                            nc.scalar.activation(qT[0:K, :], qk_T(h)[0], ACT.Copy,
                                                 scale=float(HD) ** -0.5).then_inc(q_ready, 1)

                    def block_of(h, tb):
                        n, b = width(tb), tb % 2
                        s = s_ps[b][:, 0:n]
                        if kind == "softmax":
                            act.wait_ge(ready_for_exp, TB * h + tb + 1)
                            act.wait_ge(turned, TB * h + tb + 1)
                            nc.scalar.activation(probs[:, b, 0:n], s, ACT.Exp, bias=peak[:, tb:tb + 1],
                                                 accum_out=total[:, tb:tb + 1]).then_inc(probs_ready, 1)
                        elif kind == "mlstm":
                            act.wait_ge(scores, TB * h + tb + 1)
                            act.wait_ge(probs_ready, TB * h + tb + 1)
                            nc.scalar.activation(work[:, b, 0:n], decay_ps[b][:, 0:n], ACT.Exp,
                                                 bias=decay[1](tb, h)).then_inc(half, 1)
                        else:
                            act.wait_ge(scores, TB * h + tb + 1)
                            act.wait_ge(ready_for_exp, TB * h + tb + 1)
                            nc.scalar.activation(work[:, b, 0:n], s, ACT.Abs)
                            act.drain()
                            nc.scalar.activation(work[:, b, 0:n], work[:, b, 0:n], ACT.Exp, scale=-1.0)
                            act.drain()
                            nc.scalar.activation(work[:, b, 0:n], work[:, b, 0:n], ACT.Ln,
                                                 bias=1.0).then_inc(half, 1)
                    def finish(h, tb):
                        n, b = width(tb), tb % 2
                        act.wait_ge(ready_for_exp, TB * h + tb + 3)
                        act.wait_ge(turned, TB * h + tb + 1)
                        nc.scalar.activation(probs[:, b, 0:n], work[:, 2 + b, 0:n], ACT.Exp).then_inc(probs_ready, 1)

                    def head(h, last):
                        for tb in range(TB):
                            block_of(h, tb)
                            if kind == "stick" and tb >= 1:
                                finish(h, tb - 1)
                            if tb == 3 and not last and kind != "stick":
                                prepare(h + 1)
                        if kind == "stick":
                            if not last:
                                prepare(h + 1)
                            finish(h, TB - 1)

                    prepare(0)
                    with act.Fori(0, heads - 1) as h:
                        head(h, False)
                    head(heads - 1, True)

                @block.vector
                def _(dve):
                    dve.sem_inc(turned_out, 2)
                    dve.sem_inc(stored, 2)
                    dve.sem_inc(turned, 2)
                    if kind == "mlstm":
                        dve.sem_inc(probs_ready, 2)
                    if kind == "stick":
                        dve.sem_inc(ready_for_exp, 2)

                    def prepare(h):
                        if stage:
                            dve.wait_ge(k_turned, h + 1)
                            dve.wait_ge(scores, TB * h)
                            if k_gain is None:
                                nc.vector.tensor_copy(kT[0:K, :], k_ps[0:K, :]).then_inc(k_ready, 1)
                            elif kbias:
                                nc.vector.tensor_scalar(kT[0:K, :], k_ps[0:K, :], k_gain(h), None, ALU.mult)
                                nc.vector.tensor_copy(kT[K:K + 1, :], kbias(h)).then_inc(k_ready, 1)
                            else:
                                nc.vector.tensor_scalar(kT[0:K, :], k_ps[0:K, :], k_gain(h), None,
                                                        ALU.mult).then_inc(k_ready, 1)
                        else:
                            dve.wait_ge(scores, TB * h)
                            nc.vector.tensor_copy(kT[0:K, :], qk_T(h)[1]).then_inc(k_ready, 1)

                    def first(h, tb):
                        n, b = width(tb), tb % 2
                        s = s_ps[b][:, 0:n]
                        if kind == "softmax":
                            dve.wait_ge(scores, TB * h + tb + 1)
                            nc.vector.tensor_reduce(peak[:, tb:tb + 1], s, AX, ALU.max,
                                                    negate=True).then_inc(ready_for_exp, 1)
                        elif kind == "mlstm":
                            dve.wait_ge(half, TB * h + tb + 1)
                            dve.wait_ge(turned, TB * h + tb + 1)
                            nc.vector.scalar_tensor_tensor(out=probs[:, b, 0:n], in0=s, scalar=1.0, in1=work[:, b, 0:n],
                                                           op0=ALU.mult, op1=ALU.mult,
                                                           accum_out=total[:, tb:tb + 1]).then_inc(probs_ready, 1)
                        else:
                            dve.wait_ge(half, TB * h + tb + 1)
                            dve.wait_ge(probs_ready, TB * h + tb + 1)
                            nc.vector.scalar_tensor_tensor(out=work[:, b, 0:n], in0=s, scalar=0.0, in1=work[:, b, 0:n],
                                                           op0=ALU.max, op1=ALU.add)
                            dve.drain()
                            nc.vector.tensor_tensor_scan(work[:, 2 + b, 0:n][:, ::-1], ones[:, 0:n],
                                                         work[:, b, 0:n][:, ::-1], 0.0, ALU.mult, ALU.add)
                            dve.drain()
                            nc.vector.tensor_tensor(work[:, 2 + b, 0:n], s, work[:, 2 + b, 0:n],
                                                    ALU.subtract).then_inc(ready_for_exp, 1)

                    def second(h, tb):
                        dve.wait_ge(turned, TB * h + tb + 3)
                        dve.wait_ge(summed, TB * h + tb + 1)
                        nc.vector.tensor_copy(probsT[:, tb % 2, 0:width(tb)],
                                              t_ps[tb % 2][:, 0:width(tb)]).then_inc(turned_out, 1)

                    def third(h, tb):
                        dve.wait_ge(summed, TB * h + tb + 3)
                        o = o_ps[tb % 2][:, 0:HD]
                        if kind == "stick":
                            nc.vector.tensor_copy(dst(tb, h), o).then_inc(stored, 1)
                            return
                        if kind == "mlstm":
                            nc.vector.scalar_tensor_tensor(out=recip[:, tb:tb + 1], in0=total[:, tb:tb + 1], scalar=-1.0,
                                                           in1=decay[2](tb, h), op0=ALU.mult, op1=ALU.max)
                            dve.drain()
                            nc.vector.tensor_tensor(total[:, tb:tb + 1], total[:, tb:tb + 1], recip[:, tb:tb + 1], ALU.max)
                            dve.drain()
                        nc.vector.reciprocal(recip[:, tb:tb + 1], total[:, tb:tb + 1])
                        dve.drain()
                        nc.vector.tensor_scalar(dst(tb, h), o, recip[:, tb:tb + 1], None, ALU.mult).then_inc(stored, 1)

                    def head(h, last):
                        first(h, 0)
                        first(h, 1)
                        if beside:
                            beside[2](dve, h, q_ps)
                        second(h, 0)
                        first(h, 2)
                        second(h, 1)
                        third(h, 0)
                        first(h, 3)
                        if not last:
                            prepare(h + 1)
                        second(h, 2)
                        third(h, 1)
                        third(h, 2)
                        second(h, 3)
                        third(h, 3)

                    dve.sem_inc(summed, 2)
                    prepare(0)
                    with dve.Fori(0, heads - 1) as h:
                        head(h, False)
                    head(heads - 1, True)

        w_in = view(0, KD, IN1)
        proj = view(17664, TB, IN1)
        w_uq, w_ukv = view(26496, Q_RANK // P, MLA_H * MLA_QK), view(28800, KV_RANK // P, MLA_H * (NOPE + MLA_V))
        pe_gain_q, pe_gain_k = view(37900, ROPE), view(37932, ROPE)
        ffn_gain = sb("ffn_gain", [P, D])
        ang = view(30848, 6, TB * ROPE // 2)
        pos_i = sb("pos_i", [TB, P], I32)
        pos_rows = sb("pos_rows", [TB, P])
        pos_f = sb("pos_f", [P, TB])
        inv_freq = sb("inv_freq", [P, ROPE // 2])
        w_in_loaded = [sem("w_in_even"), sem("w_in_odd")]
        up_loaded = sem("up_loaded")
        x_loaded = [sem(f"x_loaded{tb}") for tb in range(TB)]

        def load_first(sync):
            for tb in range(TB):
                sync.dma_start(x[:, tb, :], a["x"][0, tb * P:(tb + 1) * P, :]).then_inc(x_loaded[tb], 16)

        vec_loaded, vec_zeroed = sem("vec_loaded"), sem("vec_zeroed")
        pos_loaded, pos_float, pos_turned, gain_loaded = sem("pos_loaded"), sem("pos_float"), sem("pos_turned"), sem("gain_loaded")
        const_ready, vec_turned, vec_ready = sem("const_ready"), sem("vec_turned"), sem("vec_ready")
        angles, cos_sin = sem("angles"), sem("cos_sin")
        small_gains = [("q_norm", MLA_QK), ("k_norm", MLA_QK), ("fox_q_g_2", HD), ("fox_k_g_2", HD),
                       ("moba_q_g_2", HD), ("moba_k_g_2", HD)]
        TWO_PI = 2 * math.pi
        TURN = (6.28125, float(np.float32(TWO_PI - 6.28125)),
                TWO_PI - 6.28125 - float(np.float32(TWO_PI - 6.28125)))
        TO_INT = 1.5 * 2.0 ** 23

        with nc.Block() as block:
            @block.sync
            def _(sync):
                load_first(sync)
                sync.dma_start(pos_i[:, :], a["positions"][0].rearrange("(b p) -> b p", p=P)).then_inc(pos_loaded, 16)
                sync.wait_ge(vec_zeroed, 2)
                for name, n in pieces:
                    src = a[name][0]
                    if name == "ml_conv_w_2":
                        src = src.rearrange("c (r p) -> (c r) p", p=P)
                    else:
                        src = src.rearrange("(r p) -> r p", p=P)
                    r0, r = place[name]
                    sync.dma_start(vec_rows[r0:r0 + r, :], src).then_inc(vec_loaded, 16)
                for i, (name, n) in enumerate(small_gains):
                    sync.dma_start(small_rows[i:i + 1, 0:n], a[name]).then_inc(vec_loaded, 16)
                sync.dma_start(pe_gain_q, a["q_norm"][:, NOPE:].to_broadcast([P, ROPE])).then_inc(gain_loaded, 16)
                sync.dma_start(pe_gain_k, a["k_norm"][:, NOPE:].to_broadcast([P, ROPE])).then_inc(gain_loaded, 16)
                sync.dma_start(ffn_gain[:, :], a["ffn_norm"].to_broadcast([P, D])).then_inc(gain_loaded, 16)
                sync.wait_ge(gain_loaded, 48)

            @block.gpsimd
            def _(pool):
                nc.gpsimd.memset(vec_rows[:, :], 0.0).then_inc(vec_zeroed, 1)
                nc.gpsimd.memset(small_rows[:, :], 0.0).then_inc(vec_zeroed, 1)
                nc.gpsimd.memset(ident[:, :], 0.0)
                nc.gpsimd.memset(ident_bf[:, :], 0.0)
                for m in (strict_mask, causal_mask, chunk_mask):
                    nc.gpsimd.memset(m[:, :], 0.0)
                for j in range(ROPE // 2):
                    f = np.float32(1.0) / np.float32(10000.0) ** np.float32(j * 2.0 / ROPE)
                    nc.gpsimd.memset(inv_freq[:, j:j + 1], float(f))
                pool.drain()
                for m in (ident, ident_bf):
                    nc.gpsimd.affine_select(out=m[:, :], in_=m[:, :], compare_op=ALU.not_equal, fill=1.0, base=0,
                                            pattern=[[-1, P]], channel_multiplier=1)
                nc.gpsimd.affine_select(out=strict_mask[:, :], in_=strict_mask[:, :], compare_op=ALU.is_gt,
                                        fill=MASKED, base=0, pattern=[[-1, P]], channel_multiplier=1)
                nc.gpsimd.affine_select(out=causal_mask[:, :], in_=causal_mask[:, :], compare_op=ALU.is_ge,
                                        fill=MASKED, base=0, pattern=[[-1, P]], channel_multiplier=1)
                for c in range(CHUNK, P, CHUNK):
                    nc.gpsimd.memset(chunk_mask[c - CHUNK:c, c:P], MASKED)
                nc.gpsimd.memset(ones[:, :], 1.0)
                pool.drain().then_inc(const_ready, 1)

            @block.tensor
            def _(pe):
                pe.wait_ge(const_ready, 1)
                pe.wait_ge(pos_float, 1)
                nc.tensor.transpose(psum[1][:, 0:TB], pos_rows[:, :], ident[0:TB, 0:TB]).then_inc(pos_turned, 1)
                pe.wait_ge(vec_loaded, 16 * (len(pieces) + len(small_gains)))
                nc.tensor.transpose(psum[0][:, 0:P], vec_rows[:, :], ident[:, :])
                nc.tensor.transpose(psum[0][:, P:P + 8], small_rows[:, :], ident[0:8, 0:8]).then_inc(vec_turned, 1)

            @block.vector
            def _(dve):
                dve.wait_ge(pos_loaded, 16)
                nc.vector.tensor_copy(pos_rows[:, :], pos_i[:, :]).then_inc(pos_float, 1)
                dve.wait_ge(pos_turned, 1)
                nc.vector.tensor_copy(pos_f[:, :], psum[1][:, 0:TB])
                dve.wait_ge(const_ready, 1)
                dve.drain()
                n = ROPE // 2
                whole = [ang[:, i, :].rearrange("p (b j) -> p b j", j=n) for i in range(6)]
                nc.vector.tensor_tensor(whole[0], pos_f[:, :].unsqueeze(2).to_broadcast([P, TB, n]),
                                        inv_freq[:, :].unsqueeze(1).to_broadcast([P, TB, n]), ALU.mult)
                for i, (quarter, shift) in enumerate(((0.0, 0.0), (0.25, math.pi / 2))):
                    t, r = ang[:, 1 + i, :], ang[:, 3 + i, :]
                    dve.drain()
                    nc.vector.tensor_scalar(t, ang[:, 0, :], 1 / TWO_PI, quarter, ALU.mult, ALU.add)
                    dve.drain()
                    nc.vector.tensor_scalar(t, t, TO_INT, TO_INT, ALU.add, ALU.subtract)
                    dve.drain()
                    nc.vector.scalar_tensor_tensor(out=r, in0=t, scalar=-TURN[0], in1=ang[:, 0, :], op0=ALU.mult,
                                                   op1=ALU.add)
                    for part in TURN[1:]:
                        dve.drain()
                        nc.vector.scalar_tensor_tensor(out=r, in0=t, scalar=-part, in1=r, op0=ALU.mult, op1=ALU.add)
                    dve.drain()
                    nc.vector.tensor_scalar(r, r, shift, 3.1415925, ALU.add, ALU.min)
                    dve.drain()
                    nc.vector.tensor_scalar(r, r, -3.1415925, None, ALU.max).then_inc(angles, 1)
                dve.wait_ge(vec_turned, 1)
                nc.vector.tensor_copy(vec[:, :], psum[0][:, 0:P])
                nc.vector.tensor_copy(small[:, :], psum[0][:, P:P + 8]).then_inc(vec_ready, 1)
                dve.drain()
                nc.vector.tensor_scalar(gains[0:NOPE, 0:1], small[0:NOPE, 0:1], MLA_QK ** -0.5, None, ALU.mult)
                nc.vector.memset(gains[NOPE:MLA_QK, 0:1], MLA_QK ** -0.5)
                nc.vector.tensor_copy(gains[0:NOPE, 1:2], small[0:NOPE, 1:2])
                nc.vector.memset(gains[NOPE:MLA_QK, 1:2], 1.0)
                for c0, n, g, scale in ((GQ, FOX_H, 2, HD ** -0.5), (GQ + FOX_H, MOBA_H, 4, HD ** -0.5),
                                        (GK, FOX_H, 3, 1.0), (GK + FOX_H, MOBA_H, 5, 1.0)):
                    nc.vector.tensor_scalar(gains[0:HD, c0:c0 + n], small[0:HD, g:g + 1].to_broadcast([HD, n]),
                                            scale, None, ALU.mult)

            @block.scalar
            def _(act):
                act.wait_ge(angles, 2)
                nc.scalar.activation(sin[:, :, :].rearrange("p b j -> p (b j)"), ang[:, 3, :], ACT.Sin)
                nc.scalar.activation(cos[:, :, :].rearrange("p b j -> p (b j)"), ang[:, 4, :], ACT.Sin).then_inc(cos_sin, 1)
                act.wait_ge(vec_ready, 1)
                c0, n = place["c_2"]
                nc.scalar.activation(silu_c[:, :], vec[:, c0:c0 + n], ACT.Silu)

        def load_w_in(sync):
            w = a["w_in"][0].rearrange("(k p) n -> p k n", p=P)
            for i in range(IN1_TILES):
                c = i * IN1_TILE
                if i >= 2:
                    sync.wait_ge(w_in_loaded[i % 2], 16 * (i // 2))
                sync.dma_start(w_in[:, :, c:c + IN1_TILE], w[:, :, c:c + IN1_TILE]).then_inc(w_in_loaded[i % 2], 16)
            sync.dma_start(w_uq, a["w_uq"][0].rearrange("(k p) n -> p k n", p=P)).then_inc(up_loaded, 16)
            sync.dma_start(w_ukv, a["w_ukv"][0].rearrange("(k p) n -> p k n", p=P)).then_inc(up_loaded, 16)

        norm_T("n1_", x, [(0, D)], rows, hT, gain_cols=lambda k: col("attn_norm", k),
               ready=lambda act, tb: act.wait_ge(x_loaded[tb], 16), loads=load_w_in)

        in_summed, in_by_act, in_by_dve = sem("in_summed"), sem("in_by_act"), sem("in_by_dve")
        with nc.Block() as block:
            @block.tensor
            def _(pe):
                with pe.Fori(0, IN1_TILES // 2) as i:
                    for odd in range(2):
                        pe.wait_ge(w_in_loaded[odd], 16 * i + 16)
                        for tb in range(TB):
                            pe.wait_ge(in_by_act if tb < 2 else in_by_dve, 4 * i + 2 * odd + tb % 2 + 1)
                            for k in range(KD):
                                ins = nc.tensor.matmul(psum[4 * odd + tb][:, 0:IN1_TILE], hT[:, k, tb * P:(tb + 1) * P],
                                                       w_in[:, k, ds((2 * i + odd) * IN1_TILE, IN1_TILE)],
                                                       start=(k == 0), stop=(k == KD - 1))
                            ins.then_inc(in_summed, 1)

            @block.scalar
            def _(act):
                act.sem_inc(in_by_act, 4)
                with act.Fori(0, IN1_TILES // 2) as i:
                    for odd in range(2):
                        for tb in (0, 1):
                            act.wait_ge(in_summed, 8 * i + TB * odd + tb + 1)
                            nc.scalar.copy(proj[:, tb, ds((2 * i + odd) * IN1_TILE, IN1_TILE)],
                                           psum[4 * odd + tb][:, 0:IN1_TILE]).then_inc(in_by_act, 1)

            @block.vector
            def _(dve):
                dve.sem_inc(in_by_dve, 4)
                with dve.Fori(0, IN1_TILES // 2) as i:
                    for odd in range(2):
                        for tb in (2, 3):
                            dve.wait_ge(in_summed, 8 * i + TB * odd + tb + 1)
                            nc.vector.tensor_copy(proj[:, tb, ds((2 * i + odd) * IN1_TILE, IN1_TILE)],
                                                  psum[4 * odd + tb][:, 0:IN1_TILE]).then_inc(in_by_dve, 1)

        ADA_TILE = 6 * D // (2 * SB_H)
        ADA_COLS = ADA_TILE // P
        ada_w = [view(0, KD, ADA_TILE), view(KD * ADA_TILE, KD, ADA_TILE)]
        ada_loaded = [sem("ada_loaded0"), sem("ada_loaded1")]
        ada_summed, ada_stored = sem("ada_summed"), sem("ada_stored")

        def ada_load(sync):
            w = a["w_ada_2"][0].rearrange("(k p) n -> p k n", p=P)
            for i in range(2):
                sync.dma_start(ada_w[i], w[:, :, i * ADA_TILE:(i + 1) * ADA_TILE]).then_inc(ada_loaded[i], 16)
            with sync.Fori(1, SB_H) as h:
                for i in range(2):
                    sync.wait_ge(ada_summed, h)
                    sync.dma_start(ada_w[i], w[:, :, ds((2 * h + i) * ADA_TILE, ADA_TILE)]).then_inc(ada_loaded[i], 16)

        def ada_product(pe, h, bank):
            for i in range(2):
                pe.wait_ge(ada_loaded[i], 16 * h + 16)
                for c in range(ADA_COLS):
                    for k in range(KD):
                        ins = nc.tensor.matmul(bank[:, i * ADA_COLS + c:i * ADA_COLS + c + 1],
                                               ada_w[i][:, k, c * P:(c + 1) * P], silu_c[:, k:k + 1],
                                               start=(k == 0), stop=(k == KD - 1))
            ins.then_inc(ada_summed, 1)

        def ada_store(dve, h, bank):
            dve.wait_ge(ada_summed, h + 1)
            n = 2 * ADA_COLS
            nc.vector.tensor_tensor(mod[:, ds(h * n, n)], bank[:, 0:n],
                                    vec[:, ds(h * n + place["b_ada_2"][0], n)], ALU.add).then_inc(ada_stored, 1)

        def stage_sb(h, q_st, k_st, staged):
            nc.gpsimd.tensor_copy(q_st[:, :, 0:HD], proj[:, :, ds(h * HD, HD)]).then_inc(staged, 1)
            nc.gpsimd.tensor_copy(k_st[:, :, 0:HD], proj[:, :, ds(h * HD + SB_W, HD)]).then_inc(staged, 1)

        SCRATCH1 = 30848
        attention("sb_", "stick", SB_H, HD, SCRATCH1, stage_sb, None, None,
                  v=lambda j, h: proj[:, j, ds(h * HD + 2 * SB_W, HD)],
                  dst=lambda tb, h: rows[:, tb, ds(h * HD, HD)], mask=strict_mask,
                  beside=(ada_load, ada_product, ada_store, ada_stored))

        latent = view(0, TB, IN1)
        q_up, kv_up = view(8832, TB, MLA_H * MLA_QK), view(11904, TB, MLA_H * (NOPE + MLA_V))
        squares_q, squares_k = view(0, TB * MLA_H, MLA_QK), view(3072, TB * MLA_H, NOPE)
        q_pe, t_pe = view(5120, TB * MLA_H, ROPE), view(6144, 4, TB * MLA_H * ROPE // 2)
        k_pe, u_pe = view(8192, TB, ROPE), view(8320, 4, TB * ROPE // 2)
        pe_rot = view(16000, TB, ROPE)
        ss_q, ss_k = view(16128, TB * MLA_H), view(16160, TB * MLA_H)
        ss_pe = view(16192, TB)
        pe_junk = view(16196, TB, ROPE)
        rms_q, rms_k = view(16324, TB, MLA_H), view(16356, TB, MLA_H)
        KQ, KKV = Q_RANK // P, KV_RANK // P

        norm_T("n2_", proj, [(CQ0, Q_RANK), (CKV0, KV_RANK)], latent, hT, gain_cols=lambda k: col("cq_norm", k))

        up_tiles = [(w_uq[:, :, i * 384:(i + 1) * 384], 384, lambda tb, i=i: q_up[:, tb, i * 384:(i + 1) * 384])
                    for i in range(2)]
        up_tiles += [(w_ukv[:, :, i * 512:(i + 1) * 512], 512, lambda tb, i=i: kv_up[:, tb, i * 512:(i + 1) * 512])
                     for i in range(2)]
        up_pe, up_act, up_dve = project_rows("up_", lambda i: hT[:, 0:KQ, :] if i < 2 else hT[:, KQ:KQ + KKV, :],
                                             lambda i: KQ if i < 2 else KKV, up_tiles,
                                             ready=lambda pe, i: pe.wait_ge(up_loaded, 32))
        with nc.Block() as block:
            @block.tensor
            def _(pe):
                up_pe(pe)

            @block.scalar
            def _(act):
                up_act(act)

            @block.vector
            def _(dve):
                up_dve(dve)

        squared, rms_mean, rms_ready, rotated = sem("squared"), sem("rms_mean"), sem("rms_ready"), sem("rotated")
        with nc.Block() as block:
            q_heads = q_up.rearrange("p b (h d) -> p (b h) d", d=MLA_QK)
            kv_heads = kv_up.rearrange("p b (h d) -> p (b h) d", d=NOPE + MLA_V)
            HALF = ROPE // 2

            @block.scalar
            def _(act):
                nc.scalar.activation(squares_q, q_heads, ACT.Square).then_inc(squared, 1)
                nc.scalar.activation(squares_k, kv_heads[:, :, 0:NOPE], ACT.Square)
                for tb in range(TB):
                    ins = nc.scalar.activation(pe_junk[:, tb, :], proj[:, tb, KPE0:KPE0 + ROPE], ACT.Square,
                                               accum_out=ss_pe[:, tb:tb + 1])
                ins.then_inc(squared, 1)
                for i, (ss, rms) in enumerate(((ss_q, rms_q), (ss_k, rms_k))):
                    act.wait_ge(rms_mean, i + 1)
                    nc.scalar.activation(ss, ss, ACT.Ln)
                    act.drain()
                    nc.scalar.activation(rms.rearrange("p b h -> p (b h)"), ss, ACT.Exp, scale=-0.5)

            @block.vector
            def _(dve):
                dve.wait_ge(squared, 1)
                nc.vector.tensor_reduce(ss_q, squares_q, AX, ALU.add)
                dve.drain()
                nc.vector.tensor_scalar(ss_q, ss_q, 1.0 / MLA_QK, EPS, ALU.mult, ALU.add).then_inc(rms_mean, 1)
                dve.wait_ge(squared, 2)
                nc.vector.tensor_reduce(ss_k, squares_k, AX, ALU.add)
                dve.drain()
                by_head = ss_k.rearrange("p (b h) -> p b h", h=MLA_H)
                nc.vector.tensor_tensor(by_head, by_head, ss_pe.unsqueeze(2).to_broadcast([P, TB, MLA_H]), ALU.add)
                dve.drain()
                nc.vector.tensor_scalar(ss_k, ss_k, 1.0 / MLA_QK, EPS, ALU.mult, ALU.add).then_inc(rms_mean, 1)
                n = TB * MLA_H
                nc.vector.tensor_tensor(q_pe, q_heads[:, :, NOPE:MLA_QK], pe_gain_q.unsqueeze(1).to_broadcast([P, n, ROPE]),
                                        ALU.mult)
                dve.drain()
                x1 = q_pe[:, :, 0:HALF].rearrange("p (b h) d -> p b h d", h=MLA_H)
                x2 = q_pe[:, :, HALF:ROPE].rearrange("p (b h) d -> p b h d", h=MLA_H)
                c = cos[:, :, :].unsqueeze(2).to_broadcast([P, TB, MLA_H, HALF])
                s = sin[:, :, :].unsqueeze(2).to_broadcast([P, TB, MLA_H, HALF])
                t = [t_pe[:, i, :].rearrange("p (b h d) -> p b h d", h=MLA_H, d=HALF) for i in range(4)]
                for o, u, w in zip(t, (x1, x2, x1, x2), (c, s, s, c)):
                    nc.vector.tensor_tensor(o, u, w, ALU.mult)
                dve.drain()
                flat = [t_pe[:, i, :].rearrange("p (n d) -> p n d", d=HALF) for i in range(4)]
                nc.vector.tensor_tensor(q_heads[:, :, NOPE:NOPE + HALF], flat[0], flat[1], ALU.subtract)
                nc.vector.tensor_tensor(q_heads[:, :, NOPE + HALF:MLA_QK], flat[2], flat[3], ALU.add)

            @block.gpsimd
            def _(pool):
                nc.gpsimd.tensor_tensor(k_pe, proj[:, :, KPE0:KPE0 + ROPE],
                                        pe_gain_k.unsqueeze(1).to_broadcast([P, TB, ROPE]), ALU.mult)
                pool.drain()
                x1, x2 = k_pe[:, :, 0:HALF], k_pe[:, :, HALF:ROPE]
                t = [u_pe[:, i, :].rearrange("p (b d) -> p b d", d=HALF) for i in range(4)]
                for o, u, w in zip(t, (x1, x2, x1, x2), (cos, sin, sin, cos)):
                    nc.gpsimd.tensor_tensor(o, u, w[:, :, :], ALU.mult)
                pool.drain()
                nc.gpsimd.tensor_tensor(pe_rot[:, :, 0:HALF], t[0], t[1], ALU.subtract)
                nc.gpsimd.tensor_tensor(pe_rot[:, :, HALF:ROPE], t[2], t[3], ALU.add)

        w_o = view(17664, KD, D)
        w_o_loaded, keys_loaded = sem("w_o_loaded"), sem("keys_loaded")
        w_q = view(26496, KD, 2 * PD)
        w_q_loaded = sem("w_q_loaded")

        def stage_mla(h, q_st, k_st, staged):
            nc.gpsimd.tensor_tensor(q_st, q_up[:, :, ds(h * MLA_QK, MLA_QK)],
                                    rms_q[:, :, ds(h, 1)].to_broadcast([P, TB, MLA_QK]), ALU.mult).then_inc(staged, 1)
            nc.gpsimd.tensor_tensor(k_st[:, :, 0:NOPE], kv_up[:, :, ds(h * (NOPE + MLA_V), NOPE)],
                                    rms_k[:, :, ds(h, 1)].to_broadcast([P, TB, NOPE]), ALU.mult)
            nc.gpsimd.tensor_tensor(k_st[:, :, NOPE:MLA_QK], pe_rot,
                                    rms_k[:, :, ds(h, 1)].to_broadcast([P, TB, ROPE]), ALU.mult).then_inc(staged, 1)

        def load_w_o(sync):
            sync.dma_start(w_o, a["w_o"][0].rearrange("(k p) n -> p k n", p=P)).then_inc(w_o_loaded, 16)
            sync.dma_start(w_q, a["peer_w_q"][0].rearrange("(k p) n -> p k n", p=P)[:, :, 0:2 * PD])\
                .then_inc(w_q_loaded, 16)

        attention("mla_", "softmax", MLA_H, MLA_QK, SCRATCH1, stage_mla, lambda h: gains[0:MLA_QK, 0:1],
                  lambda h: gains[0:MLA_QK, 1:2],
                  v=lambda j, h: kv_up[:, j, ds(h * (NOPE + MLA_V) + NOPE, MLA_V)],
                  dst=lambda tb, h: rows[:, tb, ds(h * MLA_V + SB_W, MLA_V)], mask=chunk_mask,
                  loads=load_w_o)

        key_rows = view(32896, 2 * PH, PD)
        keysT = view(30848, 2 * PH, PN)

        def load_keys(sync):
            sync.dma_start(key_rows, a["peer_sub_keys"][0].rearrange("c h n d -> n (c h) d")).then_inc(keys_loaded, 16)

        norm_T("n3_", rows, [(0, SB_W), (SB_W, MLA_H * MLA_V)], rows, hT,
               gain_cols=lambda k: col("sb_out_norm", k), loads=load_keys, scratch=view(0, TB, D))

        def out_projection(tag, w, order, loaded, gate_row=None):
            summed, added, gated = sem(tag + "summed"), sem(tag + "added"), view(0, 2, 512)
            with nc.Block() as block:
                @block.tensor
                def _(pe):
                    pe.wait_ge(loaded, 16)
                    for half in range(2):
                        for tb in range(TB):
                            for k in range(KD):
                                ins = nc.tensor.matmul(psum[4 * half + tb][:, :], hT[:, k, tb * P:(tb + 1) * P],
                                                       w[:, order[k], half * 512:(half + 1) * 512], start=(k == 0),
                                                       stop=(k == KD - 1))
                            ins.then_inc(summed, 1)

                @block.vector
                def _(dve):
                    for half in range(2):
                        c = slice(half * 512, (half + 1) * 512)
                        for tb in range(TB):
                            dve.wait_ge(summed, TB * half + tb + 1)
                            y = psum[4 * half + tb][:, :]
                            if gate_row is not None:
                                nc.vector.tensor_tensor(gated[:, tb % 2, :], y, gate_row[:, c], ALU.mult)
                                dve.drain()
                                y = gated[:, tb % 2, :]
                            nc.vector.tensor_tensor(x[:, tb, c], x[:, tb, c], y, ALU.add)

        out_projection("o1_", w_o, range(KD), w_o_loaded)
        norm_T("n4_", x, [(0, D)], rows, hT, gain_row=ffn_gain)

        RING = 8
        u_ring, v_ring = view(0, RING, D), view(RING * D, RING, D)
        diag = view(16384, RING, P)
        q_T = view(17664, 2, T)
        half_sc = view(34944, 2, TB * PN)
        TK = 35968
        left = view(TK, PN)
        cand, cand_left = view(TK + 128, PK, PK), view(TK + 384, PK * PK)
        picked = view(TK + 640, 2, PK * PK)
        half_top, half_at = view(TK + 1152, 2, PK), view(TK + 1184, 2, PK)
        best, best_exp, best_neg, best_sum = (view(TK + 1216, PK), view(TK + 1232, PK), view(TK + 1248, 1),
                                              view(TK + 1249, 1))
        pos, pos_f2, ids = view(TK + 1250, 2, PK), view(TK + 1282, 2, PK), view(TK + 1314, 2, PK)
        iota16 = view(TK + 1346, PK)
        iota16_i = view(TK + 1362, PK).bitcast(I32)
        best_at = view(TK + 1378, PK).bitcast(U32)
        half_at_u = view(TK + 1394, 2, PK).bitcast(U32)
        share = view(TK + 1426, TB, PK)
        expert = view(TK + 1490, TB, PK).bitcast(I32)
        pre, gelu = view(TK + 1554, PK), view(TK + 1570, PK)
        coef = view(TK + 1586, 2, PK)
        assert TK + 1618 <= 37900
        STEPS = PH * TB

        keys_turned, keys_ready, iota_ready = sem("keys_turned"), sem("keys_ready"), sem("iota_ready")
        q_summed, q_copied, sc_summed, sc_copied = sem("q_summed"), sem("q_copied"), sem("sc_summed"), sem("sc_copied")
        best_ready, exp_done, chosen = sem("best_ready"), sem("exp_done"), sem("chosen")
        u_in = [sem(f"u_in{i}") for i in range(RING)]
        v_in = [sem(f"v_in{i}") for i in range(RING)]
        u_used, v_used, pre_ready, gelu_ready = sem("u_used"), sem("v_used"), sem("pre_ready"), sem("gelu_ready")
        coef_ready, diag_ready, y_added = sem("coef_ready"), sem("diag_ready"), sem("y_added")

        with nc.Block() as block:
            @block.sync
            def _(sync):
                w = a["peer_w_q"][0].rearrange("(k p) n -> p k n", p=P)
                with sync.Fori(1, PH) as h:
                    sync.wait_ge(q_summed, 2 * h)
                    sync.dma_start(w_q, w[:, :, ds(h * 2 * PD, 2 * PD)]).then_inc(w_q_loaded, 16)

            @block.gpsimd
            def _(pool):
                nc.gpsimd.iota(iota16_i, [[1, PK]], base=0, channel_multiplier=0).then_inc(iota_ready, 1)

                def gather(table, slot, step, j):
                    tb = step[1]
                    ring, used, arrived = (u_ring, u_used, u_in) if table == "peer_u" else (v_ring, v_used, v_in)
                    pool.wait_ge(used, step[0] * PK + j + 1)
                    if j == 0 and table == "peer_u":
                        pool.wait_ge(chosen, step[0] + 1)
                    pool.nop(nofuse=True)
                    nc.gpsimd.indirect_dma_start(
                        out=ring[:, slot, :], out_offset=None, in_=a[table][0],
                        in_offset=bass.IndirectOffsetOnAxis(ap=expert[:, tb, j:j + 1], axis=0),
                    ).then_inc(arrived[slot], 16)

                def step_of(h, tb, last):
                    for j in range(PK):
                        gather("peer_v", j % RING, (TB * h + tb, tb), j)
                        if not last:
                            gather("peer_u", j % RING, (TB * h + tb + 1, (tb + 1) % TB), j)

                for j in range(PK):
                    gather("peer_u", j % RING, (0, 0), j)
                with pool.Fori(0, PH - 1) as h:
                    for tb in range(TB):
                        step_of(h, tb, False)
                for tb in range(TB):
                    step_of(PH - 1, tb, tb == TB - 1)

            @block.tensor
            def _(pe):
                pe.wait_ge(keys_loaded, 16)
                for g in range(4):
                    for i in range(4):
                        ins = nc.tensor.transpose(psum[g][:, i * PN:(i + 1) * PN], key_rows[:, 4 * g + i, :], ident[:, :])
                    ins.then_inc(keys_turned, 1)

                def query(h):
                    pe.wait_ge(w_q_loaded, 16 * h + 16)
                    for c in range(2):
                        for k in range(KD):
                            ins = nc.tensor.matmul(psum[4 + c][:, :], w_q[:, k, c * PD:(c + 1) * PD], hT[:, k, :],
                                                   start=(k == 0), stop=(k == KD - 1))
                        ins.then_inc(q_summed, 1)
                    for c in range(2):
                        pe.wait_ge(q_copied, 2 * h + c + 1)
                        for tb in range(TB):
                            ins = nc.tensor.matmul(psum[6 + c][:, tb * PN:(tb + 1) * PN], q_T[:, c, tb * P:(tb + 1) * P],
                                                   keysT[:, ds(h + c * PH, 1), :].squeeze(1), start=True, stop=True)
                        ins.then_inc(sc_summed, 1)

                def values(h, tb):
                    step = TB * h + tb
                    pe.wait_ge(y_added, step + 1)
                    for j in range(PK):
                        pe.wait_ge(v_in[j % RING], step * 32 + 16 * (j // RING) + 16)
                        pe.wait_ge(diag_ready, step * PK + j + 1)
                        for half in range(2):
                            ins = nc.tensor.matmul(psum[2 * (tb % 2) + half][:, :], diag[:, j % RING, :],
                                                   v_ring[:, j % RING, half * 512:(half + 1) * 512], start=(j == 0),
                                                   stop=(j == PK - 1))
                        ins.then_inc(v_used, 1)

                pe.wait_ge(keys_ready, 4)
                query(0)
                with pe.Fori(0, PH - 1) as h:
                    query(h + 1)
                    for tb in range(TB):
                        values(h, tb)
                for tb in range(TB):
                    values(PH - 1, tb)

            @block.scalar
            def _(act):
                act.sem_inc(v_used, RING)
                for g in range(4):
                    act.wait_ge(keys_turned, g + 1)
                    nc.scalar.copy(keysT[:, 4 * g:4 * g + 4, :].rearrange("p a b -> p (a b)"),
                                   psum[g][:, :]).then_inc(keys_ready, 1)

                def query(h):
                    for c in range(2):
                        act.wait_ge(q_summed, 2 * h + c + 1)
                        nc.scalar.copy(q_T[:, c, :], psum[4 + c][:, :]).then_inc(q_copied, 1)
                    act.wait_ge(chosen, TB * h)
                    for c in range(2):
                        act.wait_ge(sc_summed, 2 * h + c + 1)
                        nc.scalar.copy(half_sc[:, c, :], psum[6 + c][:, :]).then_inc(sc_copied, 1)

                def share_exp(step):
                    act.wait_ge(best_ready, step + 1)
                    nc.scalar.activation(best_exp, best, ACT.Exp, bias=best_neg, accum_out=best_sum).then_inc(exp_done, 1)

                def gelus(step):
                    act.wait_ge(pre_ready, step + 1)
                    nc.scalar.activation(gelu, pre, ACT.Gelu).then_inc(gelu_ready, 1)

                def diags(h, tb):
                    step = TB * h + tb
                    act.wait_ge(coef_ready, step + 1)
                    for j in range(PK):
                        act.wait_ge(v_used, step * PK + j + 1)
                        nc.scalar.activation(diag[:, j % RING, :], ident[:, :], ACT.Copy,
                                             scale=coef[:, tb % 2, j:j + 1]).then_inc(diag_ready, 1)

                query(0)
                share_exp(0)
                share_exp(1)
                gelus(0)
                share_exp(2)
                share_exp(3)
                with act.Fori(0, PH - 1) as h:
                    query(h + 1)
                    for tb in range(TB):
                        diags(h, tb)
                        gelus(TB * h + tb + 1)
                        share_exp(TB * h + tb + TB)
                for tb in range(TB):
                    diags(PH - 1, tb)
                    if tb < TB - 1:
                        gelus(TB * (PH - 1) + tb + 1)

            @block.vector
            def _(dve):
                dve.sem_inc(u_used, RING)
                dve.sem_inc(y_added, 2)
                dve.wait_ge(iota_ready, 1)
                nc.vector.tensor_copy(iota16, iota16_i)

                def top16(values_in, rest, top, at):
                    nc.vector.max(top[:, 0:8], values_in)
                    dve.drain()
                    nc.vector.max_index(at[:, 0:8], top[:, 0:8], values_in)
                    nc.vector.match_replace(rest, top[:, 0:8], values_in, -3.0e38)
                    dve.drain()
                    nc.vector.max(top[:, 8:16], rest)
                    dve.drain()
                    nc.vector.max_index(at[:, 8:16], top[:, 8:16], rest)

                def choose(h, tb):
                    dve.drain()
                    if tb == 0:
                        dve.wait_ge(sc_copied, 2 * h + 2)
                        dve.nop(nofuse=True)
                    for c in range(2):
                        top16(half_sc[:, c, tb * PN:(tb + 1) * PN], left, half_top[:, c, :], half_at_u[:, c, :])
                    dve.drain()
                    nc.vector.tensor_copy(half_at, half_at_u)
                    nc.vector.tensor_tensor(cand, half_top[:, 0, :].unsqueeze(2).to_broadcast([P, PK, PK]),
                                            half_top[:, 1, :].unsqueeze(1).to_broadcast([P, PK, PK]), ALU.add)
                    dve.drain()
                    top16(cand.rearrange("p a b -> p (a b)"), cand_left, best, best_at)
                    dve.drain()
                    nc.vector.tensor_scalar(best_neg, best[:, 0:1], -1.0, None, ALU.mult).then_inc(best_ready, 1)
                    nc.vector.tensor_scalar(pos[:, 0, :].bitcast(U32), best_at, 4, None, ALU.logical_shift_right)
                    nc.vector.tensor_scalar(pos[:, 1, :].bitcast(U32), best_at, PK - 1, None, ALU.bitwise_and)
                    dve.drain()
                    nc.vector.tensor_copy(pos_f2, pos.bitcast(U32))
                    dve.drain()
                    for c in range(2):
                        nc.vector.tensor_tensor(picked[:, c, :].rearrange("p (k m) -> p k m", m=PK),
                                                pos_f2[:, c, :].unsqueeze(2).to_broadcast([P, PK, PK]),
                                                iota16.unsqueeze(1).to_broadcast([P, PK, PK]), ALU.is_equal)
                    dve.drain()
                    for c in range(2):
                        p = picked[:, c, :].rearrange("p (k m) -> p k m", m=PK)
                        nc.vector.tensor_tensor(p, p, half_at[:, c, :].unsqueeze(1).to_broadcast([P, PK, PK]), ALU.mult)
                    dve.drain()
                    nc.vector.tensor_reduce(ids.rearrange("p c k -> p (c k)"),
                                            picked.rearrange("p c (k m) -> p (c k) m", m=PK), AX, ALU.add)
                    dve.drain()
                    nc.vector.scalar_tensor_tensor(out=expert[:, tb, :], in0=ids[:, 0, :], scalar=float(PN),
                                                   in1=ids[:, 1, :], op0=ALU.mult, op1=ALU.add)
                    dve.wait_ge(exp_done, TB * h + tb + 1)
                    nc.vector.reciprocal(best_sum, best_sum)
                    dve.drain()
                    nc.vector.tensor_scalar(share[:, tb, :], best_exp, best_sum, None, ALU.mult).then_inc(chosen, 1)

                def dots(step, tb):
                    for j in range(PK):
                        dve.wait_ge(u_in[j % RING], step * 32 + 16 * (j // RING) + 16)
                        ins = nc.vector.scalar_tensor_tensor(out=u_ring[:, j % RING, :], in0=u_ring[:, j % RING, :],
                                                             scalar=1.0, in1=rows[:, tb, :], op0=ALU.mult,
                                                             op1=ALU.mult, accum_out=pre[:, j:j + 1])
                        ins.then_inc(u_used, 1)
                    dve.drain().then_inc(pre_ready, 1)
                    dve.wait_ge(gelu_ready, step + 1)
                    nc.vector.tensor_tensor(coef[:, tb % 2, :], gelu, share[:, tb, :], ALU.mult).then_inc(coef_ready, 1)

                def add(step, tb):
                    dve.wait_ge(v_used, RING + (step + 1) * PK)
                    for half in range(2):
                        c = slice(half * 512, (half + 1) * 512)
                        ins = nc.vector.tensor_tensor(x[:, tb, c], x[:, tb, c], psum[2 * (tb % 2) + half][:, :], ALU.add)
                    ins.then_inc(y_added, 1)

                choose(0, 0)
                choose(0, 1)
                dots(0, 0)
                choose(0, 2)
                choose(0, 3)
                with dve.Fori(0, PH - 1) as h:
                    for tb in range(TB):
                        dots(TB * h + tb + 1, (tb + 1) % TB)
                        add(TB * h + tb, tb)
                        choose(h + 1, tb)
                for tb in range(TB):
                    if tb < TB - 1:
                        dots(TB * (PH - 1) + tb + 1, tb + 1)
                    add(TB * (PH - 1) + tb, tb)

        proj2 = view(0, TB, 3 * SM_W)
        mvo = view(9216, TB, 2 * ML_W)
        conv_in = view(11264, 4, CONV - 1 + T)
        conv_out = view(13324, 4, T)
        ml_q, ml_k = view(15372, ML_H, T), view(17420, ML_H, T)
        w_mqk, w_gates = view(19468, KD, 2 * ML_W), view(23564, KD, 72)
        kbias = view(19468, SM_H, T)
        w_mvo = view(31756, KD, 2 * ML_W)
        gate_pre, gate_t, cum, log_f, ml_a = (view(25612 + i * T, T) for i in range(5))
        ml_m, ml_floor, mi_rows = (view(28172 + i * T, T) for i in range(3))
        a_rows = view(29708, ML_H, T)
        w_2 = [view(31756 - 1536, KD, 384), view(31756 - 1536 + KD * 384, KD, 384)]
        SCRATCH2 = 31756
        SMALL2 = 37700
        gate_bias = view(SMALL2, 1)
        ml_cols = view(SMALL2 + 4, 2, TB, ML_H)
        ss_2 = view(SMALL2 + 36, 2, TB, SM_H)
        rms_2 = view(SMALL2 + 132, 2, TB, SM_H)
        assert SMALL2 + 228 <= ARENA
        w_2_loaded = [sem("w_fox_loaded"), sem("w_moba_loaded")]
        w_ml_loaded, bias_loaded, gates_zeroed = sem("w_ml_loaded"), sem("bias_loaded"), sem("gates_zeroed")
        in2_summed, in2_by_act, in2_by_dve = sem("in2_summed"), sem("in2_by_act"), sem("in2_by_dve")
        w_in_2 = a["w_in_2"][0].rearrange("(k p) n -> p k n", p=P)
        MI, MF = 64, 32

        mod_gain = sb("mod_gain", [P, 2 * KD])

        def modulated_gain(tag, norm, scale0, g0):
            with nc.Block() as block:
                @block.vector
                def _(dve):
                    c0, n = place[norm]
                    nc.vector.scalar_tensor_tensor(out=mod_gain[:, g0:g0 + KD], in0=mod[:, scale0:scale0 + KD],
                                                   scalar=1.0, in1=vec[:, c0:c0 + n], op0=ALU.add, op1=ALU.mult)

        modulated_gain("g1_", "norm1_g_2", SC1, 0)
        modulated_gain("g2_", "norm2_g_2", SC2, KD)

        def load_ml(sync):
            sync.wait_ge(gates_zeroed, 2)
            for c0, n, at in ((FF0, FOX_H, 0), (MF0, ML_H, MF), (MI0, ML_H, MI)):
                sync.dma_start(w_gates[:, :, at:at + n], w_in_2[:, :, c0:c0 + n]).then_inc(w_ml_loaded, 16)
            sync.dma_start(w_mqk, w_in_2[:, :, MQK0:MQK0 + 2 * ML_W]).then_inc(w_ml_loaded, 16)
            for name, n, at in (("fox_f_bias_2", FOX_H, 0), ("ml_f_bias_2", ML_H, MF), ("ml_i_bias_2", ML_H, MI)):
                sync.dma_start(gate_bias[at:at + n, :], a[name].rearrange("o n -> n o")).then_inc(bias_loaded, 16)

        def zero_gates(pool):
            nc.gpsimd.memset(w_gates, 0.0).then_inc(gates_zeroed, 1)
            nc.gpsimd.memset(gate_bias, 0.0).then_inc(gates_zeroed, 1)

        norm_T("n5_", x, [(0, D)], rows, hT, gain_cols=lambda k: mod_gain[:, k:k + 1],
               shift_cols=lambda k: mod[:, SH1 + k:SH1 + k + 1], loads=load_ml, pool_part=zero_gates)

        with nc.Block() as block:
            @block.sync
            def _(sync):
                for odd, c0 in enumerate((0, BQ0)):
                    sync.dma_start(w_2[odd], w_in_2[:, :, c0:c0 + 384]).then_inc(w_2_loaded[odd], 16)
                with sync.Fori(1, 3) as i:
                    for odd, c0 in enumerate((0, BQ0)):
                        sync.wait_ge(in2_summed, 8 * i)
                        sync.dma_start(w_2[odd], w_in_2[:, :, ds(i * 384 + c0, 384)]).then_inc(w_2_loaded[odd], 16)

            @block.tensor
            def _(pe):
                with pe.Fori(0, 3) as i:
                    for odd in range(2):
                        pe.wait_ge(w_2_loaded[odd], 16 * i + 16)
                        for tb in range(TB):
                            pe.wait_ge(in2_by_act if tb < 2 else in2_by_dve, 4 * i + 2 * odd + tb % 2 + 1)
                            for k in range(KD):
                                ins = nc.tensor.matmul(psum[4 * odd + tb][:, 0:384], hT[:, k, tb * P:(tb + 1) * P],
                                                       w_2[odd][:, k, :], start=(k == 0), stop=(k == KD - 1))
                            ins.then_inc(in2_summed, 1)

            @block.scalar
            def _(act):
                act.sem_inc(in2_by_act, 4)
                with act.Fori(0, 3) as i:
                    for odd in range(2):
                        for tb in (0, 1):
                            act.wait_ge(in2_summed, 8 * i + TB * odd + tb + 1)
                            nc.scalar.copy(proj2[:, tb, ds(i * SM_W + odd * FOX_W, 384)],
                                           psum[4 * odd + tb][:, 0:384]).then_inc(in2_by_act, 1)

            @block.vector
            def _(dve):
                dve.sem_inc(in2_by_dve, 4)
                with dve.Fori(0, 3) as i:
                    for odd in range(2):
                        for tb in (2, 3):
                            dve.wait_ge(in2_summed, 8 * i + TB * odd + tb + 1)
                            nc.vector.tensor_copy(proj2[:, tb, ds(i * SM_W + odd * FOX_W, 384)],
                                                  psum[4 * odd + tb][:, 0:384]).then_inc(in2_by_dve, 1)

        ml_summed, ml_copied, squared2, rms2_mean = sem("ml_summed"), sem("ml_copied"), sem("squared2"), sem("rms2_mean")
        gate_added, log_ready, conv_summed = sem("gate_added"), sem("log_ready"), sem("conv_summed")
        cum_ready, mi_moved, row_moved = sem("cum_ready"), sem("mi_moved"), sem("row_moved")
        conv_ready, heads_moved, cols_turned = sem("conv_ready"), sem("heads_moved"), sem("cols_turned")
        m_ready, floor_ready, negated, pad_zeroed, w_mvo_loaded = (sem("m_ready"), sem("floor_ready"), sem("negated"),
                                                                   sem("pad_zeroed"), sem("w_mvo_loaded"))
        NG = MI + ML_H
        squares2 = view(SCRATCH2, TB * SM_H, HD)
        with nc.Block() as block:
            @block.tensor
            def _(pe):
                pe.wait_ge(w_ml_loaded, 64)
                for k in range(KD):
                    ins = nc.tensor.matmul(psum[4][0:NG, :], w_gates[:, k, 0:NG], hT[:, k, :], start=(k == 0),
                                           stop=(k == KD - 1))
                ins.then_inc(ml_summed, 1)
                for j in range(4):
                    for k in range(KD):
                        ins = nc.tensor.matmul(psum[j][:, :], w_mqk[:, k, j * P:(j + 1) * P], hT[:, k, :],
                                               start=(k == 0), stop=(k == KD - 1))
                    ins.then_inc(ml_summed, 1)

            @block.gpsimd
            def _(pool):
                nc.gpsimd.memset(conv_in[:, :, 0:CONV - 1], 0.0).then_inc(pad_zeroed, 1)

            @block.scalar
            def _(act):
                act.wait_ge(gate_added, 1)
                nc.scalar.activation(gate_t[0:NG, :], gate_pre[0:NG, :], ACT.Abs)
                act.drain()
                nc.scalar.activation(gate_t[0:NG, :], gate_t[0:NG, :], ACT.Exp, scale=-1.0)
                act.drain()
                nc.scalar.activation(gate_t[0:NG, :], gate_t[0:NG, :], ACT.Ln, bias=1.0).then_inc(log_ready, 1)
                for j in range(4):
                    act.wait_ge(ml_summed, 2 + j)
                    nc.scalar.copy(conv_in[:, j, CONV - 1:], psum[j][:, :]).then_inc(ml_copied, 1)
                for i in range(2):
                    if i:
                        act.wait_ge(rms2_mean, 1)
                    nc.scalar.activation(squares2.rearrange("p (b h) d -> p b (h d)", h=SM_H),
                                         proj2[:, :, i * SM_W:(i + 1) * SM_W], ACT.Square).then_inc(squared2, 1)
                flat = rms_2.rearrange("p i b h -> p (i b h)")
                act.wait_ge(rms2_mean, 2)
                nc.scalar.activation(flat, ss_2.rearrange("p i b h -> p (i b h)"), ACT.Ln)
                act.drain()
                nc.scalar.activation(flat, flat, ACT.Exp, scale=-0.5)
                act.wait_ge(m_ready, 1)
                nc.scalar.activation(ml_floor[MF:MF + ML_H, :], ml_floor[MF:MF + ML_H, :], ACT.Exp,
                                     scale=-1.0).then_inc(floor_ready, 1)
                for j in range(4):
                    act.wait_ge(conv_summed, j + 1)
                    nc.scalar.activation(conv_out[:, j, :], conv_out[:, j, :], ACT.Silu).then_inc(conv_ready, 1)

            @block.vector
            def _(dve):
                dve.wait_ge(bias_loaded, 48)
                dve.wait_ge(ml_summed, 1)
                nc.vector.tensor_scalar(gate_pre[0:NG, :], psum[4][0:NG, :], gate_bias[0:NG, :], None,
                                        ALU.add).then_inc(gate_added, 1)
                dve.wait_ge(log_ready, 1)
                n = MF + ML_H
                nc.vector.scalar_tensor_tensor(out=log_f[0:n, :], in0=gate_pre[0:n, :], scalar=0.0, in1=gate_t[0:n, :],
                                               op0=ALU.min, op1=ALU.subtract)
                dve.drain()
                nc.vector.tensor_tensor_scan(cum[0:n, :], ones[0:n, :], log_f[0:n, :], 0.0, ALU.mult, ALU.add)
                dve.drain()
                nc.vector.tensor_scalar(log_f[0:FOX_H, :], cum[0:FOX_H, :], -1.0, None, ALU.mult).then_inc(negated, 1)
                r = slice(MF, MF + ML_H)
                dve.wait_ge(mi_moved, 16)
                nc.vector.tensor_tensor(ml_a[r, :], mi_rows[r, :], cum[r, :], ALU.subtract)
                dve.drain()
                nc.vector.tensor_tensor_scan(ml_m[r, :], ml_a[r, :], ml_a[r, :], 0.0, ALU.max, ALU.max).then_inc(cum_ready, 1)
                dve.drain()
                nc.vector.tensor_tensor(ml_floor[r, :], ml_m[r, :], cum[r, :], ALU.add).then_inc(m_ready, 1)
                nc.vector.tensor_scalar(ml_m[r, :], ml_m[r, :], -1.0, None, ALU.mult).then_inc(m_ready, 1)
                for i in range(2):
                    dve.wait_ge(squared2, i + 1)
                    s = ss_2[:, i, :, :].rearrange("p b h -> p (b h)")
                    nc.vector.tensor_reduce(s, squares2, AX, ALU.add)
                    dve.drain()
                    nc.vector.tensor_scalar(s, s, 1.0 / HD, EPS, ALU.mult, ALU.add).then_inc(rms2_mean, 1)
                dve.wait_ge(pad_zeroed, 1)
                for j in range(4):
                    dve.wait_ge(ml_copied, j + 1)
                    nc.vector.tensor_scalar(conv_out[:, j, :], conv_in[:, j, 0:T], col("ml_conv_w_2", j),
                                            col("ml_conv_b_2", j), ALU.mult, ALU.add)
                    for c in range(1, CONV):
                        dve.drain()
                        ins = nc.vector.scalar_tensor_tensor(out=conv_out[:, j, :], in0=conv_in[:, j, c:c + T],
                                                             scalar=col("ml_conv_w_2", 4 * c + j), in1=conv_out[:, j, :],
                                                             op0=ALU.mult, op1=ALU.add)
                    ins.then_inc(conv_summed, 1)

            @block.sync
            def _(sync):
                sync.wait_ge(gate_added, 1)
                sync.dma_start(mi_rows[MF:MF + ML_H, :], gate_pre[MI:MI + ML_H, :]).then_inc(mi_moved, 16)
                sync.wait_ge(ml_summed, 5)
                sync.wait_ge(negated, 1)
                for h in range(FOX_H):
                    sync.dma_start(kbias[HD:HD + 1, h, :], log_f[h:h + 1, :]).then_inc(row_moved, 16)
                sync.wait_ge(cum_ready, 1)
                for h in range(ML_H):
                    sync.dma_start(a_rows[0:1, h, :], ml_a[MF + h:MF + h + 1, :]).then_inc(row_moved, 16)
                for j in range(4):
                    sync.wait_ge(conv_ready, j + 1)
                    o = ml_q if j < 2 else ml_k
                    for odd in range(2):
                        sync.dma_start(o[0:HD, 2 * (j % 2) + odd, :],
                                       conv_out[odd * HD:(odd + 1) * HD, j, :]).then_inc(heads_moved, 16)
                sync.wait_ge(row_moved, 16 * (FOX_H + ML_H))
                sync.wait_ge(heads_moved, 16 * 8)

        mo_tiles = [(w_mvo[:, :, i * ML_W:(i + 1) * ML_W], ML_W, lambda tb, i=i: mvo[:, tb, i * ML_W:(i + 1) * ML_W])
                    for i in range(2)]
        mo_pe, mo_act, mo_dve = project_rows("mo_", lambda i: hT[:, :, :], lambda i: KD, mo_tiles,
                                             ready=lambda pe, i: pe.wait_ge(*[(w_mvo_loaded, 32), (cols_copied, 1)][i]))
        cols_copied = sem("cols_copied")
        with nc.Block() as block:
            @block.sync
            def _(sync):
                for i, c0 in enumerate((MV0, MO0)):
                    sync.dma_start(w_mvo[:, :, i * ML_W:(i + 1) * ML_W],
                                   w_in_2[:, :, c0:c0 + ML_W]).then_inc(w_mvo_loaded, 16)

            @block.tensor
            def _(pe):
                r = slice(MF, MF + ML_H)
                for i, rows_of in enumerate((ml_m, ml_floor)):
                    for tb in range(TB):
                        ins = nc.tensor.transpose(psum[7][:, (i * TB + tb) * ML_H:(i * TB + tb + 1) * ML_H],
                                                  rows_of[r, tb * P:(tb + 1) * P], ident[r, r])
                ins.then_inc(cols_turned, 1)
                mo_pe(pe)

            @block.gpsimd
            def _(pool):
                r = slice(HD, HD + 1)
                nc.gpsimd.iota(gate_t[r, :], [[1, T]], base=0, channel_multiplier=0,
                               allow_small_or_imprecise_dtypes=True)
                pool.drain()
                for h in range(MOBA_H):
                    nc.gpsimd.tensor_scalar(kbias[r, FOX_H + h, :], gate_t[r, :], 2.0 ** (-8.0 * (h + 1) / MOBA_H), None,
                                            ALU.mult)

            @block.scalar
            def _(act):
                mo_act(act)

            @block.vector
            def _(dve):
                dve.wait_ge(cols_turned, 1)
                nc.vector.tensor_copy(ml_cols.rearrange("p i b h -> p (i b h)"), psum[7][:, 0:2 * TB * ML_H]).then_inc(cols_copied, 1)
                mo_dve(dve)

        attention("ml_", "mlstm", ML_H, HD, SCRATCH2, None, None, None,
                  v=lambda j, h: mvo[:, j, ds(h * HD, HD)],
                  dst=lambda tb, h: rows[:, tb, ds(h * HD + SM_W, HD)], mask=causal_mask,
                  qk_T=lambda h: (ml_q[0:HD, ds(h, 1), :].squeeze(1), ml_k[0:HD, ds(h, 1), :].squeeze(1)),
                  decay=(lambda h, n: a_rows[0:1, ds(h, 1), 0:n].squeeze(1),
                         lambda tb, h: ml_cols[:, 0, tb, ds(h, 1)], lambda tb, h: ml_cols[:, 1, tb, ds(h, 1)]))

        w_out = view(11264, KD, D)
        w_out_loaded = sem("w_out_loaded")

        def stage_2(h, q_st, k_st, staged):
            for i, st in enumerate((q_st, k_st)):
                nc.gpsimd.tensor_tensor(st[:, :, 0:HD], proj2[:, :, ds(h * HD + i * SM_W, HD)],
                                        rms_2[:, i, :, ds(h, 1)].to_broadcast([P, TB, HD]), ALU.mult).then_inc(staged, 1)

        attention("sm_", "softmax", SM_H, HD, SCRATCH2, stage_2, lambda h: gains[0:HD, ds(h + GQ, 1)],
                  lambda h: gains[0:HD, ds(h + GK, 1)],
                  v=lambda j, h: proj2[:, j, ds(h * HD + 2 * SM_W, HD)],
                  dst=lambda tb, h: rows[:, tb, ds(h * HD, HD)], mask=causal_mask,
                  kbias=lambda h: kbias[HD:HD + 1, ds(h, 1), :].squeeze(1),
                  loads=lambda sync: sync.dma_start(w_out, a["w_out_2"][0].rearrange("(k p) n -> p k n", p=P))
                  .then_inc(w_out_loaded, 16))

        ml_gain, gate_row = view(SCRATCH2, ML_W), ffn_gain
        ml_sq, ml_ss, ml_sig = view(SCRATCH2 + 256, TB * ML_H, HD), view(SCRATCH2 + 1280, TB * ML_H), view(SCRATCH2 + 1400, TB, ML_W)
        ml_gain_loaded, ml_squared, ml_mean, ml_rms = sem("ml_gain_loaded"), sem("ml_squared"), sem("ml_mean"), sem("ml_rms")
        ml_opened, y_turned, y_copied = sem("ml_opened"), sem("y_turned"), sem("y_copied")
        g_summed, g_stored = sem("g_summed"), sem("g_stored")

        def gate_rows(pe, g0):
            for k in range(KD):
                ins = nc.tensor.matmul(psum[6 + k // 4][:, k % 4 * P:k % 4 * P + P],
                                       mod[:, g0 + k:g0 + k + 1].to_broadcast([P, P]), ident[:, :], start=True, stop=True)
            ins.then_inc(g_summed, 1)

        with nc.Block() as block:
            @block.sync
            def _(sync):
                sync.dma_start(ml_gain, a["ml_h_g_2"].to_broadcast([P, ML_W])).then_inc(ml_gain_loaded, 16)

            @block.scalar
            def _(act):
                heads = rows[:, :, SM_W:].rearrange("p b (h d) -> p b h d", d=HD)
                nc.scalar.activation(ml_sq.rearrange("p (b h) d -> p b (h d)", h=ML_H), rows[:, :, SM_W:],
                                     ACT.Square).then_inc(ml_squared, 1)
                nc.scalar.activation(ml_sig, mvo[:, :, ML_W:], ACT.Sigmoid)
                act.wait_ge(ml_mean, 1)
                nc.scalar.activation(ml_ss, ml_ss, ACT.Ln)
                act.drain()
                nc.scalar.activation(ml_ss, ml_ss, ACT.Exp, scale=-0.5).then_inc(ml_rms, 1)
                for k in range(KD):
                    act.wait_ge(y_turned, k + 1)
                    nc.scalar.copy(hT[:, k, :], psum[k % 4][:, :]).then_inc(y_copied, 1)

            @block.vector
            def _(dve):
                dve.wait_ge(g_summed, 1)
                for i in range(2):
                    nc.vector.tensor_copy(gate_row[:, i * 512:(i + 1) * 512], psum[6 + i][:, :])
                dve.wait_ge(ml_squared, 1)
                nc.vector.tensor_reduce(ml_ss, ml_sq, AX, ALU.add)
                dve.drain()
                nc.vector.tensor_scalar(ml_ss, ml_ss, 1.0 / HD, EPS, ALU.mult, ALU.add).then_inc(ml_mean, 1)
                dve.wait_ge(ml_rms, 1)
                y = rows[:, :, SM_W:]
                for tb in range(TB):
                    o = y[:, tb, :].rearrange("p (h d) -> p h d", d=HD)
                    r = ml_ss[:, tb * ML_H:(tb + 1) * ML_H].unsqueeze(2).to_broadcast([P, ML_H, HD])
                    nc.vector.tensor_tensor(o, o, r, ALU.mult)
                dve.drain()
                dve.wait_ge(ml_gain_loaded, 16)
                nc.vector.tensor_tensor(y, y, ml_gain.unsqueeze(1).to_broadcast([P, TB, ML_W]), ALU.mult)
                dve.drain()
                nc.vector.tensor_tensor(y, y, ml_sig, ALU.mult).then_inc(ml_opened, 1)

            @block.tensor
            def _(pe):
                gate_rows(pe, G1)
                for k in range(KD):
                    if k >= 4:
                        pe.wait_ge(y_copied, k - 3)
                    if k == SM_W // P:
                        pe.wait_ge(ml_opened, 1)
                    for tb in range(TB):
                        ins = nc.tensor.transpose(psum[k % 4][:, tb * P:(tb + 1) * P], rows[:, tb, k * P:(k + 1) * P],
                                                  ident[:, :])
                    ins.then_inc(y_turned, 1)

        KFOX, KML = FOX_W // P, ML_W // P
        order = [*range(KFOX), *range(KFOX + KML, KD), *range(KFOX, KFOX + KML)]
        out_projection("o2_", w_out, order, w_out_loaded, gate_row=gate_row)

        act_T = view(0, KF, T)
        w_gu = [view(19468 + i * KD * 2 * P, KD, 2, P) for i in range(2)]
        DOWN = 256
        w_dn = [view(25612, KF, DOWN), view(25612 + KF * DOWN, KF, DOWN)]
        gu_loaded, dn_loaded = [sem("gu_loaded0"), sem("gu_loaded1")], [sem("dn_loaded0"), sem("dn_loaded1")]
        gu_summed, silu_ready, act_ready = sem("gu_summed"), sem("silu_ready"), sem("act_ready")
        dn_summed, dn_added, stored_out = sem("dn_summed"), sem("dn_added"), sem("stored_out")
        silu_g = view(25612 - 1024, 2, T)
        gated_y = view(11264, 2, DOWN)
        w_gate_up = a["w_gate_up_2"][0].rearrange("(k p) n -> p k n", p=P)
        w_down = a["w_down_2"][0].rearrange("(k p) n -> p k n", p=P)

        def load_gu(sync, i, odd):
            for g in range(2):
                sync.dma_start(w_gu[odd][:, :, g, :], w_gate_up[:, :, ds((2 * i + odd) * P + g * D_FF, P)])\
                    .then_inc(gu_loaded[odd], 16)

        def load_first_ffn(sync):
            for odd in range(2):
                load_gu(sync, 0, odd)
            for i in range(2):
                sync.dma_start(w_dn[i], w_down[:, :, i * DOWN:(i + 1) * DOWN]).then_inc(dn_loaded[i], 16)

        norm_T("n6_", x, [(0, D)], rows, hT, gain_cols=lambda k: mod_gain[:, KD + k:KD + k + 1],
               shift_cols=lambda k: mod[:, SH2 + k:SH2 + k + 1], loads=load_first_ffn)

        with nc.Block() as block:
            @block.sync
            def _(sync):
                with sync.Fori(1, KF // 2) as i:
                    for odd in range(2):
                        sync.wait_ge(gu_summed, 4 * i - 2 + 2 * odd)
                        load_gu(sync, i, odd)

            @block.tensor
            def _(pe):
                gate_rows(pe, G2)
                with pe.Fori(0, KF // 2) as i:
                    for odd in range(2):
                        pe.wait_ge(gu_loaded[odd], 32 * i + 32)
                        pe.wait_ge(act_ready, 2 * i + odd + 1)
                        for g in range(2):
                            for k in range(KD):
                                ins = nc.tensor.matmul(psum[2 * odd + g][:, :], w_gu[odd][:, k, g, :], hT[:, k, :],
                                                       start=(k == 0), stop=(k == KD - 1))
                            ins.then_inc(gu_summed, 1)

            @block.scalar
            def _(act):
                with act.Fori(0, KF // 2) as i:
                    for odd in range(2):
                        act.wait_ge(gu_summed, 4 * i + 2 * odd + 1)
                        act.wait_ge(act_ready, 2 * i + odd + 1)
                        nc.scalar.activation(silu_g[:, odd, :], psum[2 * odd][:, :], ACT.Silu).then_inc(silu_ready, 1)

            @block.vector
            def _(dve):
                dve.sem_inc(act_ready, 2)
                dve.wait_ge(g_summed, 2)
                for i in range(2):
                    nc.vector.tensor_copy(gate_row[:, i * 512:(i + 1) * 512], psum[6 + i][:, :])
                with dve.Fori(0, KF // 2) as i:
                    for odd in range(2):
                        dve.wait_ge(silu_ready, 2 * i + odd + 1)
                        dve.wait_ge(gu_summed, 4 * i + 2 * odd + 2)
                        nc.vector.tensor_tensor(act_T[:, ds(2 * i + odd, 1), :].squeeze(1), silu_g[:, odd, :],
                                                psum[2 * odd + 1][:, :], ALU.mult).then_inc(act_ready, 1)

        N_DOWN = D // DOWN
        with nc.Block() as block:
            @block.sync
            def _(sync):
                for i in range(2, N_DOWN):
                    sync.wait_ge(dn_summed, TB * (i - 1))
                    sync.dma_start(w_dn[i % 2], w_down[:, :, i * DOWN:(i + 1) * DOWN]).then_inc(dn_loaded[i % 2], 16)
                for i in range(N_DOWN):
                    c = slice(i * DOWN, (i + 1) * DOWN)
                    sync.wait_ge(dn_added, TB * (i + 1))
                    sync.dma_start(out[0].rearrange("(b p) n -> p b n", p=P)[:, :, c], x[:, :, c]).then_inc(stored_out, 16)
                sync.wait_ge(stored_out, 16 * N_DOWN)

            @block.tensor
            def _(pe):
                for i in range(N_DOWN):
                    pe.wait_ge(dn_loaded[i % 2], 16 * (i // 2) + 16)
                    for tb in range(TB):
                        if i >= 2:
                            pe.wait_ge(dn_added, TB * (i - 2) + tb + 1)
                        for f in range(KF):
                            ins = nc.tensor.matmul(psum[TB * (i % 2) + tb][:, 0:DOWN], act_T[:, f, tb * P:(tb + 1) * P],
                                                   w_dn[i % 2][:, f, :], start=(f == 0), stop=(f == KF - 1))
                        ins.then_inc(dn_summed, 1)

            @block.vector
            def _(dve):
                for i in range(N_DOWN):
                    c = slice(i * DOWN, (i + 1) * DOWN)
                    for tb in range(TB):
                        dve.wait_ge(dn_summed, TB * i + tb + 1)
                        nc.vector.tensor_tensor(gated_y[:, tb % 2, :], psum[TB * (i % 2) + tb][:, 0:DOWN],
                                                gate_row[:, c], ALU.mult)
                        dve.drain()
                        nc.vector.tensor_tensor(x[:, tb, c], x[:, tb, c], gated_y[:, tb % 2, :],
                                                ALU.add).then_inc(dn_added, 1)


_INS = ["x", "positions", "attn_norm", "w_in", "cq_norm", "w_uq", "ckv_norm", "w_ukv", "q_norm", "k_norm",
        "sb_out_norm", "mla_out_norm", "w_o", "ffn_norm", "peer_w_q", "peer_sub_keys", "peer_u", "peer_v", "c_2",
        "w_ada_2", "b_ada_2", "norm1_g_2", "norm2_g_2", "w_in_2", "fox_f_bias_2", "fox_q_g_2", "fox_k_g_2",
        "ml_conv_w_2", "ml_conv_b_2", "ml_i_bias_2", "ml_f_bias_2", "ml_h_g_2", "moba_q_g_2", "moba_k_g_2",
        "w_out_2", "w_gate_up_2", "w_down_2"]


def kernel(**inputs):
    import numpy as _np
    import concourse.bacc as _bacc
    from concourse import mybir as _mybir
    from concourse.bass_utils import run_bass_kernel_spmd as _run

    nc = _bacc.Bacc("TRN2", target_bir_lowering=False, num_devices=1)
    arrays, args = {}, {}
    for name in _INS:
        v = _np.ascontiguousarray(inputs[name])
        arrays[f"in_{name}"] = v
        args[name] = nc.dram_tensor(f"in_{name}", v.shape, _mybir.dt.from_np(v.dtype), kind="ExternalInput").ap()
    out = nc.dram_tensor("out", (1, T, D), F32, kind="ExternalOutput").ap()
    program(nc, args, out)
    r = _run(nc, [arrays], core_ids=[0])
    return r.results[0]["out"]
```

```python
from contextlib import ExitStack
import math

import numpy as np
import concourse.bass as bass
import concourse.mybir as mybir

F32 = mybir.dt.float32
F32R = mybir.dt.float32r
BF16 = mybir.dt.bfloat16
I32 = mybir.dt.int32
U32 = mybir.dt.uint32
ALU = mybir.AluOpType
ACT = mybir.ActivationFunctionType
AX = mybir.AxisListType.X
ds = bass.ds

P = 128
T = 512
TB = T // P
D = 1024
KD = D // P
EPS = 1e-6
MASKED = -1e30

SB_H, HD = 8, 64
SB_W = SB_H * HD
MLA_H, NOPE, ROPE, MLA_QK, MLA_V = 8, 64, 32, 96, 64
Q_RANK, KV_RANK = 384, 256
IN1 = 3 * SB_W + Q_RANK + KV_RANK + ROPE
CQ0, CKV0, KPE0 = 3 * SB_W, 3 * SB_W + Q_RANK, 3 * SB_W + Q_RANK + KV_RANK
IN1_TILE, IN1_TILES = IN1 // 6, 6
CHUNK = 64

PH, PK, PN, PD = 8, 16, 128, 128

ML_H, FOX_H, MOBA_H = 4, 6, 6
SM_H = FOX_H + MOBA_H
FOX_W, ML_W, MOBA_W = FOX_H * HD, ML_H * HD, MOBA_H * HD
SM_W = FOX_W + MOBA_W
FF0 = 3 * FOX_W
MQK0 = FF0 + FOX_H
MV0 = MQK0 + 2 * ML_W
MI0 = MV0 + ML_W
MF0 = MI0 + ML_H
MO0 = MF0 + ML_H
BQ0 = MO0 + ML_W
CONV = 4
D_FF = ((8 * D // 3 + 255) // 256) * 256
KF = D_FF // P


def program(nc, a, out):
    with ExitStack() as ctx:
        def sb(name, shape, dt=F32):
            return ctx.enter_context(nc.sbuf_tensor(name, shape, dt))

        def sb_twin(name, shape):
            offset = nc.sbuf_base
            return sb(name, shape), nc.alloc_sbuf_tensor_at(name + "_r", shape, F32R, offset=offset)

        def sem(name):
            return ctx.enter_context(nc.semaphore(name))

        psum = [ctx.enter_context(nc.psum_tensor(f"bank{i}", [P, 512], F32)) for i in range(8)]

        x = sb("x", [P, TB, D])
        rows, rows_r = sb_twin("rows", [P, TB, D])
        hT, hT_r = sb_twin("hT", [P, KD, T])
        ident = sb("ident", [P, P])
        ident_bf = sb("ident_bf", [P, P], BF16)
        strict_mask = sb("strict_mask", [P, P], BF16)
        causal_mask = sb("causal_mask", [P, P], BF16)
        chunk_mask = sb("chunk_mask", [P, P], BF16)
        ones = sb("ones", [P, T])
        vec_rows = sb("vec_rows", [P, P])
        vec = sb("vec", [P, P])
        small_rows = sb("small_rows", [8, P])
        small = sb("small", [P, 8])
        cos = sb("cos", [P, TB, ROPE // 2])
        sin = sb("sin", [P, TB, ROPE // 2])
        GQ, GK = 2, 2 + SM_H
        gains = sb("gains", [P, GK + SM_H])
        silu_c = sb("silu_c", [P, KD])
        mod = sb("mod", [P, 6 * KD])
        SH1, SC1, G1, SH2, SC2, G2 = (i * KD for i in range(6))
        stat = sb("stat", [P, 2, TB])
        rstd = sb("rstd", [P, 2, TB])
        ARENA = 38000
        arena_at = nc.sbuf_base
        arena = sb("arena", [P, ARENA])

        def view(start, *dims, of=None):
            n = math.prod(dims)
            assert start + n <= ARENA, (start, dims)
            ap = arena[:, start:start + n] if of is None else of[:, :]
            if len(dims) == 2:
                ap = ap.rearrange("p (a b) -> p a b", b=dims[1])
            if len(dims) == 3:
                ap = ap.rearrange("p (a b c) -> p a b c", b=dims[1], c=dims[2])
            return ap

        def view_r(start, *dims):
            n = math.prod(dims)
            return view(start, *dims, of=nc.alloc_sbuf_tensor_at(f"parts_{start}_{n}", [P, n], F32R,
                                                                 offset=arena_at + 4 * start))

        at, place = 0, {}
        pieces = [("attn_norm", D), ("cq_norm", Q_RANK), ("ckv_norm", KV_RANK), ("sb_out_norm", SB_W),
                  ("mla_out_norm", MLA_H * MLA_V), ("norm1_g_2", D), ("norm2_g_2", D), ("c_2", D),
                  ("b_ada_2", 6 * D), ("ml_conv_b_2", 2 * ML_W), ("ml_conv_w_2", CONV * 2 * ML_W)]
        for name, n in pieces:
            place[name] = (at, n // P)
            at += n // P
        N_VEC = at

        def col(name, k):
            return vec[:, place[name][0] + k:place[name][0] + k + 1]

        def split(dve, value, high, low):
            nc.vector.tensor_copy(high, value)
            dve.drain()
            return nc.vector.tensor_tensor(low, value, high.bitcast(F32), ALU.subtract)

        def product(out, lhsT, rhs, first, last):
            nc.tensor.matmul(out, lhsT[0], rhs[0], start=first, stop=False)
            nc.tensor.matmul(out, lhsT[0], rhs[1], start=False, stop=False)
            return nc.tensor.matmul(out, lhsT[1], rhs[0], start=False, stop=last)

        def h_rows(k, tb):
            return rows_r[:, tb, k * P:(k + 1) * P], hT_r[:, k, tb * P:(tb + 1) * P]

        def h_all(k):
            return rows_r[:, :, k * P:(k + 1) * P], hT_r[:, k, :].rearrange("p (b t) -> p b t", t=P)

        def split_h(dve, k):
            return split(dve, hT[:, k, :].rearrange("p (b t) -> p b t", t=P), *h_all(k))

        def counts_from_zero(sems):
            with nc.Block() as block:
                @block.gpsimd
                def _(pool):
                    for s in sems:
                        pool.sem_clear(s)

        norm_sems = [sem("norm_" + n) for n in ("squared", "mean_ready", "rstd_ready", "normed", "turned", "evacuated")]

        def norm_T(tag, src, segments, dst, dstT, gain_cols=None, shift_cols=None, gain_row=None,
                   ready=None, loads=None, scratch=None, pool_part=None, parts=False,
                   pe_first=None, dve_first=None):
            squared, mean_ready, rstd_ready, normed, turned, evacuated = norm_sems
            counts_from_zero(norm_sems)
            kt = sum(w for _, w in segments) // P
            ns = len(segments)
            with nc.Block() as block:
                if loads:
                    @block.sync
                    def _(sync):
                        loads(sync)

                if pool_part:
                    @block.gpsimd
                    def _(pool):
                        pool_part(pool)

                @block.scalar
                def _(act):
                    act.preload_act_table_set("natural_log_exp_and_others")
                    for tb in range(TB // 2):
                        if ready:
                            ready(act, tb)
                        for s, (c0, w) in enumerate(segments):
                            nc.scalar.activation((dst if scratch is None else scratch)[:, tb, c0:c0 + w],
                                                 src[:, tb, c0:c0 + w], ACT.Square,
                                                 accum_out=stat[:, s, tb:tb + 1]).then_inc(squared, 1)
                    act.wait_ge(mean_ready, ns)
                    nc.scalar.activation(stat[:, 0:ns, :], stat[:, 0:ns, :], ACT.Ln)
                    act.drain()
                    nc.scalar.activation(rstd[:, 0:ns, :], stat[:, 0:ns, :], ACT.Exp,
                                         scale=-0.5).then_inc(rstd_ready, 1)
                    for k in range(kt):
                        act.wait_ge(turned, k + 1)
                        o, i = dstT[:, k, :], psum[k % 4][:, :]
                        if shift_cols is not None:
                            ins = nc.scalar.activation(o, i, ACT.Identity, scale=gain_cols(k), bias=shift_cols(k))
                        elif gain_cols is not None:
                            ins = nc.scalar.activation(o, i, ACT.Copy, scale=gain_cols(k))
                        else:
                            ins = nc.scalar.copy(o, i)
                        ins.then_inc(evacuated, 1)

                @block.vector
                def _(dve):
                    for tb in range(TB // 2, TB):
                        if ready:
                            ready(dve, tb)
                        for s, (c0, w) in enumerate(segments):
                            i = src[:, tb, c0:c0 + w]
                            nc.vector.scalar_tensor_tensor(out=(dst if scratch is None else scratch)[:, tb, c0:c0 + w],
                                                           in0=i, scalar=1.0, in1=i, op0=ALU.mult, op1=ALU.mult,
                                                           accum_out=stat[:, s, tb:tb + 1])
                    if dve_first:
                        dve_first(dve)
                    dve.drain()
                    dve.wait_ge(squared, ns * TB // 2)
                    for s, (c0, w) in enumerate(segments):
                        nc.vector.tensor_scalar(stat[:, s, :], stat[:, s, :], 1.0 / w, EPS, ALU.mult,
                                                ALU.add).then_inc(mean_ready, 1)
                    dve.wait_ge(rstd_ready, 1)
                    for tb in range(TB):
                        for s, (c0, w) in enumerate(segments):
                            o, i, r = dst[:, tb, c0:c0 + w], src[:, tb, c0:c0 + w], rstd[:, s, tb:tb + 1]
                            if gain_row is not None:
                                ins = nc.vector.scalar_tensor_tensor(out=o, in0=i, scalar=r, in1=gain_row[:, c0:c0 + w],
                                                                     op0=ALU.mult, op1=ALU.mult)
                            else:
                                ins = nc.vector.tensor_scalar(o, i, r, None, ALU.mult)
                            ins.then_inc(normed, 1)
                    if parts:
                        for k in range(kt):
                            dve.wait_ge(evacuated, k + 1)
                            split_h(dve, k)

                @block.tensor
                def _(pe):
                    if pe_first:
                        pe_first(pe)
                    cols = [c0 + j for c0, w in segments for j in range(0, w, P)]
                    pe.wait_ge(normed, ns * TB)
                    for k, c in enumerate(cols):
                        if k >= 4:
                            pe.wait_ge(evacuated, k - 3)
                        for tb in range(TB):
                            ins = nc.tensor.transpose(psum[k % 4][:, tb * P:(tb + 1) * P], dst[:, tb, c:c + P],
                                                      ident[:, :])
                        ins.then_inc(turned, 1)

        attention_sems = [sem("att_" + n) for n in ("staged", "q_turned", "k_turned", "q_ready", "k_ready", "scores", "half",
                                           "ready_for_exp", "probs_ready", "probs_turned", "turned_out", "summed", "stored")]

        def attention(tag, kind, heads, K, scratch, stage, q_gain, k_gain, v, dst, mask, kbias=None,
                      decay=None, qk_T=None, loads=None):
            s0 = scratch
            q_st, k_st = view(s0, TB, 96), view(s0 + 384, TB, 96)
            qT, kT = view(s0 + 768, 512), view(s0 + 1280, 512)
            probs = view(s0 + 1792, 2, 512)
            probsT = view(s0 + 2816, 2, 512)
            work = view(s0 + 3840, 4, 512)
            peak, total = view(s0 + 5888, TB), view(s0 + 5896, TB)
            recip = view(s0 + 5904, TB)
            q_ps, k_ps = psum[0], psum[1]
            s_ps, t_ps, o_ps = [psum[2], psum[3]], [psum[4], psum[5]], [psum[6], psum[7]]
            decay_ps = [psum[0], psum[1]]
            (staged, q_turned, k_turned, q_ready, k_ready, scores, half, ready_for_exp, probs_ready, turned, turned_out,
             summed, stored) = attention_sems
            counts_from_zero(attention_sems)

            deep = kind == "stick"
            AHEAD = TB if deep else 2
            if deep:
                s_ps, t_ps, o_ps = psum[2:6], [psum[6]] * 2, [psum[7]] * 2
                work = view(s0 + 5920, 2 * TB, 512)

            def width(tb):
                return (tb + 1) * P

            with nc.Block() as block:
                if loads:
                    @block.sync
                    def _(sync):
                        loads(sync)

                @block.gpsimd
                def _(pool):
                    nc.gpsimd.memset(qT[K:, :], 0.0)
                    pool.drain()
                    nc.gpsimd.memset(kT[K:, :], 0.0)
                    pool.drain()
                    if kbias:
                        nc.gpsimd.memset(qT[K:K + 1, :], 1.0)
                    pool.drain().then_inc(staged, 1)
                    if stage:
                        stage(0, q_st, k_st, staged)
                        with pool.Fori(1, heads) as h:
                            pool.wait_ge(q_turned, h)
                            pool.wait_ge(k_turned, h)
                            stage(h, q_st, k_st, staged)

                @block.tensor
                def _(pe):
                    pe.wait_ge(staged, 1)

                    def turn(h):
                        pe.wait_ge(staged, 2 * h + 3)
                        pe.wait_ge(q_ready, h)
                        pe.wait_ge(k_ready, h)
                        pe.nop(nofuse=True)
                        for tb in range(TB):
                            ins = nc.tensor.transpose(q_ps[0:K, tb * P:(tb + 1) * P], q_st[:, tb, 0:K], ident[:, :])
                        ins.then_inc(q_turned, 1)
                        for tb in range(TB):
                            ins = nc.tensor.transpose(k_ps[0:K, tb * P:(tb + 1) * P], k_st[:, tb, 0:K], ident[:, :])
                        ins.then_inc(k_turned, 1)

                    def score(h, tb):
                        n = width(tb)
                        pe.wait_ge(probs_ready, TB * h + tb + 1)
                        nc.tensor.matmul(s_ps[tb % AHEAD][:, 0:n], qT[:, tb * P:(tb + 1) * P], kT[:, 0:n],
                                         start=True, stop=(kind == "mlstm"))
                        if kind == "mlstm":
                            nc.tensor.matmul(decay_ps[tb % 2][:, 0:n], ones[:, 0:P], decay[0](h, n),
                                             start=True, stop=False)
                        o = decay_ps if kind == "mlstm" else s_ps
                        nc.tensor.matmul(o[tb % AHEAD][:, tb * P:n], ident_bf[:, :], mask[:, :], start=False,
                                         stop=True).then_inc(scores, 1)

                    def turn_probs(h, tb):
                        pe.wait_ge(probs_ready, TB * h + tb + 1 + AHEAD)
                        pe.wait_ge(turned_out, TB * h + tb + 1 + deep)
                        for j in range(tb + 1):
                            ins = nc.tensor.transpose(t_ps[tb % 2][:, j * P:(j + 1) * P],
                                                      probs[:, tb % 2, j * P:(j + 1) * P], ident[:, :])
                        ins.then_inc(turned, 1)

                    def values(h, tb):
                        pe.wait_ge(turned_out, TB * h + tb + 3)
                        pe.wait_ge(stored, TB * h + tb + 1 + deep)
                        for j in range(tb + 1):
                            ins = nc.tensor.matmul(o_ps[tb % 2][:, 0:HD],
                                                   probsT[:, tb % 2, j * P:(j + 1) * P], v(j, h),
                                                   start=(j == 0), stop=(j == tb))
                        ins.then_inc(summed, 1)

                    def start(h):
                        pe.wait_ge(q_ready, h + 1)
                        pe.wait_ge(k_ready, h + 1)
                        score(h, 0)

                    def deep_head(h, last):
                        turn_probs(h, 0)
                        if not last:
                            turn(h + 1)
                        values(h, 0)
                        turn_probs(h, 1)
                        if not last:
                            start(h + 1)
                        values(h, 1)
                        turn_probs(h, 2)
                        if not last:
                            score(h + 1, 1)
                            score(h + 1, 2)
                        values(h, 2)
                        turn_probs(h, 3)
                        if not last:
                            score(h + 1, 3)
                        values(h, 3)

                    def head(h, last):
                        if deep:
                            return deep_head(h, last)
                        turn_probs(h, 0)
                        score(h, 2)
                        turn_probs(h, 1)
                        if stage and not last:
                            turn(h + 1)
                        values(h, 0)
                        score(h, 3)
                        values(h, 1)
                        turn_probs(h, 2)
                        if not last:
                            start(h + 1)
                        turn_probs(h, 3)
                        values(h, 2)
                        if not last:
                            score(h + 1, 1)
                        values(h, 3)

                    if stage:
                        turn(0)
                    start(0)
                    for tb in range(1, AHEAD):
                        score(0, tb)
                    with pe.Fori(0, heads - 1) as h:
                        head(h, False)
                    head(heads - 1, True)

                @block.scalar
                def _(act):
                    act.preload_act_table_set("natural_log_exp_and_others")
                    if kind != "mlstm":
                        act.sem_inc(probs_ready, AHEAD)

                    def prepare(h):
                        if stage:
                            act.wait_ge(q_turned, h + 1)
                            act.wait_ge(scores, TB * h)
                            if q_gain is None:
                                nc.scalar.activation(qT[0:K, :], q_ps[0:K, :], ACT.Copy,
                                                     scale=float(HD) ** -0.5).then_inc(q_ready, 1)
                            else:
                                nc.scalar.activation(qT[0:K, :], q_ps[0:K, :], ACT.Copy,
                                                     scale=q_gain(h)).then_inc(q_ready, 1)
                        else:
                            act.wait_ge(scores, TB * h)
                            nc.scalar.activation(qT[0:K, :], qk_T(h)[0], ACT.Copy,
                                                 scale=float(HD) ** -0.5).then_inc(q_ready, 1)

                    def block_of(h, tb):
                        n, b = width(tb), tb % AHEAD
                        s = s_ps[b][:, 0:n]
                        if kind == "softmax":
                            act.wait_ge(ready_for_exp, TB * h + tb + 1)
                            act.wait_ge(turned, TB * h + tb + 1)
                            nc.scalar.activation(probs[:, b, 0:n], s, ACT.Exp, bias=peak[:, tb:tb + 1],
                                                 accum_out=total[:, tb:tb + 1]).then_inc(probs_ready, 1)
                        elif kind == "mlstm":
                            act.wait_ge(scores, TB * h + tb + 1)
                            act.wait_ge(probs_ready, TB * h + tb + 1)
                            nc.scalar.activation(work[:, b, 0:n], decay_ps[b][:, 0:n], ACT.Exp,
                                                 bias=decay[1](tb, h)).then_inc(half, 1)
                        else:
                            act.wait_ge(scores, TB * h + tb + 1)
                            act.wait_ge(ready_for_exp, TB * h + tb + 1)
                            nc.scalar.activation(work[:, b, 0:n], s, ACT.Abs)
                            act.drain()
                            nc.scalar.activation(work[:, b, 0:n], work[:, b, 0:n], ACT.Exp, scale=-1.0)
                            act.drain()
                            nc.scalar.activation(work[:, b, 0:n], work[:, b, 0:n], ACT.Ln,
                                                 bias=1.0).then_inc(half, 1)
                    def finish(h, tb):
                        n = width(tb)
                        act.wait_ge(ready_for_exp, TB * h + tb + 1 + AHEAD)
                        act.wait_ge(turned, TB * h + tb + 1)
                        nc.scalar.activation(probs[:, tb % 2, 0:n], work[:, AHEAD + tb, 0:n],
                                             ACT.Exp).then_inc(probs_ready, 1)

                    def head(h, last):
                        if kind == "softmax":
                            for tb in range(TB):
                                if tb == 3 and not last:
                                    prepare(h + 1)
                                block_of(h, tb)
                            return
                        if deep:
                            finish(h, 0)
                            finish(h, 1)
                            if not last:
                                prepare(h + 1)
                            finish(h, 2)
                            if not last:
                                block_of(h + 1, 0)
                            finish(h, 3)
                            for tb in range(1, TB):
                                if not last:
                                    block_of(h + 1, tb)
                            return
                        for tb in range(TB):
                            if tb == 1 and not last:
                                prepare(h + 1)
                            if tb < 2 or not last:
                                block_of(*((h, tb + 2) if tb < 2 else (h + 1, tb - 2)))

                    prepare(0)
                    if kind != "softmax":
                        for tb in range(AHEAD):
                            block_of(0, tb)
                    with act.Fori(0, heads - 1) as h:
                        head(h, False)
                    head(heads - 1, True)

                @block.vector
                def _(dve):
                    dve.sem_inc(turned_out, 2)
                    dve.sem_inc(stored, 2)
                    dve.sem_inc(turned, 2)
                    if kind == "mlstm":
                        dve.sem_inc(probs_ready, 2)
                    if kind == "stick":
                        dve.sem_inc(ready_for_exp, AHEAD)

                    def prepare(h):
                        if stage:
                            dve.wait_ge(k_turned, h + 1)
                            dve.wait_ge(scores, TB * h)
                            if k_gain is None:
                                nc.vector.tensor_copy(kT[0:K, :], k_ps[0:K, :]).then_inc(k_ready, 1)
                            elif kbias:
                                nc.vector.tensor_scalar(kT[0:K, :], k_ps[0:K, :], k_gain(h), None, ALU.mult)
                                nc.vector.tensor_copy(kT[K:K + 1, :], kbias(h)).then_inc(k_ready, 1)
                            else:
                                nc.vector.tensor_scalar(kT[0:K, :], k_ps[0:K, :], k_gain(h), None,
                                                        ALU.mult).then_inc(k_ready, 1)
                        else:
                            dve.wait_ge(scores, TB * h)
                            nc.vector.tensor_copy(kT[0:K, :], qk_T(h)[1]).then_inc(k_ready, 1)

                    def first(h, tb):
                        n, b = width(tb), tb % AHEAD
                        s = s_ps[b][:, 0:n]
                        if kind == "softmax":
                            dve.wait_ge(scores, TB * h + tb + 1)
                            nc.vector.tensor_reduce(peak[:, tb:tb + 1], s, AX, ALU.max,
                                                    negate=True).then_inc(ready_for_exp, 1)
                        elif kind == "mlstm":
                            dve.wait_ge(half, TB * h + tb + 1)
                            dve.wait_ge(turned, TB * h + tb + 1)
                            nc.vector.scalar_tensor_tensor(out=probs[:, b, 0:n], in0=s, scalar=1.0, in1=work[:, b, 0:n],
                                                           op0=ALU.mult, op1=ALU.mult,
                                                           accum_out=total[:, tb:tb + 1]).then_inc(probs_ready, 1)
                        else:
                            dve.wait_ge(half, TB * h + tb + 1)
                            dve.wait_ge(probs_ready, TB * h + tb + 1)
                            nc.vector.scalar_tensor_tensor(out=work[:, b, 0:n], in0=s, scalar=0.0, in1=work[:, b, 0:n],
                                                           op0=ALU.max, op1=ALU.add)
                            dve.drain()
                            nc.vector.tensor_tensor_scan(work[:, AHEAD + b, 0:n][:, ::-1], ones[:, 0:n],
                                                         work[:, b, 0:n][:, ::-1], 0.0, ALU.mult, ALU.add)
                            dve.drain()
                            nc.vector.tensor_tensor(work[:, AHEAD + b, 0:n], s, work[:, AHEAD + b, 0:n],
                                                    ALU.subtract).then_inc(ready_for_exp, 1)

                    def second(h, tb):
                        dve.wait_ge(turned, TB * h + tb + 3)
                        dve.wait_ge(summed, TB * h + tb + 1)
                        nc.vector.tensor_copy(probsT[:, tb % 2, 0:width(tb)],
                                              t_ps[tb % 2][:, 0:width(tb)]).then_inc(turned_out, 1)

                    def third(h, tb):
                        dve.wait_ge(summed, TB * h + tb + 3)
                        o = o_ps[tb % 2][:, 0:HD]
                        if kind == "stick":
                            nc.vector.tensor_copy(dst(tb, h), o).then_inc(stored, 1)
                            return
                        if kind == "mlstm":
                            nc.vector.scalar_tensor_tensor(out=recip[:, tb:tb + 1], in0=total[:, tb:tb + 1], scalar=-1.0,
                                                           in1=decay[2](tb, h), op0=ALU.mult, op1=ALU.max)
                            dve.drain()
                            nc.vector.tensor_tensor(total[:, tb:tb + 1], total[:, tb:tb + 1], recip[:, tb:tb + 1], ALU.max)
                            dve.drain()
                        nc.vector.reciprocal(recip[:, tb:tb + 1], total[:, tb:tb + 1])
                        dve.drain()
                        nc.vector.tensor_scalar(dst(tb, h), o, recip[:, tb:tb + 1], None, ALU.mult).then_inc(stored, 1)

                    def head(h, last):
                        if deep:
                            second(h, 0)
                            if not last:
                                prepare(h + 1)
                            third(h, 0)
                            for tb in range(1, TB):
                                second(h, tb)
                                if not last:
                                    first(h + 1, tb - 1)
                                third(h, tb)
                            if not last:
                                first(h + 1, 3)
                            return
                        second(h, 0)
                        first(h, 2)
                        second(h, 1)
                        third(h, 0)
                        if not last:
                            prepare(h + 1)
                        first(h, 3)
                        third(h, 1)
                        second(h, 2)
                        if not last:
                            first(h + 1, 0)
                        second(h, 3)
                        third(h, 2)
                        if not last:
                            first(h + 1, 1)
                        third(h, 3)

                    dve.sem_inc(summed, 2)
                    prepare(0)
                    for tb in range(AHEAD):
                        first(0, tb)
                    with dve.Fori(0, heads - 1) as h:
                        head(h, False)
                    head(heads - 1, True)

        w_in = [view(i * KD * IN1_TILE, KD, IN1_TILE) for i in range(2)]
        w_in_parts = [(view_r((2 + i) * KD * IN1_TILE, KD, IN1_TILE), view_r(i * KD * IN1_TILE, KD, IN1_TILE))
                      for i in range(2)]
        proj = view(17664, TB, IN1)
        w_uq, w_ukv = view(26496, Q_RANK // P, MLA_H * MLA_QK), view(28800, KV_RANK // P, MLA_H * (NOPE + MLA_V))
        pe_gain_q, pe_gain_k = view(37900, ROPE), view(37932, ROPE)
        ffn_gain = sb("ffn_gain", [P, D])
        ang = view(30848, 6, TB * ROPE // 2)
        pos_i = sb("pos_i", [TB, P], I32)
        pos_rows = sb("pos_rows", [TB, P])
        pos_f = sb("pos_f", [P, TB])
        inv_freq = sb("inv_freq", [P, ROPE // 2])
        w_in_loaded = [sem("w_in_even"), sem("w_in_odd")]
        up_loaded = sem("up_loaded")
        x_loaded = [sem(f"x_loaded{tb}") for tb in range(TB)]

        def load_first(sync):
            for tb in range(TB):
                sync.dma_start(x[:, tb, :], a["x"][0, tb * P:(tb + 1) * P, :]).then_inc(x_loaded[tb], 16)

        vec_loaded, vec_zeroed = sem("vec_loaded"), sem("vec_zeroed")
        pos_loaded, pos_float, pos_turned, gain_loaded = sem("pos_loaded"), sem("pos_float"), sem("pos_turned"), sem("gain_loaded")
        const_ready, vec_turned, vec_ready = sem("const_ready"), sem("vec_turned"), sem("vec_ready")
        angles, cos_sin = sem("angles"), sem("cos_sin")
        small_gains = [("q_norm", MLA_QK), ("k_norm", MLA_QK), ("fox_q_g_2", HD), ("fox_k_g_2", HD),
                       ("moba_q_g_2", HD), ("moba_k_g_2", HD)]
        TWO_PI = 2 * math.pi
        TURN = (6.28125, float(np.float32(TWO_PI - 6.28125)),
                TWO_PI - 6.28125 - float(np.float32(TWO_PI - 6.28125)))
        TO_INT = 1.5 * 2.0 ** 23

        with nc.Block() as block:
            @block.sync
            def _(sync):
                load_first(sync)
                sync.dma_start(pos_i[:, :], a["positions"][0].rearrange("(b p) -> b p", p=P)).then_inc(pos_loaded, 16)
                sync.wait_ge(vec_zeroed, 2)
                for name, n in pieces:
                    src = a[name][0]
                    if name == "ml_conv_w_2":
                        src = src.rearrange("c (r p) -> (c r) p", p=P)
                    else:
                        src = src.rearrange("(r p) -> r p", p=P)
                    r0, r = place[name]
                    sync.dma_start(vec_rows[r0:r0 + r, :], src).then_inc(vec_loaded, 16)
                for i, (name, n) in enumerate(small_gains):
                    sync.dma_start(small_rows[i:i + 1, 0:n], a[name]).then_inc(vec_loaded, 16)
                sync.dma_start(pe_gain_q, a["q_norm"][:, NOPE:].to_broadcast([P, ROPE])).then_inc(gain_loaded, 16)
                sync.dma_start(pe_gain_k, a["k_norm"][:, NOPE:].to_broadcast([P, ROPE])).then_inc(gain_loaded, 16)
                sync.dma_start(ffn_gain[:, :], a["ffn_norm"].to_broadcast([P, D])).then_inc(gain_loaded, 16)
                sync.wait_ge(gain_loaded, 48)

            @block.gpsimd
            def _(pool):
                nc.gpsimd.memset(vec_rows[:, :], 0.0).then_inc(vec_zeroed, 1)
                nc.gpsimd.memset(small_rows[:, :], 0.0).then_inc(vec_zeroed, 1)
                nc.gpsimd.memset(ident[:, :], 0.0)
                nc.gpsimd.memset(ident_bf[:, :], 0.0)
                for m in (strict_mask, causal_mask, chunk_mask):
                    nc.gpsimd.memset(m[:, :], 0.0)
                for j in range(ROPE // 2):
                    f = np.float32(1.0) / np.float32(10000.0) ** np.float32(j * 2.0 / ROPE)
                    nc.gpsimd.memset(inv_freq[:, j:j + 1], float(f))
                pool.drain()
                for m in (ident, ident_bf):
                    nc.gpsimd.affine_select(out=m[:, :], in_=m[:, :], compare_op=ALU.not_equal, fill=1.0, base=0,
                                            pattern=[[-1, P]], channel_multiplier=1)
                nc.gpsimd.affine_select(out=strict_mask[:, :], in_=strict_mask[:, :], compare_op=ALU.is_gt,
                                        fill=MASKED, base=0, pattern=[[-1, P]], channel_multiplier=1)
                nc.gpsimd.affine_select(out=causal_mask[:, :], in_=causal_mask[:, :], compare_op=ALU.is_ge,
                                        fill=MASKED, base=0, pattern=[[-1, P]], channel_multiplier=1)
                for c in range(CHUNK, P, CHUNK):
                    nc.gpsimd.memset(chunk_mask[c - CHUNK:c, c:P], MASKED)
                nc.gpsimd.memset(ones[:, :], 1.0)
                pool.drain().then_inc(const_ready, 1)

            @block.tensor
            def _(pe):
                pe.wait_ge(const_ready, 1)
                pe.wait_ge(pos_float, 1)
                nc.tensor.transpose(psum[1][:, 0:TB], pos_rows[:, :], ident[0:TB, 0:TB]).then_inc(pos_turned, 1)
                pe.wait_ge(vec_loaded, 16 * (len(pieces) + len(small_gains)))
                nc.tensor.transpose(psum[0][:, 0:P], vec_rows[:, :], ident[:, :])
                nc.tensor.transpose(psum[0][:, P:P + 8], small_rows[:, :], ident[0:8, 0:8]).then_inc(vec_turned, 1)

            @block.vector
            def _(dve):
                dve.wait_ge(pos_loaded, 16)
                nc.vector.tensor_copy(pos_rows[:, :], pos_i[:, :]).then_inc(pos_float, 1)
                dve.wait_ge(pos_turned, 1)
                nc.vector.tensor_copy(pos_f[:, :], psum[1][:, 0:TB])
                dve.wait_ge(const_ready, 1)
                dve.drain()
                n = ROPE // 2
                whole = [ang[:, i, :].rearrange("p (b j) -> p b j", j=n) for i in range(6)]
                nc.vector.tensor_tensor(whole[0], pos_f[:, :].unsqueeze(2).to_broadcast([P, TB, n]),
                                        inv_freq[:, :].unsqueeze(1).to_broadcast([P, TB, n]), ALU.mult)
                for i, (quarter, shift) in enumerate(((0.0, 0.0), (0.25, math.pi / 2))):
                    t, r = ang[:, 1 + i, :], ang[:, 3 + i, :]
                    dve.drain()
                    nc.vector.tensor_scalar(t, ang[:, 0, :], 1 / TWO_PI, quarter, ALU.mult, ALU.add)
                    dve.drain()
                    nc.vector.tensor_scalar(t, t, TO_INT, TO_INT, ALU.add, ALU.subtract)
                    dve.drain()
                    nc.vector.scalar_tensor_tensor(out=r, in0=t, scalar=-TURN[0], in1=ang[:, 0, :], op0=ALU.mult,
                                                   op1=ALU.add)
                    for part in TURN[1:]:
                        dve.drain()
                        nc.vector.scalar_tensor_tensor(out=r, in0=t, scalar=-part, in1=r, op0=ALU.mult, op1=ALU.add)
                    dve.drain()
                    nc.vector.tensor_scalar(r, r, shift, 3.1415925, ALU.add, ALU.min)
                    dve.drain()
                    nc.vector.tensor_scalar(r, r, -3.1415925, None, ALU.max).then_inc(angles, 1)
                dve.wait_ge(vec_turned, 1)
                nc.vector.tensor_copy(vec[:, :], psum[0][:, 0:P])
                nc.vector.tensor_copy(small[:, :], psum[0][:, P:P + 8]).then_inc(vec_ready, 1)
                dve.drain()
                nc.vector.tensor_scalar(gains[0:NOPE, 0:1], small[0:NOPE, 0:1], MLA_QK ** -0.5, None, ALU.mult)
                nc.vector.memset(gains[NOPE:MLA_QK, 0:1], MLA_QK ** -0.5)
                nc.vector.tensor_copy(gains[0:NOPE, 1:2], small[0:NOPE, 1:2])
                nc.vector.memset(gains[NOPE:MLA_QK, 1:2], 1.0)
                for c0, n, g, scale in ((GQ, FOX_H, 2, HD ** -0.5), (GQ + FOX_H, MOBA_H, 4, HD ** -0.5),
                                        (GK, FOX_H, 3, 1.0), (GK + FOX_H, MOBA_H, 5, 1.0)):
                    nc.vector.tensor_scalar(gains[0:HD, c0:c0 + n], small[0:HD, g:g + 1].to_broadcast([HD, n]),
                                            scale, None, ALU.mult)

            @block.scalar
            def _(act):
                act.wait_ge(angles, 2)
                nc.scalar.activation(sin[:, :, :].rearrange("p b j -> p (b j)"), ang[:, 3, :], ACT.Sin)
                nc.scalar.activation(cos[:, :, :].rearrange("p b j -> p (b j)"), ang[:, 4, :], ACT.Sin).then_inc(cos_sin, 1)
                act.wait_ge(vec_ready, 1)
                c0, n = place["c_2"]
                nc.scalar.activation(silu_c[:, :], vec[:, c0:c0 + n], ACT.Silu)

        w_in_all = a["w_in"][0].rearrange("(k p) n -> p k n", p=P)

        def load_w_in(sync):
            for i in range(2):
                sync.dma_start(w_in[i], w_in_all[:, :, i * IN1_TILE:(i + 1) * IN1_TILE]).then_inc(w_in_loaded[i], 16)

        norm_T("n1_", x, [(0, D)], rows, hT, gain_cols=lambda k: col("attn_norm", k),
               ready=lambda engine, tb: engine.wait_ge(x_loaded[tb], 16), loads=load_w_in, parts=True)

        in_summed, in_copied = sem("in_summed"), sem("in_copied")
        w_in_split = sem("w_in_split")
        ADA_TILE = 512
        ADA_TILES = 6 * D // ADA_TILE
        ada_w = [view(4 * KD * IN1_TILE, KD, ADA_TILE), view(26496, KD, ADA_TILE)]
        ada_sum = view(30848, 6 * D)
        ada_loaded, ada_used = [sem("ada_loaded0"), sem("ada_loaded1")], [sem("ada_used0"), sem("ada_used1")]
        ada_summed = sem("ada_summed")
        w_ada = a["w_ada_2"][0].rearrange("(k p) n -> p k n", p=P)
        ADA_EARLY = 8
        assert ADA_EARLY == IN1_TILES + 2

        def modulate(dve, t, slot, w):
            dve.wait_ge(ada_loaded[slot], 16 * t + 16)
            o = ada_sum[:, ds((2 * t + slot) * ADA_TILE, ADA_TILE)]
            nc.vector.tensor_scalar(o, w[:, 0, :], silu_c[:, 0:1], None, ALU.mult)
            for k in range(1, KD):
                dve.drain()
                ins = nc.vector.scalar_tensor_tensor(out=o, in0=w[:, k, :], scalar=silu_c[:, k:k + 1], in1=o,
                                                     op0=ALU.mult, op1=ALU.add)
            ins.then_inc(ada_used[slot], 1)

        with nc.Block() as block:
            @block.sync
            def _(sync):
                with sync.Fori(1, IN1_TILES // 2) as i:
                    for odd in range(2):
                        sync.wait_ge(in_summed, 8 * i + TB * (odd - 1))
                        sync.dma_start(w_in[odd], w_in_all[:, :, ds((2 * i + odd) * IN1_TILE, IN1_TILE)])\
                            .then_inc(w_in_loaded[odd], 16)

            @block.gpsimd
            def _(pool):
                for slot in range(2):
                    nc.gpsimd.dma_start(ada_w[slot], w_ada[:, :, slot * ADA_TILE:(slot + 1) * ADA_TILE])\
                        .then_inc(ada_loaded[slot], 16)
                with pool.Fori(1, ADA_EARLY // 2) as t:
                    for slot in range(2):
                        pool.wait_ge(ada_used[slot], t)
                        nc.gpsimd.dma_start(ada_w[slot], w_ada[:, :, ds((2 * t + slot) * ADA_TILE, ADA_TILE)])\
                            .then_inc(ada_loaded[slot], 16)

            @block.tensor
            def _(pe):
                with pe.Fori(0, IN1_TILES // 2) as i:
                    for odd in range(2):
                        pe.wait_ge(w_in_split, 2 * i + odd + 1)
                        for tb in range(TB):
                            pe.wait_ge(in_copied, 8 * i + TB * odd + tb + 1)
                            for k in range(KD):
                                ins = product(psum[4 * odd + tb][:, 0:IN1_TILE], h_rows(k, tb),
                                              [part[:, k, :] for part in w_in_parts[odd]], k == 0, k == KD - 1)
                            ins.then_inc(in_summed, 1)

            @block.scalar
            def _(act):
                act.sem_inc(in_copied, 8)
                with act.Fori(0, IN1_TILES // 2) as i:
                    for odd in range(2):
                        for tb in range(TB):
                            act.wait_ge(in_summed, 8 * i + TB * odd + tb + 1)
                            nc.scalar.copy(proj[:, tb, ds((2 * i + odd) * IN1_TILE, IN1_TILE)],
                                           psum[4 * odd + tb][:, 0:IN1_TILE]).then_inc(in_copied, 1)

            @block.vector
            def _(dve):

                def split_tile(i, odd):
                    dve.wait_ge(w_in_loaded[odd], 16 * i + 16)
                    split(dve, w_in[odd], *w_in_parts[odd]).then_inc(w_in_split, 1)

                last = IN1_TILES // 2 - 1
                split_tile(0, 0)
                with dve.Fori(0, last) as i:
                    for odd in range(2):
                        split_tile(i + odd, 1 - odd)
                        modulate(dve, i, odd, ada_w[odd])
                split_tile(last, 1)
                for t in range(2 * last, ADA_EARLY):
                    modulate(dve, t // 2, t % 2, ada_w[t % 2])

        def load_up(sync):
            sync.dma_start(w_uq, a["w_uq"][0].rearrange("(k p) n -> p k n", p=P)).then_inc(up_loaded, 16)
            sync.dma_start(w_ukv, a["w_ukv"][0].rearrange("(k p) n -> p k n", p=P)).then_inc(up_loaded, 16)

        def stage_sb(h, q_st, k_st, staged):
            nc.gpsimd.tensor_copy(q_st[:, :, 0:HD], proj[:, :, ds(h * HD, HD)]).then_inc(staged, 1)
            nc.gpsimd.tensor_copy(k_st[:, :, 0:HD], proj[:, :, ds(h * HD + SB_W, HD)]).then_inc(staged, 1)

        SCRATCH1 = 30848
        attention("sb_", "stick", SB_H, HD, 0, stage_sb, None, None,
                  v=lambda j, h: proj[:, j, ds(h * HD + 2 * SB_W, HD)],
                  dst=lambda tb, h: rows[:, tb, ds(h * HD, HD)], mask=strict_mask,
                  loads=load_up)

        latent = view(0, TB, IN1)
        q_up, kv_up = view(8832, TB, MLA_H * MLA_QK), view(11904, TB, MLA_H * (NOPE + MLA_V))
        squares_q, squares_k = view(0, TB * MLA_H, MLA_QK), view(3072, TB * MLA_H, NOPE)
        q_pe, t_pe = view(5120, TB * MLA_H, ROPE), view(6144, 4, TB * MLA_H * ROPE // 2)
        k_pe, u_pe = view(8192, TB, ROPE), view(8320, 4, TB * ROPE // 2)
        pe_rot = view(16000, TB, ROPE)
        ss_q, ss_k = view(16128, TB * MLA_H), view(16160, TB * MLA_H)
        ss_pe = view(16192, TB)
        pe_junk = view(16196, TB, ROPE)
        rms_q, rms_k = view(16324, TB, MLA_H), view(16356, TB, MLA_H)
        KQ, KKV = Q_RANK // P, KV_RANK // P

        norm_T("n2_", proj, [(CQ0, Q_RANK), (CKV0, KV_RANK)], latent, hT, gain_cols=lambda k: col("cq_norm", k))

        up_tiles = [(w_uq[:, :, i * 384:(i + 1) * 384], 384, lambda tb, i=i: q_up[:, tb, i * 384:(i + 1) * 384])
                    for i in range(2)]
        up_tiles += [(w_ukv[:, :, i * 512:(i + 1) * 512], 512, lambda tb, i=i: kv_up[:, tb, i * 512:(i + 1) * 512])
                     for i in range(2)]
        up_summed, up_copied = sem("up_summed"), sem("up_copied")
        ada_late = [view(i * KD * ADA_TILE, KD, ADA_TILE) for i in range(2)]
        with nc.Block() as block:
            @block.gpsimd
            def _(pool):
                for t in range(ADA_EARLY, ADA_TILES):
                    if t >= ADA_EARLY + 2:
                        pool.wait_ge(ada_used[t % 2], t // 2)
                    nc.gpsimd.dma_start(ada_late[t % 2], w_ada[:, :, t * ADA_TILE:(t + 1) * ADA_TILE])\
                        .then_inc(ada_loaded[t % 2], 16)

            @block.tensor
            def _(pe):
                pe.wait_ge(up_loaded, 32)
                for i, (w, n, _) in enumerate(up_tiles):
                    k0, kt = (0, KQ) if i < 2 else (KQ, KKV)
                    for tb in range(TB):
                        if i >= 2:
                            pe.wait_ge(up_copied, TB * (i - 2) + tb + 1)
                        for k in range(kt):
                            ins = nc.tensor.matmul(psum[4 * (i % 2) + tb][:, 0:n], hT[:, k0 + k, tb * P:(tb + 1) * P],
                                                   w[:, k, :], start=(k == 0), stop=(k == kt - 1))
                        ins.then_inc(up_summed, 1)

            @block.scalar
            def _(act):
                for i, (_, n, dst) in enumerate(up_tiles):
                    for tb in range(TB):
                        act.wait_ge(up_summed, TB * i + tb + 1)
                        nc.scalar.copy(dst(tb), psum[4 * (i % 2) + tb][:, 0:n]).then_inc(up_copied, 1)

            @block.vector
            def _(dve):
                for t in range(ADA_EARLY, ADA_TILES):
                    modulate(dve, t // 2, t % 2, ada_late[t % 2])

        squared, rms_mean, rms_ready, rotated = sem("squared"), sem("rms_mean"), sem("rms_ready"), sem("rotated")
        with nc.Block() as block:
            q_heads = q_up.rearrange("p b (h d) -> p (b h) d", d=MLA_QK)
            kv_heads = kv_up.rearrange("p b (h d) -> p (b h) d", d=NOPE + MLA_V)
            HALF = ROPE // 2

            @block.tensor
            def _(pe):
                for c in range(6 * KD):
                    ins = nc.tensor.matmul(psum[0][:, c:c + 1], ada_sum[:, c * P:(c + 1) * P], ones[:, 0:1],
                                           start=True, stop=True)
                ins.then_inc(ada_summed, 1)

            @block.scalar
            def _(act):
                nc.scalar.activation(squares_q, q_heads, ACT.Square).then_inc(squared, 1)
                nc.scalar.activation(squares_k, kv_heads[:, :, 0:NOPE], ACT.Square)
                for tb in range(TB):
                    ins = nc.scalar.activation(pe_junk[:, tb, :], proj[:, tb, KPE0:KPE0 + ROPE], ACT.Square,
                                               accum_out=ss_pe[:, tb:tb + 1])
                ins.then_inc(squared, 1)
                for i, (ss, rms) in enumerate(((ss_q, rms_q), (ss_k, rms_k))):
                    act.wait_ge(rms_mean, i + 1)
                    nc.scalar.activation(ss, ss, ACT.Ln)
                    act.drain()
                    nc.scalar.activation(rms.rearrange("p b h -> p (b h)"), ss, ACT.Exp, scale=-0.5)

            @block.vector
            def _(dve):
                dve.wait_ge(squared, 1)
                nc.vector.tensor_reduce(ss_q, squares_q, AX, ALU.add)
                dve.drain()
                nc.vector.tensor_scalar(ss_q, ss_q, 1.0 / MLA_QK, EPS, ALU.mult, ALU.add).then_inc(rms_mean, 1)
                dve.wait_ge(squared, 2)
                nc.vector.tensor_reduce(ss_k, squares_k, AX, ALU.add)
                dve.drain()
                by_head = ss_k.rearrange("p (b h) -> p b h", h=MLA_H)
                nc.vector.tensor_tensor(by_head, by_head, ss_pe.unsqueeze(2).to_broadcast([P, TB, MLA_H]), ALU.add)
                dve.drain()
                nc.vector.tensor_scalar(ss_k, ss_k, 1.0 / MLA_QK, EPS, ALU.mult, ALU.add).then_inc(rms_mean, 1)
                n = TB * MLA_H
                nc.vector.tensor_tensor(q_pe, q_heads[:, :, NOPE:MLA_QK], pe_gain_q.unsqueeze(1).to_broadcast([P, n, ROPE]),
                                        ALU.mult)
                dve.drain()
                x1 = q_pe[:, :, 0:HALF].rearrange("p (b h) d -> p b h d", h=MLA_H)
                x2 = q_pe[:, :, HALF:ROPE].rearrange("p (b h) d -> p b h d", h=MLA_H)
                c = cos[:, :, :].unsqueeze(2).to_broadcast([P, TB, MLA_H, HALF])
                s = sin[:, :, :].unsqueeze(2).to_broadcast([P, TB, MLA_H, HALF])
                t = [t_pe[:, i, :].rearrange("p (b h d) -> p b h d", h=MLA_H, d=HALF) for i in range(4)]
                for o, u, w in zip(t, (x1, x2, x1, x2), (c, s, s, c)):
                    nc.vector.tensor_tensor(o, u, w, ALU.mult)
                dve.drain()
                flat = [t_pe[:, i, :].rearrange("p (n d) -> p n d", d=HALF) for i in range(4)]
                nc.vector.tensor_tensor(q_heads[:, :, NOPE:NOPE + HALF], flat[0], flat[1], ALU.subtract)
                nc.vector.tensor_tensor(q_heads[:, :, NOPE + HALF:MLA_QK], flat[2], flat[3], ALU.add)
                dve.wait_ge(ada_summed, 1)
                c0, n = place["b_ada_2"]
                nc.vector.tensor_tensor(mod[:, :], psum[0][:, 0:n], vec[:, c0:c0 + n], ALU.add)

            @block.gpsimd
            def _(pool):
                nc.gpsimd.tensor_tensor(k_pe, proj[:, :, KPE0:KPE0 + ROPE],
                                        pe_gain_k.unsqueeze(1).to_broadcast([P, TB, ROPE]), ALU.mult)
                pool.drain()
                x1, x2 = k_pe[:, :, 0:HALF], k_pe[:, :, HALF:ROPE]
                t = [u_pe[:, i, :].rearrange("p (b d) -> p b d", d=HALF) for i in range(4)]
                for o, u, w in zip(t, (x1, x2, x1, x2), (cos, sin, sin, cos)):
                    nc.gpsimd.tensor_tensor(o, u, w[:, :, :], ALU.mult)
                pool.drain()
                nc.gpsimd.tensor_tensor(pe_rot[:, :, 0:HALF], t[0], t[1], ALU.subtract)
                nc.gpsimd.tensor_tensor(pe_rot[:, :, HALF:ROPE], t[2], t[3], ALU.add)

        w_o = view(17664, KD, D)
        w_o_loaded, keys_loaded = sem("w_o_loaded"), sem("keys_loaded")
        w_q = view(26496, KD, 2 * PD)
        w_q_loaded = sem("w_q_loaded")

        def stage_mla(h, q_st, k_st, staged):
            nc.gpsimd.tensor_tensor(q_st, q_up[:, :, ds(h * MLA_QK, MLA_QK)],
                                    rms_q[:, :, ds(h, 1)].to_broadcast([P, TB, MLA_QK]), ALU.mult).then_inc(staged, 1)
            nc.gpsimd.tensor_tensor(k_st[:, :, 0:NOPE], kv_up[:, :, ds(h * (NOPE + MLA_V), NOPE)],
                                    rms_k[:, :, ds(h, 1)].to_broadcast([P, TB, NOPE]), ALU.mult)
            nc.gpsimd.tensor_tensor(k_st[:, :, NOPE:MLA_QK], pe_rot,
                                    rms_k[:, :, ds(h, 1)].to_broadcast([P, TB, ROPE]), ALU.mult).then_inc(staged, 1)

        def load_w_o(sync):
            sync.dma_start(w_o, a["w_o"][0].rearrange("(k p) n -> p k n", p=P)).then_inc(w_o_loaded, 16)
            sync.dma_start(w_q, a["peer_w_q"][0].rearrange("(k p) n -> p k n", p=P)[:, :, 0:2 * PD])\
                .then_inc(w_q_loaded, 16)

        attention("mla_", "softmax", MLA_H, MLA_QK, SCRATCH1, stage_mla, lambda h: gains[0:MLA_QK, 0:1],
                  lambda h: gains[0:MLA_QK, 1:2],
                  v=lambda j, h: kv_up[:, j, ds(h * (NOPE + MLA_V) + NOPE, MLA_V)],
                  dst=lambda tb, h: rows[:, tb, ds(h * MLA_V + SB_W, MLA_V)], mask=chunk_mask,
                  loads=load_w_o)

        key_rows = view(32896, 2 * PH, PD)
        keysT = view(30848, 2 * PH, PN)

        def load_keys(sync):
            sync.dma_start(key_rows, a["peer_sub_keys"][0].rearrange("c h n d -> n (c h) d")).then_inc(keys_loaded, 16)

        norm_T("n3_", rows, [(0, SB_W), (SB_W, MLA_H * MLA_V)], rows, hT,
               gain_cols=lambda k: col("sb_out_norm", k), loads=load_keys, scratch=view(0, TB, D), parts=True)

        def out_projection(tag, w, w_parts, order, loaded, gate_row=None):
            split_w, summed = sem(tag + "split"), sem(tag + "summed")
            with nc.Block() as block:
                @block.tensor
                def _(pe):
                    for k in range(KD):
                        pe.wait_ge(split_w, k + 1)
                        for tb in range(TB):
                            for half in range(2):
                                c = slice(half * 512, (half + 1) * 512)
                                ins = product(psum[4 * half + tb][:, :], h_rows(k, tb),
                                              [part[:, order[k], c] for part in w_parts], k == 0, k == KD - 1)
                            if k == KD - 1:
                                ins.then_inc(summed, 1)

                @block.vector
                def _(dve):
                    dve.wait_ge(loaded, 16)
                    for k in range(KD):
                        if gate_row is not None:
                            nc.vector.tensor_tensor(w[:, order[k], :], w[:, order[k], :], gate_row[:, :], ALU.mult)
                            dve.drain()
                        split(dve, w[:, order[k], :], *[part[:, order[k], :] for part in w_parts]).then_inc(split_w, 1)
                    for tb in range(TB):
                        dve.wait_ge(summed, tb + 1)
                        for half in range(2):
                            c = slice(half * 512, (half + 1) * 512)
                            nc.vector.tensor_tensor(x[:, tb, c], x[:, tb, c], psum[4 * half + tb][:, :], ALU.add)

        out_projection("o1_", w_o, (view_r(4096, KD, D), view_r(17664, KD, D)), range(KD), w_o_loaded)
        keys_turned = sem("keys_turned")

        def turn_keys(pe):
            pe.wait_ge(keys_loaded, 16)
            for g in range(4):
                for i in range(4):
                    ins = nc.tensor.transpose(psum[4 + g][:, i * PN:(i + 1) * PN], key_rows[:, 4 * g + i, :], ident[:, :])
                ins.then_inc(keys_turned, 1)

        def copy_keys(dve):
            for g in range(4):
                dve.wait_ge(keys_turned, g + 1)
                nc.vector.tensor_copy(keysT[:, 4 * g:4 * g + 4, :].rearrange("p a b -> p (a b)"), psum[4 + g][:, :])

        norm_T("n4_", x, [(0, D)], rows, hT, gain_row=ffn_gain, pe_first=turn_keys, dve_first=copy_keys)

        RING = 8
        u_ring, v_ring = view(0, RING, D), view(RING * D, RING, D)
        diag = view(16384, RING, P)
        q_T = view(17664, 2, T)
        half_sc = view(34944, 2, TB * PN)
        TK = 35968
        left = view(TK, PN)
        cand, cand_left = view(TK + 128, PK, PK), view(TK + 384, PK * PK)
        picked = view(TK + 640, 2, PK * PK)
        half_top, half_at = view(TK + 1152, 2, PK), view(TK + 1184, 2, PK)
        best, best_exp, best_neg, best_sum = (view(TK + 1216, PK), view(TK + 1232, PK), view(TK + 1248, 1),
                                              view(TK + 1249, 1))
        pos, pos_f2, ids = view(TK + 1250, 2, PK), view(TK + 1282, 2, PK), view(TK + 1314, 2, PK)
        iota16 = view(TK + 1346, PK)
        iota16_i = view(TK + 1362, PK).bitcast(I32)
        best_at = view(TK + 1378, PK).bitcast(U32)
        half_at_u = view(TK + 1394, 2, PK).bitcast(U32)
        share = view(TK + 1426, TB, PK)
        expert = view(TK + 1490, TB, PK).bitcast(I32)
        pre, gelu = view(TK + 1554, PK), view(TK + 1570, PK)
        coef = view(TK + 1586, 2, PK)
        assert TK + 1618 <= 37900
        STEPS = PH * TB

        iota_ready = sem("iota_ready")
        q_summed, q_copied, sc_summed, sc_copied = sem("q_summed"), sem("q_copied"), sem("sc_summed"), sem("sc_copied")
        first_q_summed, first_q_copied = sem("first_q_summed"), sem("first_q_copied")
        first_sc_summed, first_sc_copied = sem("first_sc_summed"), sem("first_sc_copied")
        best_ready, exp_done, chosen = sem("best_ready"), sem("exp_done"), sem("chosen")
        u_in = [sem(f"u_in{i}") for i in range(RING)]
        v_in = [sem(f"v_in{i}") for i in range(RING)]
        u_used, v_used, pre_ready, gelu_ready = sem("u_used"), sem("v_used"), sem("pre_ready"), sem("gelu_ready")
        coef_ready, diag_ready, y_added = sem("coef_ready"), sem("diag_ready"), sem("y_added")

        with nc.Block() as block:
            @block.sync
            def _(sync):
                w = a["peer_w_q"][0].rearrange("(k p) n -> p k n", p=P)
                with sync.Fori(1, PH) as h:
                    sync.wait_ge(q_summed, 2 * h)
                    sync.dma_start(w_q, w[:, :, ds(h * 2 * PD, 2 * PD)]).then_inc(w_q_loaded, 16)

            @block.gpsimd
            def _(pool):
                nc.gpsimd.iota(iota16_i, [[1, PK]], base=0, channel_multiplier=0).then_inc(iota_ready, 1)

                def gather(table, slot, step, j):
                    tb = step[1]
                    ring, used, arrived = (u_ring, u_used, u_in) if table == "peer_u" else (v_ring, v_used, v_in)
                    pool.wait_ge(used, step[0] * PK + j + 1)
                    if j == 0 and table == "peer_u":
                        pool.wait_ge(chosen, step[0] + 1)
                    pool.nop(nofuse=True)
                    nc.gpsimd.indirect_dma_start(
                        out=ring[:, slot, :], out_offset=None, in_=a[table][0],
                        in_offset=bass.IndirectOffsetOnAxis(ap=expert[:, tb, j:j + 1], axis=0),
                    ).then_inc(arrived[slot], 16)

                def step_of(h, tb, last):
                    for j in range(PK):
                        gather("peer_v", j % RING, (TB * h + tb, tb), j)
                        if not last:
                            gather("peer_u", j % RING, (TB * h + tb + 1, (tb + 1) % TB), j)

                for j in range(PK):
                    gather("peer_u", j % RING, (0, 0), j)
                with pool.Fori(0, PH - 1) as h:
                    for tb in range(TB):
                        step_of(h, tb, False)
                for tb in range(TB):
                    step_of(PH - 1, tb, tb == TB - 1)

            @block.tensor
            def _(pe):
                def first_query():
                    pe.wait_ge(w_q_loaded, 16)
                    for c in range(2):
                        for k in range(KD):
                            ins = nc.tensor.matmul(psum[c][:, 0:P], w_q[:, k, c * PD:(c + 1) * PD], hT[:, k, 0:P],
                                                   start=(k == 0), stop=(k == KD - 1))
                        ins.then_inc(first_q_summed, 1)
                    for c in range(2):
                        pe.wait_ge(first_q_copied, c + 1)
                        nc.tensor.matmul(psum[2 + c][:, 0:PN], q_T[:, c, 0:P], keysT[:, c * PH, :],
                                         start=True, stop=True).then_inc(first_sc_summed, 1)

                def query(h, tb0=0):
                    pe.wait_ge(w_q_loaded, 16 * h + 16)
                    for c in range(2):
                        for k in range(KD):
                            ins = nc.tensor.matmul(psum[4 + c][:, tb0 * P:], w_q[:, k, c * PD:(c + 1) * PD],
                                                   hT[:, k, tb0 * P:], start=(k == 0), stop=(k == KD - 1))
                        ins.then_inc(q_summed, 1)
                    for c in range(2):
                        pe.wait_ge(q_copied, 2 * h + c + 1)
                        for tb in range(tb0, TB):
                            ins = nc.tensor.matmul(psum[6 + c][:, tb * PN:(tb + 1) * PN], q_T[:, c, tb * P:(tb + 1) * P],
                                                   keysT[:, ds(h + c * PH, 1), :].squeeze(1), start=True, stop=True)
                        ins.then_inc(sc_summed, 1)

                def values(h, tb):
                    step = TB * h + tb
                    pe.wait_ge(y_added, step + 1)
                    for j in range(PK):
                        pe.wait_ge(v_in[j % RING], step * 32 + 16 * (j // RING) + 16)
                        pe.wait_ge(diag_ready, step * PK + j + 1)
                        for half in range(2):
                            ins = nc.tensor.matmul(psum[2 * (tb % 2) + half][:, :], diag[:, j % RING, :],
                                                   v_ring[:, j % RING, half * 512:(half + 1) * 512], start=(j == 0),
                                                   stop=(j == PK - 1))
                        ins.then_inc(v_used, 1)

                first_query()
                query(0, 1)
                with pe.Fori(0, PH - 1) as h:
                    query(h + 1)
                    for tb in range(TB):
                        values(h, tb)
                for tb in range(TB):
                    values(PH - 1, tb)

            @block.scalar
            def _(act):
                act.sem_inc(v_used, RING)

                def first_query():
                    for c in range(2):
                        act.wait_ge(first_q_summed, c + 1)
                        nc.scalar.copy(q_T[:, c, 0:P], psum[c][:, 0:P]).then_inc(first_q_copied, 1)
                    for c in range(2):
                        act.wait_ge(first_sc_summed, c + 1)
                        nc.scalar.copy(half_sc[:, c, 0:PN], psum[2 + c][:, 0:PN]).then_inc(first_sc_copied, 1)

                def query(h, tb0=0):
                    for c in range(2):
                        act.wait_ge(q_summed, 2 * h + c + 1)
                        nc.scalar.copy(q_T[:, c, tb0 * P:], psum[4 + c][:, tb0 * P:]).then_inc(q_copied, 1)
                    if tb0 == 0:
                        act.wait_ge(chosen, TB * h)
                    for c in range(2):
                        act.wait_ge(sc_summed, 2 * h + c + 1)
                        nc.scalar.copy(half_sc[:, c, tb0 * PN:], psum[6 + c][:, tb0 * PN:]).then_inc(sc_copied, 1)

                def share_exp(step):
                    act.wait_ge(best_ready, step + 1)
                    nc.scalar.activation(best_exp, best, ACT.Exp, bias=best_neg, accum_out=best_sum).then_inc(exp_done, 1)

                def gelus(step):
                    act.wait_ge(pre_ready, step + 1)
                    nc.scalar.activation(gelu, pre, ACT.Gelu).then_inc(gelu_ready, 1)

                def diags(h, tb):
                    step = TB * h + tb
                    act.wait_ge(coef_ready, step + 1)
                    for j in range(PK):
                        act.wait_ge(v_used, step * PK + j + 1)
                        nc.scalar.activation(diag[:, j % RING, :], ident[:, :], ACT.Copy,
                                             scale=coef[:, tb % 2, j:j + 1]).then_inc(diag_ready, 1)

                first_query()
                query(0, 1)
                share_exp(0)
                share_exp(1)
                gelus(0)
                share_exp(2)
                share_exp(3)
                with act.Fori(0, PH - 1) as h:
                    query(h + 1)
                    for tb in range(TB):
                        diags(h, tb)
                        gelus(TB * h + tb + 1)
                        share_exp(TB * h + tb + TB)
                for tb in range(TB):
                    diags(PH - 1, tb)
                    if tb < TB - 1:
                        gelus(TB * (PH - 1) + tb + 1)

            @block.vector
            def _(dve):
                dve.sem_inc(u_used, RING)
                dve.sem_inc(y_added, 2)
                dve.wait_ge(iota_ready, 1)
                nc.vector.tensor_copy(iota16, iota16_i)

                def top16(values_in, rest, top, at):
                    nc.vector.max(top[:, 0:8], values_in)
                    dve.drain()
                    nc.vector.max_index(at[:, 0:8], top[:, 0:8], values_in)
                    nc.vector.match_replace(rest, top[:, 0:8], values_in, -3.0e38)
                    dve.drain()
                    nc.vector.max(top[:, 8:16], rest)
                    dve.drain()
                    nc.vector.max_index(at[:, 8:16], top[:, 8:16], rest)

                def choose(h, tb, scores):
                    dve.drain()
                    if scores is not None:
                        dve.wait_ge(*scores)
                        dve.nop(nofuse=True)
                    for c in range(2):
                        top16(half_sc[:, c, tb * PN:(tb + 1) * PN], left, half_top[:, c, :], half_at_u[:, c, :])
                    dve.drain()
                    nc.vector.tensor_copy(half_at, half_at_u)
                    nc.vector.tensor_tensor(cand, half_top[:, 0, :].unsqueeze(2).to_broadcast([P, PK, PK]),
                                            half_top[:, 1, :].unsqueeze(1).to_broadcast([P, PK, PK]), ALU.add)
                    dve.drain()
                    top16(cand.rearrange("p a b -> p (a b)"), cand_left, best, best_at)
                    dve.drain()
                    nc.vector.tensor_scalar(best_neg, best[:, 0:1], -1.0, None, ALU.mult).then_inc(best_ready, 1)
                    nc.vector.tensor_scalar(pos[:, 0, :].bitcast(U32), best_at, 4, None, ALU.logical_shift_right)
                    nc.vector.tensor_scalar(pos[:, 1, :].bitcast(U32), best_at, PK - 1, None, ALU.bitwise_and)
                    dve.drain()
                    nc.vector.tensor_copy(pos_f2, pos.bitcast(U32))
                    dve.drain()
                    for c in range(2):
                        nc.vector.tensor_tensor(picked[:, c, :].rearrange("p (k m) -> p k m", m=PK),
                                                pos_f2[:, c, :].unsqueeze(2).to_broadcast([P, PK, PK]),
                                                iota16.unsqueeze(1).to_broadcast([P, PK, PK]), ALU.is_equal)
                    dve.drain()
                    for c in range(2):
                        p = picked[:, c, :].rearrange("p (k m) -> p k m", m=PK)
                        nc.vector.tensor_tensor(p, p, half_at[:, c, :].unsqueeze(1).to_broadcast([P, PK, PK]), ALU.mult)
                    dve.drain()
                    nc.vector.tensor_reduce(ids.rearrange("p c k -> p (c k)"),
                                            picked.rearrange("p c (k m) -> p (c k) m", m=PK), AX, ALU.add)
                    dve.drain()
                    nc.vector.scalar_tensor_tensor(out=expert[:, tb, :], in0=ids[:, 0, :], scalar=float(PN),
                                                   in1=ids[:, 1, :], op0=ALU.mult, op1=ALU.add)
                    dve.wait_ge(exp_done, TB * h + tb + 1)
                    nc.vector.reciprocal(best_sum, best_sum)
                    dve.drain()
                    nc.vector.tensor_scalar(share[:, tb, :], best_exp, best_sum, None, ALU.mult).then_inc(chosen, 1)

                def dots(step, tb):
                    for j in range(PK):
                        dve.wait_ge(u_in[j % RING], step * 32 + 16 * (j // RING) + 16)
                        ins = nc.vector.scalar_tensor_tensor(out=u_ring[:, j % RING, :], in0=u_ring[:, j % RING, :],
                                                             scalar=1.0, in1=rows[:, tb, :], op0=ALU.mult,
                                                             op1=ALU.mult, accum_out=pre[:, j:j + 1])
                        ins.then_inc(u_used, 1)
                    dve.drain().then_inc(pre_ready, 1)
                    dve.wait_ge(gelu_ready, step + 1)
                    nc.vector.tensor_tensor(coef[:, tb % 2, :], gelu, share[:, tb, :], ALU.mult).then_inc(coef_ready, 1)

                def add(step, tb):
                    dve.wait_ge(v_used, RING + (step + 1) * PK)
                    for half in range(2):
                        c = slice(half * 512, (half + 1) * 512)
                        ins = nc.vector.tensor_tensor(x[:, tb, c], x[:, tb, c], psum[2 * (tb % 2) + half][:, :], ALU.add)
                    ins.then_inc(y_added, 1)

                choose(0, 0, (first_sc_copied, 2))
                choose(0, 1, (sc_copied, 2))
                dots(0, 0)
                choose(0, 2, None)
                choose(0, 3, None)
                with dve.Fori(0, PH - 1) as h:
                    for tb in range(TB):
                        dots(TB * h + tb + 1, (tb + 1) % TB)
                        add(TB * h + tb, tb)
                        choose(h + 1, tb, (sc_copied, 2 * h + 4) if tb == 0 else None)
                for tb in range(TB):
                    if tb < TB - 1:
                        dots(TB * (PH - 1) + tb + 1, tb + 1)
                    add(TB * (PH - 1) + tb, tb)

        proj2 = view(0, TB, 3 * SM_W)
        mvo = view(9216, TB, 2 * ML_W)
        conv_in = view(11264, 4, CONV - 1 + T)
        conv_out = view(13324, 4, T)
        ml_q, ml_k = view(15372, ML_H, T), view(17420, ML_H, T)
        kbias = view(19468, SM_H, T)
        GATES = 25616
        gate_pre, gate_t, cum, log_f, ml_a, ml_m, ml_floor, mi_rows = (view(GATES + i * T, T) for i in range(8))
        a_rows = view(11264, ML_H, T)
        W2 = (15376, 29712)
        w_2 = [view(at, KD, 384) for at in W2]
        w_2_parts = [(view_r(at + KD * 384, KD, 384), view_r(at, KD, 384)) for at in W2]
        w_mqk, w_gates, w_mvo = view(0, KD, 2 * ML_W), view(33808, KD, 72), view(29712, KD, 2 * ML_W)
        w_mqk_parts = view_r(4096, KD, 2 * ML_W), view_r(0, KD, 2 * ML_W)
        w_gates_parts = view_r(34384, KD, 72), view_r(33808, KD, 72)
        w_mvo_parts = view_r(21520, KD, 2 * ML_W), view_r(29712, KD, 2 * ML_W)
        squares2 = view(21520, TB * SM_H, HD)
        SCRATCH2 = 31756
        SMALL2 = 37700
        gate_bias = view(SMALL2, 1)
        ml_cols = view(SMALL2 + 4, 2, TB, ML_H)
        ss_2 = view(SMALL2 + 36, 2, TB, SM_H)
        rms_2 = view(SMALL2 + 132, 2, TB, SM_H)
        assert SMALL2 + 228 <= ARENA
        w_2_loaded = [sem("w_fox_loaded"), sem("w_moba_loaded")]
        w_ml_loaded, w_mvo_loaded = sem("w_ml_loaded"), sem("w_mvo_loaded")
        bias_loaded, gates_zeroed = sem("bias_loaded"), sem("gates_zeroed")
        in2_summed, in2_copied = sem("in2_summed"), sem("in2_copied")
        w_in_2 = a["w_in_2"][0].rearrange("(k p) n -> p k n", p=P)
        MI, MF = 64, 32

        mod_gain = sb("mod_gain", [P, 2 * KD])

        with nc.Block() as block:
            @block.vector
            def _(dve):
                for i, (norm, scale0) in enumerate((("norm1_g_2", SC1), ("norm2_g_2", SC2))):
                    c0, n = place[norm]
                    nc.vector.scalar_tensor_tensor(out=mod_gain[:, i * KD:(i + 1) * KD], in0=mod[:, scale0:scale0 + KD],
                                                   scalar=1.0, in1=vec[:, c0:c0 + n], op0=ALU.add, op1=ALU.mult)

        def load_ml(sync):
            sync.wait_ge(gates_zeroed, 2)
            for c0, n, at in ((FF0, FOX_H, 0), (MF0, ML_H, MF), (MI0, ML_H, MI)):
                sync.dma_start(w_gates[:, :, at:at + n], w_in_2[:, :, c0:c0 + n]).then_inc(w_ml_loaded, 16)
            sync.dma_start(w_mqk, w_in_2[:, :, MQK0:MQK0 + 2 * ML_W]).then_inc(w_ml_loaded, 16)
            for i, c0 in enumerate((MV0, MO0)):
                sync.dma_start(w_mvo[:, :, i * ML_W:(i + 1) * ML_W], w_in_2[:, :, c0:c0 + ML_W]).then_inc(w_mvo_loaded, 16)
            sync.dma_start(w_2[0], w_in_2[:, :, 0:384]).then_inc(w_2_loaded[0], 16)
            for name, n, at in (("fox_f_bias_2", FOX_H, 0), ("ml_f_bias_2", ML_H, MF), ("ml_i_bias_2", ML_H, MI)):
                sync.dma_start(gate_bias[at:at + n, :], a[name].rearrange("o n -> n o")).then_inc(bias_loaded, 16)

        def zero_gates(pool):
            nc.gpsimd.memset(w_gates, 0.0).then_inc(gates_zeroed, 1)
            nc.gpsimd.memset(gate_bias, 0.0).then_inc(gates_zeroed, 1)

        norm_T("n5_", x, [(0, D)], rows, hT, gain_cols=lambda k: mod_gain[:, k:k + 1],
               shift_cols=lambda k: mod[:, SH1 + k:SH1 + k + 1], loads=load_ml, pool_part=zero_gates,
               parts=True)

        w_2_split, w_ml_split, w_mvo_split = sem("w_2_split"), sem("w_ml_split"), sem("w_mvo_split")
        ml_summed, ml_copied, squared2, rms2_mean = sem("ml_summed"), sem("ml_copied"), sem("squared2"), sem("rms2_mean")
        gate_added, log_ready, conv_summed = sem("gate_added"), sem("log_ready"), sem("conv_summed")
        mi_moved, row_moved, mvo_summed = sem("mi_moved"), sem("row_moved"), sem("mvo_summed")
        heads_moved, cols_turned = sem("heads_moved"), sem("cols_turned")
        m_ready, pad_zeroed, places_ready = sem("m_ready"), sem("pad_zeroed"), sem("places_ready")
        m_negated, floor_ready = sem("m_negated"), sem("floor_ready")
        conv_ready, a_zeroed = sem("conv_ready"), sem("a_zeroed")
        NG = MI + ML_H
        places = mi_rows[HD:HD + 1, :]
        with nc.Block() as block:
            @block.sync
            def _(sync):
                sync.wait_ge(gate_added, 1)
                sync.dma_start(mi_rows[MF:MF + ML_H, :], gate_pre[MI:MI + ML_H, :]).then_inc(mi_moved, 16)
                sync.wait_ge(mvo_summed, TB)
                sync.dma_start(w_2[1], w_in_2[:, :, BQ0:BQ0 + 384]).then_inc(w_2_loaded[1], 16)
                with sync.Fori(1, 3) as i:
                    for odd, c0 in enumerate((0, BQ0)):
                        sync.wait_ge(in2_summed, 8 * i + TB * (odd - 1))
                        sync.dma_start(w_2[odd], w_in_2[:, :, ds(i * 384 + c0, 384)]).then_inc(w_2_loaded[odd], 16)
                sync.wait_ge(m_ready, 1)
                sync.wait_ge(a_zeroed, 1)
                for h in range(ML_H):
                    sync.dma_start(a_rows[0:1, h, :], ml_a[MF + h:MF + h + 1, :]).then_inc(row_moved, 16)
                sync.wait_ge(in2_summed, 8 * 2 + TB)
                for j in range(4):
                    o = ml_q if j < 2 else ml_k
                    for odd in range(2):
                        sync.dma_start(o[0:HD, 2 * (j % 2) + odd, :],
                                       conv_out[odd * HD:(odd + 1) * HD, j, :]).then_inc(heads_moved, 16)
                sync.wait_ge(rms2_mean, 3)
                for h in range(FOX_H):
                    sync.dma_start(kbias[HD:HD + 1, h, :], log_f[h:h + 1, :]).then_inc(row_moved, 16)
                sync.wait_ge(row_moved, 16 * (FOX_H + ML_H))
                sync.wait_ge(heads_moved, 16 * 8)

            @block.gpsimd
            def _(pool):
                nc.gpsimd.memset(conv_in[:, :, 0:CONV - 1], 0.0).then_inc(pad_zeroed, 1)
                pool.drain()
                nc.gpsimd.iota(places, [[1, T]], base=0, channel_multiplier=0,
                               allow_small_or_imprecise_dtypes=True).then_inc(places_ready, 1)
                pool.drain()
                pool.wait_ge(conv_ready, 4)
                nc.gpsimd.memset(a_rows, 0.0).then_inc(a_zeroed, 1)

            @block.tensor
            def _(pe):
                pe.wait_ge(w_ml_split, 1)
                for k in range(KD):
                    ins = product(psum[4][0:NG, :], [part[:, k, 0:NG] for part in w_gates_parts], h_all(k),
                                  k == 0, k == KD - 1)
                ins.then_inc(ml_summed, 1)
                for j in range(4):
                    pe.wait_ge(w_ml_split, j + 2)
                    c = slice(j * P, (j + 1) * P)
                    for k in range(KD):
                        ins = product(psum[j][:, :], [part[:, k, c] for part in w_mqk_parts], h_all(k),
                                      k == 0, k == KD - 1)
                    ins.then_inc(ml_summed, 1)
                pe.wait_ge(w_mvo_split, 1)
                pe.wait_ge(gate_added, 1)
                for tb in range(TB):
                    for k in range(KD):
                        ins = product(psum[4 + tb][:, :], h_rows(k, tb), [part[:, k, :] for part in w_mvo_parts],
                                      k == 0, k == KD - 1)
                    ins.then_inc(mvo_summed, 1)
                pe.wait_ge(ml_copied, 4)
                with pe.Fori(0, 3) as i:
                    for odd in range(2):
                        pe.wait_ge(w_2_split, 2 * i + odd + 1)
                        for tb in range(TB):
                            pe.wait_ge(in2_copied, 8 * i + 4 * odd + tb + 1)
                            for k in range(KD):
                                ins = product(psum[4 * odd + tb][:, 0:384], h_rows(k, tb),
                                              [part[:, k, :] for part in w_2_parts[odd]], k == 0, k == KD - 1)
                            ins.then_inc(in2_summed, 1)
                pe.wait_ge(in2_copied, 8 + 8 * 2 + 1)
                pe.wait_ge(m_negated, 1)
                pe.wait_ge(floor_ready, 1)
                r = slice(MF, MF + ML_H)
                for i, rows_of in enumerate((ml_m, ml_floor)):
                    for tb in range(TB):
                        ins = nc.tensor.transpose(psum[0][:, (i * TB + tb) * ML_H:(i * TB + tb + 1) * ML_H],
                                                  rows_of[r, tb * P:(tb + 1) * P], ident[r, r])
                ins.then_inc(cols_turned, 1)

            @block.scalar
            def _(act):
                act.sem_inc(in2_copied, 4)
                act.wait_ge(gate_added, 1)
                nc.scalar.activation(gate_t[0:NG, :], gate_pre[0:NG, :], ACT.Abs)
                act.drain()
                nc.scalar.activation(gate_t[0:NG, :], gate_t[0:NG, :], ACT.Exp, scale=-1.0)
                act.drain()
                nc.scalar.activation(gate_t[0:NG, :], gate_t[0:NG, :], ACT.Ln, bias=1.0).then_inc(log_ready, 1)
                for j in range(4):
                    act.wait_ge(ml_summed, 2 + j)
                    nc.scalar.copy(conv_in[:, j, CONV - 1:], psum[j][:, :]).then_inc(ml_copied, 1)
                act.wait_ge(m_ready, 1)
                nc.scalar.activation(ml_floor[MF:MF + ML_H, :], ml_floor[MF:MF + ML_H, :], ACT.Exp,
                                     scale=-1.0).then_inc(floor_ready, 1)
                for tb in range(TB):
                    act.wait_ge(mvo_summed, tb + 1)
                    nc.scalar.copy(mvo[:, tb, :], psum[4 + tb][:, :]).then_inc(in2_copied, 1)
                for j in range(4):
                    act.wait_ge(conv_summed, j + 1)
                    nc.scalar.activation(conv_out[:, j, :], conv_out[:, j, :], ACT.Silu).then_inc(conv_ready, 1)

                def copy_out(i):
                    for odd in range(2):
                        for tb in range(TB):
                            act.wait_ge(in2_summed, 8 * i + TB * odd + tb + 1)
                            nc.scalar.copy(proj2[:, tb, ds(i * SM_W + odd * FOX_W, 384)],
                                           psum[4 * odd + tb][:, 0:384]).then_inc(in2_copied, 1)

                with act.Fori(0, 2) as i:
                    copy_out(i)
                    act.drain()
                    act.wait_ge(rms2_mean, i + 1)
                    act.nop(nofuse=True)
                    nc.scalar.activation(squares2.rearrange("p (b h) d -> p b (h d)", h=SM_H),
                                         proj2[:, :, ds(i * SM_W, SM_W)], ACT.Square).then_inc(squared2, 1)
                copy_out(2)
                flat = rms_2.rearrange("p i b h -> p (i b h)")
                act.wait_ge(rms2_mean, 3)
                nc.scalar.activation(flat, ss_2.rearrange("p i b h -> p (i b h)"), ACT.Ln)
                act.drain()
                nc.scalar.activation(flat, flat, ACT.Exp, scale=-0.5)

            @block.vector
            def _(dve):
                dve.sem_inc(rms2_mean, 1)
                dve.wait_ge(w_ml_loaded, 64)
                split(dve, w_gates, *w_gates_parts).then_inc(w_ml_split, 1)
                for j in range(4):
                    c = slice(j * P, (j + 1) * P)
                    split(dve, w_mqk[:, :, c], *[part[:, :, c] for part in w_mqk_parts]).then_inc(w_ml_split, 1)
                dve.wait_ge(bias_loaded, 48)
                dve.wait_ge(ml_summed, 1)
                nc.vector.tensor_scalar(gate_pre[0:NG, :], psum[4][0:NG, :], gate_bias[0:NG, :], None,
                                        ALU.add).then_inc(gate_added, 1)
                dve.wait_ge(w_mvo_loaded, 32)
                split(dve, w_mvo, *w_mvo_parts).then_inc(w_mvo_split, 1)
                dve.wait_ge(w_2_loaded[0], 16)
                split(dve, w_2[0], *w_2_parts[0]).then_inc(w_2_split, 1)
                dve.wait_ge(log_ready, 1)
                n = MF + ML_H
                nc.vector.scalar_tensor_tensor(out=log_f[0:n, :], in0=gate_pre[0:n, :], scalar=0.0, in1=gate_t[0:n, :],
                                               op0=ALU.min, op1=ALU.subtract)
                dve.drain()
                nc.vector.tensor_tensor_scan(cum[0:n, :], ones[0:n, :], log_f[0:n, :], 0.0, ALU.mult, ALU.add)
                dve.drain()
                nc.vector.tensor_scalar(log_f[0:FOX_H, :], cum[0:FOX_H, :], -1.0, None, ALU.mult)
                r = slice(MF, MF + ML_H)
                dve.wait_ge(mi_moved, 16)
                nc.vector.tensor_tensor(ml_a[r, :], mi_rows[r, :], cum[r, :], ALU.subtract)
                dve.drain()
                nc.vector.tensor_tensor_scan(ml_m[r, :], ml_a[r, :], ml_a[r, :], 0.0, ALU.max, ALU.max)
                dve.drain()
                nc.vector.tensor_tensor(ml_floor[r, :], ml_m[r, :], cum[r, :], ALU.add).then_inc(m_ready, 1)
                nc.vector.tensor_scalar(ml_m[r, :], ml_m[r, :], -1.0, None, ALU.mult).then_inc(m_negated, 1)
                dve.wait_ge(pad_zeroed, 1)
                for j in range(4):
                    dve.wait_ge(ml_copied, j + 1)
                    nc.vector.tensor_scalar(conv_out[:, j, :], conv_in[:, j, 0:T], col("ml_conv_w_2", j),
                                            col("ml_conv_b_2", j), ALU.mult, ALU.add)
                    for c in range(1, CONV):
                        dve.drain()
                        ins = nc.vector.scalar_tensor_tensor(out=conv_out[:, j, :], in0=conv_in[:, j, c:c + T],
                                                             scalar=col("ml_conv_w_2", 4 * c + j), in1=conv_out[:, j, :],
                                                             op0=ALU.mult, op1=ALU.add)
                    ins.then_inc(conv_summed, 1)

                def split_tile(i, odd):
                    dve.wait_ge(w_2_loaded[odd], 16 * i + 16)
                    split(dve, w_2[odd], *w_2_parts[odd]).then_inc(w_2_split, 1)

                with dve.Fori(0, 2) as i:
                    split_tile(i, 1)
                    split_tile(i + 1, 0)
                    dve.wait_ge(squared2, i + 1)
                    s = ss_2[:, ds(i, 1), :, :].rearrange("p i b h -> p (i b h)")
                    nc.vector.tensor_reduce(s, squares2, AX, ALU.add)
                    dve.drain()
                    nc.vector.tensor_scalar(s, s, 1.0 / HD, EPS, ALU.mult, ALU.add).then_inc(rms2_mean, 1)
                split_tile(2, 1)
                dve.wait_ge(places_ready, 1)
                for h in range(MOBA_H):
                    nc.vector.tensor_scalar(kbias[HD:HD + 1, FOX_H + h, :], places, 2.0 ** (-8.0 * (h + 1) / MOBA_H),
                                            None, ALU.mult)
                dve.wait_ge(cols_turned, 1)
                nc.vector.tensor_copy(ml_cols.rearrange("p i b h -> p (i b h)"), psum[0][:, 0:2 * TB * ML_H])

        attention("ml_", "mlstm", ML_H, HD, SCRATCH2, None, None, None,
                  v=lambda j, h: mvo[:, j, ds(h * HD, HD)],
                  dst=lambda tb, h: rows[:, tb, ds(h * HD + SM_W, HD)], mask=causal_mask,
                  qk_T=lambda h: (ml_q[0:HD, ds(h, 1), :].squeeze(1), ml_k[0:HD, ds(h, 1), :].squeeze(1)),
                  decay=(lambda h, n: a_rows[:, ds(h, 1), 0:n].squeeze(1),
                         lambda tb, h: ml_cols[:, 0, tb, ds(h, 1)], lambda tb, h: ml_cols[:, 1, tb, ds(h, 1)]))

        w_out = view(11264, KD, D)
        w_out_loaded = sem("w_out_loaded")

        def stage_2(h, q_st, k_st, staged):
            for i, st in enumerate((q_st, k_st)):
                nc.gpsimd.tensor_tensor(st[:, :, 0:HD], proj2[:, :, ds(h * HD + i * SM_W, HD)],
                                        rms_2[:, i, :, ds(h, 1)].to_broadcast([P, TB, HD]), ALU.mult).then_inc(staged, 1)

        attention("sm_", "softmax", SM_H, HD, SCRATCH2, stage_2, lambda h: gains[0:HD, ds(h + GQ, 1)],
                  lambda h: gains[0:HD, ds(h + GK, 1)],
                  v=lambda j, h: proj2[:, j, ds(h * HD + 2 * SM_W, HD)],
                  dst=lambda tb, h: rows[:, tb, ds(h * HD, HD)], mask=causal_mask,
                  kbias=lambda h: kbias[HD:HD + 1, ds(h, 1), :].squeeze(1),
                  loads=lambda sync: sync.dma_start(w_out, a["w_out_2"][0].rearrange("(k p) n -> p k n", p=P))
                  .then_inc(w_out_loaded, 16))

        ml_gain, gate_row = view(SCRATCH2, ML_W), ffn_gain
        ml_sq, ml_ss, ml_sig = view(SCRATCH2 + 256, TB * ML_H, HD), view(SCRATCH2 + 1280, TB * ML_H), view(SCRATCH2 + 1400, TB, ML_W)
        ml_gain_loaded, ml_squared, ml_mean, ml_rms = sem("ml_gain_loaded"), sem("ml_squared"), sem("ml_mean"), sem("ml_rms")
        ml_opened, y_turned, y_copied = sem("ml_opened"), sem("y_turned"), sem("y_copied")
        g_summed, g_stored = sem("g_summed"), sem("g_stored")

        def gate_rows(pe, g0):
            for k in range(KD):
                ins = nc.tensor.matmul(psum[6 + k // 4][:, k % 4 * P:k % 4 * P + P],
                                       mod[:, g0 + k:g0 + k + 1].to_broadcast([P, P]), ident[:, :], start=True, stop=True)
            ins.then_inc(g_summed, 1)

        with nc.Block() as block:
            @block.sync
            def _(sync):
                sync.dma_start(ml_gain, a["ml_h_g_2"].to_broadcast([P, ML_W])).then_inc(ml_gain_loaded, 16)

            @block.scalar
            def _(act):
                heads = rows[:, :, SM_W:].rearrange("p b (h d) -> p b h d", d=HD)
                nc.scalar.activation(ml_sq.rearrange("p (b h) d -> p b (h d)", h=ML_H), rows[:, :, SM_W:],
                                     ACT.Square).then_inc(ml_squared, 1)
                nc.scalar.activation(ml_sig, mvo[:, :, ML_W:], ACT.Sigmoid)
                act.wait_ge(ml_mean, 1)
                nc.scalar.activation(ml_ss, ml_ss, ACT.Ln)
                act.drain()
                nc.scalar.activation(ml_ss, ml_ss, ACT.Exp, scale=-0.5).then_inc(ml_rms, 1)
                for k in range(KD):
                    act.wait_ge(y_turned, k + 1)
                    nc.scalar.copy(hT[:, k, :], psum[k % 4][:, :]).then_inc(y_copied, 1)

            @block.vector
            def _(dve):
                dve.wait_ge(g_summed, 1)
                for i in range(2):
                    nc.vector.tensor_copy(gate_row[:, i * 512:(i + 1) * 512], psum[6 + i][:, :])
                dve.wait_ge(ml_squared, 1)
                nc.vector.tensor_reduce(ml_ss, ml_sq, AX, ALU.add)
                dve.drain()
                nc.vector.tensor_scalar(ml_ss, ml_ss, 1.0 / HD, EPS, ALU.mult, ALU.add).then_inc(ml_mean, 1)
                dve.wait_ge(ml_rms, 1)
                y = rows[:, :, SM_W:]
                for tb in range(TB):
                    o = y[:, tb, :].rearrange("p (h d) -> p h d", d=HD)
                    r = ml_ss[:, tb * ML_H:(tb + 1) * ML_H].unsqueeze(2).to_broadcast([P, ML_H, HD])
                    nc.vector.tensor_tensor(o, o, r, ALU.mult)
                dve.drain()
                dve.wait_ge(ml_gain_loaded, 16)
                nc.vector.tensor_tensor(y, y, ml_gain.unsqueeze(1).to_broadcast([P, TB, ML_W]), ALU.mult)
                dve.drain()
                nc.vector.tensor_tensor(y, y, ml_sig, ALU.mult).then_inc(ml_opened, 1)
                for k in range(KD):
                    dve.wait_ge(y_copied, k + 1)
                    split_h(dve, k)

            @block.tensor
            def _(pe):
                gate_rows(pe, G1)
                for k in range(KD):
                    if k >= 4:
                        pe.wait_ge(y_copied, k - 3)
                    if k == SM_W // P:
                        pe.wait_ge(ml_opened, 1)
                    for tb in range(TB):
                        ins = nc.tensor.transpose(psum[k % 4][:, tb * P:(tb + 1) * P], rows[:, tb, k * P:(k + 1) * P],
                                                  ident[:, :])
                    ins.then_inc(y_turned, 1)

        KFOX, KML = FOX_W // P, ML_W // P
        order = [*range(KFOX), *range(KFOX + KML, KD), *range(KFOX, KFOX + KML)]
        out_projection("o2_", w_out, (view_r(19472, KD, D), view_r(11264, KD, D)), order, w_out_loaded, gate_row=gate_row)

        act_value = nc.alloc_sbuf_tensor_at("act_value", [P, T], F32, offset=arena_at + 4 * (ARENA - 2160))
        act_high, act_low = view_r(0, KF, T), view_r(KF * T, KF, T)
        GU = 2 * KF * T
        GU_SIZE = 2 * KD * P
        w_gu = [view(GU + i * GU_SIZE, KD * 2, P) for i in range(2)]
        w_gu_parts = [(view_r(GU + (2 + i) * GU_SIZE, KD * 2, P), view_r(GU + i * GU_SIZE, KD * 2, P)) for i in range(2)]
        DN_SLOTS = 4
        w_dn = view(GU + 4 * GU_SIZE, DN_SLOTS, D)
        w_dn_parts = view_r(GU, DN_SLOTS, D), view_r(GU + 4 * GU_SIZE, DN_SLOTS, D)
        silu_g = view(GU + 4 * GU_SIZE + DN_SLOTS * D, 2, T)
        gu_loaded, dn_loaded = [sem("gu_loaded0"), sem("gu_loaded1")], [sem(f"dn_loaded{i}") for i in range(DN_SLOTS)]
        gu_split, gu_summed, silu_ready, act_ready = sem("gu_split"), sem("gu_summed"), sem("silu_ready"), sem("act_ready")
        dn_split, dn_used, dn_added, stored_out = sem("dn_split"), sem("dn_used"), sem("dn_added"), sem("stored_out")
        act_f = view_r(GU + 4 * GU_SIZE + DN_SLOTS * D + 2 * T, 2, 2 * T).rearrange("p s (a t) -> p s a t", a=2)
        y_summed, act_placed = sem("y_summed"), sem("act_placed")
        w_gate_up = a["w_gate_up_2"][0].rearrange("(k p) n -> p k n", p=P)
        w_down = a["w_down_2"][0].rearrange("(k p) n -> p k n", p=P)

        def load_gu(sync, i, odd):
            for g in range(2):
                sync.dma_start(w_gu[odd][:, g * KD:(g + 1) * KD, :], w_gate_up[:, :, ds((2 * i + odd) * P + g * D_FF, P)])\
                    .then_inc(gu_loaded[odd], 16)

        def load_dn(sync, f, slot):
            sync.dma_start(w_dn[:, slot, :], w_down[:, ds(f, 1), :].squeeze(1)).then_inc(dn_loaded[slot], 16)

        def load_first_ffn(sync):
            for odd in range(2):
                load_gu(sync, 0, odd)
            for slot in range(DN_SLOTS):
                load_dn(sync, slot, slot)

        norm_T("n6_", x, [(0, D)], rows, hT, gain_cols=lambda k: mod_gain[:, KD + k:KD + k + 1],
               shift_cols=lambda k: mod[:, SH2 + k:SH2 + k + 1], loads=load_first_ffn, parts=True)

        with nc.Block() as block:
            @block.sync
            def _(sync):
                with sync.Fori(1, KF // 2) as i:
                    for odd in range(2):
                        sync.wait_ge(gu_summed, 4 * i - 2 + 2 * odd)
                        load_gu(sync, i, odd)

            @block.tensor
            def _(pe):
                gate_rows(pe, G2)
                with pe.Fori(0, KF // 2) as i:
                    for odd in range(2):
                        pe.wait_ge(gu_split, 2 * i + odd + 1)
                        pe.wait_ge(act_ready, 2 * i + odd + 1)
                        for g in range(2):
                            for k in range(KD):
                                j = g * KD + k
                                ins = product(psum[2 * odd + g][:, :], [part[:, j, :] for part in w_gu_parts[odd]],
                                              h_all(k), k == 0, k == KD - 1)
                            ins.then_inc(gu_summed, 1)

            @block.scalar
            def _(act):
                with act.Fori(0, KF // 2) as i:
                    for odd in range(2):
                        act.wait_ge(gu_summed, 4 * i + 2 * odd + 1)
                        act.wait_ge(act_ready, 2 * i + odd + 1)
                        nc.scalar.activation(silu_g[:, odd, :], psum[2 * odd][:, :], ACT.Silu).then_inc(silu_ready, 1)

            @block.vector
            def _(dve):
                dve.sem_inc(act_ready, 2)

                def split_tile(i, odd):
                    dve.wait_ge(gu_loaded[odd], 32 * i + 32)
                    split(dve, w_gu[odd], *w_gu_parts[odd]).then_inc(gu_split, 1)

                def activate(i, odd):
                    dve.wait_ge(silu_ready, 2 * i + odd + 1)
                    dve.wait_ge(gu_summed, 4 * i + 2 * odd + 2)
                    high, low = (t[:, ds(2 * i + odd, 1), :].squeeze(1) for t in (act_high, act_low))
                    dve.nop(nofuse=True)
                    dve.drain()
                    nc.vector.tensor_tensor(act_value[:, :], silu_g[:, odd, :], psum[2 * odd + 1][:, :],
                                            ALU.mult).then_inc(act_ready, 1)
                    dve.drain()
                    split(dve, act_value[:, :], high, low)

                split_tile(0, 0)
                dve.wait_ge(g_summed, 2)
                for i in range(2):
                    nc.vector.tensor_copy(gate_row[:, i * 512:(i + 1) * 512], psum[6 + i][:, :])
                last = KF // 2 - 1
                with dve.Fori(0, last) as i:
                    split_tile(i, 1)
                    activate(i, 0)
                    split_tile(i + 1, 0)
                    activate(i, 1)
                split_tile(last, 1)
                activate(last, 0)
                activate(last, 1)

        LOOP = (KF - 2) // DN_SLOTS - 1
        FIRST, LAST = range(2), range(2 + LOOP * DN_SLOTS, KF)

        def over_f(engine, tile):
            for f in FIRST:
                tile(f, f, 0)
            with engine.Fori(0, LOOP) as i:
                for m in range(DN_SLOTS):
                    tile(i * DN_SLOTS + 2 + m, (2 + m) % DN_SLOTS, i + (2 + m) // DN_SLOTS)
            for f in LAST:
                tile(f, f % DN_SLOTS, f // DN_SLOTS)

        with nc.Block() as block:
            @block.sync
            def _(sync):
                with sync.Fori(1, KF // DN_SLOTS) as i:
                    for slot in range(DN_SLOTS):
                        sync.wait_ge(dn_used, i * DN_SLOTS + slot - DN_SLOTS + 1)
                        load_dn(sync, i * DN_SLOTS + slot, slot)
                for f in range(KF // DN_SLOTS * DN_SLOTS, KF):
                    sync.wait_ge(dn_used, f - DN_SLOTS + 1)
                    load_dn(sync, f, f % DN_SLOTS)
                for tb in range(TB):
                    sync.wait_ge(dn_added, 2 * tb + 2)
                    sync.dma_start(out[0, tb * P:(tb + 1) * P, :], x[:, tb, :]).then_inc(stored_out, 16)
                sync.wait_ge(stored_out, 16 * TB)

            @block.tensor
            def _(pe):
                def tile(f, slot, turn):
                    first, last = f is FIRST[0], f is LAST[-1]
                    pe.wait_ge(dn_split, f + 1)
                    pe.wait_ge(act_placed, f + 1)
                    for tb in range(TB):
                        t = slice(tb * P, (tb + 1) * P)
                        lhsT = [act_f[:, slot % 2, part, t] for part in range(2)]
                        for half in range(2):
                            c = slice(half * 512, (half + 1) * 512)
                            ins = product(psum[4 * half + tb][:, :], lhsT, [part[:, slot, c] for part in w_dn_parts],
                                          first, last)
                            if last:
                                ins.then_inc(y_summed, 1)
                    if not last:
                        ins.then_inc(dn_used, 1)
                over_f(pe, tile)

            @block.scalar
            def _(act):
                def tile(f, slot, turn):
                    if f is not FIRST[0] and f is not FIRST[1]:
                        act.wait_ge(dn_used, f - 1)
                    nc.scalar.copy(act_f[:, slot % 2, 0, :], act_high[:, ds(f, 1), :].squeeze(1).bitcast(F32))
                    nc.scalar.copy(act_f[:, slot % 2, 1, :], act_low[:, ds(f, 1), :].squeeze(1).bitcast(F32)).then_inc(act_placed, 1)
                over_f(act, tile)

            @block.vector
            def _(dve):
                def tile(f, slot, turn):
                    dve.wait_ge(dn_loaded[slot], 16 * turn + 16)
                    w = w_dn[:, slot, :]
                    nc.vector.tensor_tensor(w, w, gate_row[:, :], ALU.mult)
                    dve.drain()
                    split(dve, w, *[part[:, slot, :] for part in w_dn_parts]).then_inc(dn_split, 1)
                over_f(dve, tile)
                for tb in range(TB):
                    for half in range(2):
                        c = slice(half * 512, (half + 1) * 512)
                        dve.wait_ge(y_summed, 2 * tb + half + 1)
                        nc.vector.tensor_tensor(x[:, tb, c], x[:, tb, c], psum[4 * half + tb][:, :],
                                                ALU.add).then_inc(dn_added, 1)


_INS = ["x", "positions", "attn_norm", "w_in", "cq_norm", "w_uq", "ckv_norm", "w_ukv", "q_norm", "k_norm",
        "sb_out_norm", "mla_out_norm", "w_o", "ffn_norm", "peer_w_q", "peer_sub_keys", "peer_u", "peer_v", "c_2",
        "w_ada_2", "b_ada_2", "norm1_g_2", "norm2_g_2", "w_in_2", "fox_f_bias_2", "fox_q_g_2", "fox_k_g_2",
        "ml_conv_w_2", "ml_conv_b_2", "ml_i_bias_2", "ml_f_bias_2", "ml_h_g_2", "moba_q_g_2", "moba_k_g_2",
        "w_out_2", "w_gate_up_2", "w_down_2"]


def kernel(**inputs):
    import numpy as _np
    import concourse.bacc as _bacc
    from concourse import mybir as _mybir
    from concourse.bass_utils import run_bass_kernel_spmd as _run

    nc = _bacc.Bacc("TRN2", target_bir_lowering=False, num_devices=1)
    arrays, args = {}, {}
    for name in _INS:
        v = _np.ascontiguousarray(inputs[name])
        arrays[f"in_{name}"] = v
        args[name] = nc.dram_tensor(f"in_{name}", v.shape, _mybir.dt.from_np(v.dtype), kind="ExternalInput").ap()
    out = nc.dram_tensor("out", (1, T, D), F32, kind="ExternalOutput").ap()
    program(nc, args, out)
    r = _run(nc, [arrays], core_ids=[0])
    return r.results[0]["out"]
```
